# Optimizing a Trainium2 kernel written in Bass

```python
import math
import jax, jax.numpy as jnp
from jax import lax
import numpy as np

D_MODEL = 1024
BATCH = 1
SEQ = 512
DEPTH = 2

N_Q_HEADS = 8
N_KV_HEADS = 2
HEAD_DIM = 64
Q_GROUP = N_Q_HEADS // N_KV_HEADS
WINDOW = 128
BLOCK = 128
ROPE_THETA = 500000.0
ROT_DIM = HEAD_DIM // 4
ATTN_WIDTH = N_Q_HEADS * HEAD_DIM
KV_WIDTH = N_KV_HEADS * HEAD_DIM
NEG_INF = -1e30
CONV_WIDTH = D_MODEL // 2
CONV_K = 3
SSM_WIDTH = D_MODEL // 2
SSM_GROUP = 16
SSM_GROUPS = SSM_WIDTH // SSM_GROUP
SSM_STATE = 64
DT_MIN = 1e-3
DT_MAX = 1e-1
N_BRANCH = 3
GATE_WIDTH = N_BRANCH * D_MODEL
FFN_HIDDEN = -(-8 * D_MODEL // (3 * 256)) * 256
NORM_EPS = 1e-6

IN_SIZES = (ATTN_WIDTH, KV_WIDTH, KV_WIDTH, CONV_WIDTH, CONV_WIDTH, CONV_WIDTH, SSM_WIDTH, GATE_WIDTH)
IN_COLS = sum(IN_SIZES)
IN_SPLITS = tuple(int(v) for v in np.cumsum(IN_SIZES)[:-1])


def rmsnorm(x, g):
    xf = x.astype(jnp.float32)
    y = xf * lax.rsqrt(jnp.mean(xf * xf, axis=-1, keepdims=True) + NORM_EPS)
    return (y * g.astype(jnp.float32)).astype(x.dtype)

def rope_tables(seq_len):
    pos = jnp.arange(seq_len, dtype=jnp.float32)
    inv_freq = ROPE_THETA ** (-jnp.arange(0, ROT_DIM, 2, dtype=jnp.float32) / ROT_DIM)
    ang = pos[:, None] * inv_freq[None, :]
    return jnp.cos(ang), jnp.sin(ang)

def partial_rope(t, cos, sin):
    half = ROT_DIM // 2
    tf = t.astype(jnp.float32)
    t1, t2, rest = tf[..., :half], tf[..., half:ROT_DIM], tf[..., ROT_DIM:]
    c = cos[None, :, None, :]
    s = sin[None, :, None, :]
    out = jnp.concatenate([t1 * c - t2 * s, t2 * c + t1 * s, rest], axis=-1)
    return out.astype(t.dtype)

def sliding_window_attention(q, k, v, sinks):
    b, l = q.shape[0], q.shape[1]
    nb = l // BLOCK
    qb = q.reshape(b, nb, BLOCK, N_KV_HEADS, Q_GROUP, HEAD_DIM).astype(jnp.float32)

    def band(t):
        tp = jnp.pad(t, ((0, 0), (BLOCK, 0), (0, 0), (0, 0)))
        tp = tp.reshape(b, nb + 1, BLOCK, N_KV_HEADS, HEAD_DIM)
        return jnp.concatenate([tp[:, :-1], tp[:, 1:]], axis=2).astype(jnp.float32)

    kb, vb = band(k), band(v)
    s = jnp.einsum("bnqkgd,bnskd->bnkgqs", qb, kb) * (HEAD_DIM ** -0.5)
    qi = jnp.arange(BLOCK)[:, None]
    kj = jnp.arange(2 * BLOCK)[None, :]
    delta = qi + BLOCK - kj
    band_ok = (delta >= 0) & (delta < WINDOW)
    kpos = jnp.arange(nb)[:, None] * BLOCK - BLOCK + kj
    mask = band_ok[None, :, :] & (kpos >= 0)[:, None, :]
    s = jnp.where(mask[None, :, None, None, :, :], s, NEG_INF)
    sink = sinks.astype(jnp.float32).reshape(N_KV_HEADS, Q_GROUP)[None, None, :, :, None, None]
    m = jnp.maximum(jnp.max(s, axis=-1, keepdims=True), sink)
    p = jnp.exp(s - m)
    denom = jnp.sum(p, axis=-1, keepdims=True) + jnp.exp(sink - m)
    o = jnp.einsum("bnkgqs,bnskd->bnqkgd", p / denom, vb)
    return o.reshape(b, l, ATTN_WIDTH).astype(q.dtype)

def short_conv(z, w):
    l = z.shape[1]
    zp = jnp.pad(z, ((0, 0), (CONV_K - 1, 0), (0, 0)))
    y = w[0] * zp[:, 0:l]
    for j in range(1, CONV_K):
        y = y + w[j] * zp[:, j:j + l]
    return y

def s5_ssm(u, a_re, a_im, b_re, b_im, c_re, c_im, d, log_dt):
    bsz, l = u.shape[0], u.shape[1]
    uf = u.astype(jnp.float32).reshape(bsz, l, SSM_GROUPS, SSM_GROUP)
    lam = lax.complex(a_re.astype(jnp.float32), a_im.astype(jnp.float32))
    dt = jnp.exp(log_dt.astype(jnp.float32))[:, None]
    lam_bar = jnp.exp(lam * dt)
    b_c = lax.complex(b_re.astype(jnp.float32), b_im.astype(jnp.float32))
    b_bar = ((lam_bar - 1.0) / lam)[..., None] * b_c
    bu = jnp.einsum("blgh,gph->blgp", uf.astype(jnp.complex64), b_bar)
    a_elems = jnp.broadcast_to(lam_bar, bu.shape)

    def combine(e1, e2):
        a1, x1 = e1
        a2, x2 = e2
        return a1 * a2, a2 * x1 + x2

    _, states = lax.associative_scan(combine, (a_elems, bu), axis=1)
    c_c = lax.complex(c_re.astype(jnp.float32), c_im.astype(jnp.float32))
    y = jnp.einsum("blgp,ghp->blgh", states, c_c).real
    y = y + d.astype(jnp.float32).reshape(SSM_GROUPS, SSM_GROUP) * uf
    return y.reshape(bsz, l, SSM_WIDTH).astype(u.dtype)

def first_inputs(seed: int = 0) -> dict:
    key = jax.random.key(seed)
    ks = jax.random.split(key, 24)
    L = DEPTH

    def nrm(k, shape, fan_in):
        return jax.random.normal(k, shape, jnp.float32) * (fan_in ** -0.5)

    x = jax.random.normal(ks[0], (BATCH, SEQ, D_MODEL), jnp.float32)
    norm_mix = 1.0 + 0.02 * jax.random.normal(ks[1], (L, D_MODEL), jnp.float32)
    w_in = nrm(ks[2], (L, D_MODEL, IN_COLS), D_MODEL)
    b_gate = 0.02 * jax.random.normal(ks[3], (L, GATE_WIDTH), jnp.float32)
    attn_sinks = 0.5 * jax.random.normal(ks[4], (L, N_Q_HEADS), jnp.float32)
    w_attn_o = nrm(ks[5], (L, ATTN_WIDTH, D_MODEL), ATTN_WIDTH)
    conv_w = nrm(ks[6], (L, CONV_K, CONV_WIDTH), CONV_K)
    w_conv_o = nrm(ks[7], (L, CONV_WIDTH, D_MODEL), CONV_WIDTH)
    ssm_a_re = -0.5 + 0.01 * jax.random.normal(ks[8], (L, SSM_GROUPS, SSM_STATE), jnp.float32)
    ssm_a_im = (math.pi * jnp.arange(SSM_STATE, dtype=jnp.float32))[None, None, :] \
        + 0.01 * jax.random.normal(ks[9], (L, SSM_GROUPS, SSM_STATE), jnp.float32)
    ssm_b_re = nrm(ks[10], (L, SSM_GROUPS, SSM_STATE, SSM_GROUP), 2 * SSM_GROUP)
    ssm_b_im = nrm(ks[11], (L, SSM_GROUPS, SSM_STATE, SSM_GROUP), 2 * SSM_GROUP)
    ssm_c_re = nrm(ks[12], (L, SSM_GROUPS, SSM_GROUP, SSM_STATE), 2 * SSM_STATE)
    ssm_c_im = nrm(ks[13], (L, SSM_GROUPS, SSM_GROUP, SSM_STATE), 2 * SSM_STATE)
    ssm_d = jax.random.normal(ks[14], (L, SSM_WIDTH), jnp.float32)
    ssm_log_dt = jax.random.uniform(ks[15], (L, SSM_GROUPS), jnp.float32,
                                    minval=math.log(DT_MIN), maxval=math.log(DT_MAX))
    w_ssm_glu = nrm(ks[16], (L, SSM_WIDTH, SSM_WIDTH), SSM_WIDTH)
    w_ssm_o = nrm(ks[17], (L, SSM_WIDTH, D_MODEL), SSM_WIDTH)
    w_mix_o = nrm(ks[18], (L, D_MODEL, D_MODEL), D_MODEL)
    norm_ffn = 1.0 + 0.02 * jax.random.normal(ks[19], (L, D_MODEL), jnp.float32)
    w_ffn_in = nrm(ks[20], (L, D_MODEL, 2 * FFN_HIDDEN), D_MODEL)
    w_ffn_out = nrm(ks[21], (L, FFN_HIDDEN, D_MODEL), FFN_HIDDEN)
    norm_final = 1.0 + 0.02 * jax.random.normal(ks[22], (D_MODEL,), jnp.float32)
    return {"x": x, "norm_mix": norm_mix, "w_in": w_in, "b_gate": b_gate,
            "attn_sinks": attn_sinks, "w_attn_o": w_attn_o, "conv_w": conv_w, "w_conv_o": w_conv_o,
            "ssm_a_re": ssm_a_re, "ssm_a_im": ssm_a_im, "ssm_b_re": ssm_b_re, "ssm_b_im": ssm_b_im,
            "ssm_c_re": ssm_c_re, "ssm_c_im": ssm_c_im, "ssm_d": ssm_d, "ssm_log_dt": ssm_log_dt,
            "w_ssm_glu": w_ssm_glu, "w_ssm_o": w_ssm_o, "w_mix_o": w_mix_o, "norm_ffn": norm_ffn,
            "w_ffn_in": w_ffn_in, "w_ffn_out": w_ffn_out, "norm_final": norm_final}

def first_block(x, norm_mix, w_in, b_gate, attn_sinks, w_attn_o, conv_w, w_conv_o,
              ssm_a_re, ssm_a_im, ssm_b_re, ssm_b_im, ssm_c_re, ssm_c_im, ssm_d, ssm_log_dt,
              w_ssm_glu, w_ssm_o, w_mix_o, norm_ffn, w_ffn_in, w_ffn_out, norm_final):
    b, l = x.shape[0], x.shape[1]
    cos, sin = rope_tables(l)
    for i in range(DEPTH):
        h = rmsnorm(x, norm_mix[i])
        proj = h @ w_in[i]
        q, k, v, cb, cc, cx, u, g = jnp.split(proj, IN_SPLITS, axis=-1)
        q = partial_rope(q.reshape(b, l, N_Q_HEADS, HEAD_DIM), cos, sin)
        k = partial_rope(k.reshape(b, l, N_KV_HEADS, HEAD_DIM), cos, sin)
        v = v.reshape(b, l, N_KV_HEADS, HEAD_DIM)
        y_attn = sliding_window_attention(q, k, v, attn_sinks[i]) @ w_attn_o[i]
        y_conv = (cb * short_conv(cc * cx, conv_w[i])) @ w_conv_o[i]
        ys = jax.nn.gelu(s5_ssm(u, ssm_a_re[i], ssm_a_im[i], ssm_b_re[i], ssm_b_im[i],
                                ssm_c_re[i], ssm_c_im[i], ssm_d[i], ssm_log_dt[i]))
        y_ssm = (ys * jax.nn.sigmoid(ys @ w_ssm_glu[i])) @ w_ssm_o[i]
        gates = jax.nn.sigmoid(g + b_gate[i]).reshape(b, l, N_BRANCH, D_MODEL)
        merged = gates[:, :, 0] * y_attn + gates[:, :, 1] * y_conv + gates[:, :, 2] * y_ssm
        x = x + merged @ w_mix_o[i]
        h = rmsnorm(x, norm_ffn[i])
        gt, up = jnp.split(h @ w_ffn_in[i], 2, axis=-1)
        x = x + (jax.nn.silu(gt) * up) @ w_ffn_out[i]
    return rmsnorm(x, norm_final)


DEPTH_2 = 1

ROPE_THETA_2 = 10000.0
EPS = 1e-6
ATTN_SCALE = HEAD_DIM ** -0.5
Q_BLOCK = 128

DSA_HEADS = 8
DSA_Q_RANK = 256
DSA_KV_RANK = 128
IDX_HEADS = 8
IDX_DIM = 64
IDX_SCALE = IDX_HEADS ** -0.5 * IDX_DIM ** -0.5
DSA_TOPK_MAX = 256

NSA_HEADS = 8
NSA_KV_HEADS = 2
NSA_GROUP = NSA_HEADS // NSA_KV_HEADS
CMP_BLOCK = 32
CMP_STRIDE = 16
SLC_BLOCK = 64
SLC_COUNT = 16
WINDOW_2 = 512
FORCE_BONUS = 1e4

MIX_WIDTH = DSA_HEADS * HEAD_DIM + NSA_HEADS * HEAD_DIM
IN_SIZES_2 = (DSA_Q_RANK, DSA_KV_RANK, IDX_DIM, IDX_HEADS,
            NSA_HEADS * HEAD_DIM, 3 * 2 * NSA_KV_HEADS * HEAD_DIM, NSA_HEADS * 3)
IN_WIDTH = sum(IN_SIZES_2)

MEM_LEN = 256
XATTN_HEADS = 4
XATTN_HEAD_DIM = 128

D_FF = 4 * D_MODEL


def _rms_norm(x, g):
    xf = x.astype(jnp.float32)
    y = xf * lax.rsqrt(jnp.mean(xf * xf, axis=-1, keepdims=True) + EPS)
    return (y * g.astype(jnp.float32)).astype(x.dtype)

def _layer_norm(x, g, b):
    xf = x.astype(jnp.float32)
    mu = jnp.mean(xf, axis=-1, keepdims=True)
    var = jnp.mean(jnp.square(xf - mu), axis=-1, keepdims=True)
    y = (xf - mu) * lax.rsqrt(var + EPS) * g.astype(jnp.float32) + b.astype(jnp.float32)
    return y.astype(x.dtype)

def _rope(x, pos):
    half = x.shape[-1] // 2
    inv = ROPE_THETA_2 ** (-jnp.arange(half, dtype=jnp.float32) / half)
    ang = pos.astype(jnp.float32)[:, None] * inv[None, :]
    cos = jnp.cos(ang)[:, None, :]
    sin = jnp.sin(ang)[:, None, :]
    xf = x.astype(jnp.float32)
    x1, x2 = xf[..., :half], xf[..., half:]
    return jnp.concatenate([x1 * cos - x2 * sin, x1 * sin + x2 * cos], axis=-1).astype(x.dtype)

def _masked_softmax(s, mask):
    s = jnp.where(mask, s, -jnp.inf)
    m = jnp.max(s, axis=-1, keepdims=True)
    m = jnp.where(jnp.isfinite(m), m, 0.0)
    p = jnp.where(mask, jnp.exp(s - m), 0.0)
    return p / jnp.maximum(jnp.sum(p, axis=-1, keepdims=True), 1e-30)

def _hybrid_mixer(h, w_in, dsa_cq_g, dsa_ckv_g, w_dsa_uq, w_dsa_ukv, w_idx_q, idx_k_ln_g, idx_k_ln_b,
                  dsa_qn_g, dsa_kn_g, nsa_cmp_pe, w_nsa_cmp, nsa_qn_g, nsa_kn_g, w_out):
    B, L, _ = h.shape
    G, R, D = NSA_KV_HEADS, NSA_GROUP, HEAD_DIM
    pos = jnp.arange(L, dtype=jnp.int32)
    splits = [int(v) for v in np.cumsum(IN_SIZES_2)[:-1]]
    proj = h @ w_in
    c_q, c_kv, k_idx, w_idx, q_nsa, kv_nsa, g_nsa = jnp.split(proj, splits, axis=-1)

    c_q = _rms_norm(c_q, dsa_cq_g)
    c_kv = _rms_norm(c_kv, dsa_ckv_g)
    q_d = _rope(_rms_norm((c_q @ w_dsa_uq).reshape(B, L, DSA_HEADS, D), dsa_qn_g), pos)
    k_d, v_d = jnp.split(c_kv @ w_dsa_ukv, 2, axis=-1)
    k_d = _rope(_rms_norm(k_d, dsa_kn_g)[:, :, None, :], pos)[:, :, 0, :]
    q_i = _rope((c_q @ w_idx_q).reshape(B, L, IDX_HEADS, IDX_DIM), pos)
    k_i = _rope(_layer_norm(k_idx, idx_k_ln_g, idx_k_ln_b)[:, :, None, :], pos)[:, :, 0, :]
    w_i = w_idx * IDX_SCALE
    k_dsa = min(DSA_TOPK_MAX, L // 4)

    q_n = _rope(_rms_norm(q_nsa.reshape(B, L, NSA_HEADS, D), nsa_qn_g), pos)
    kv = kv_nsa.reshape(B, L, 3, 2, G, D)
    k_br, v_br = kv[:, :, :, 0], kv[:, :, :, 1]
    k_slc = _rope(_rms_norm(k_br[:, :, 1], nsa_kn_g[1]), pos)
    k_win = _rope(_rms_norm(k_br[:, :, 2], nsa_kn_g[2]), pos)
    v_slc, v_win = v_br[:, :, 1], v_br[:, :, 2]

    n_cmp = (L - CMP_BLOCK) // CMP_STRIDE + 1
    tok = jnp.arange(n_cmp)[:, None] * CMP_STRIDE + jnp.arange(CMP_BLOCK)[None, :]
    cmp_end = tok[:, -1]
    k_blocks = k_br[:, :, 0][:, tok] + nsa_cmp_pe[0][:, None, :]
    v_blocks = v_br[:, :, 0][:, tok] + nsa_cmp_pe[1][:, None, :]
    k_c = jnp.einsum('bnlgd,lde->bnge', k_blocks, w_nsa_cmp[0])
    v_c = jnp.einsum('bnlgd,lde->bnge', v_blocks, w_nsa_cmp[1])
    k_c = _rope(_rms_norm(k_c, nsa_kn_g[0]), cmp_end)

    n_slc = L // SLC_BLOCK
    n_sel = min(SLC_COUNT, n_slc)
    ci = jnp.arange(n_cmp)[:, None] * CMP_STRIDE
    sj = jnp.arange(n_slc)[None, :] * SLC_BLOCK
    overlap = ((ci < sj + SLC_BLOCK) & (ci + CMP_BLOCK > sj)).astype(jnp.float32)
    k_slc_blk = k_slc.reshape(B, n_slc, SLC_BLOCK, G, D).transpose(0, 3, 1, 2, 4)
    v_slc_blk = v_slc.reshape(B, n_slc, SLC_BLOCK, G, D).transpose(0, 3, 1, 2, 4)

    k_win_pad = jnp.pad(k_win, ((0, 0), (WINDOW_2, 0), (0, 0), (0, 0)))
    v_win_pad = jnp.pad(v_win, ((0, 0), (WINDOW_2, 0), (0, 0), (0, 0)))

    gates = jax.nn.sigmoid(g_nsa.astype(jnp.float32)).astype(h.dtype).reshape(B, L, NSA_HEADS, 3)

    n_qb = L // Q_BLOCK

    def blocks(a):
        return jnp.moveaxis(a.reshape((B, n_qb, Q_BLOCK) + a.shape[2:]), 1, 0)

    bidx3 = jnp.arange(B)[:, None, None]
    bidx4 = jnp.arange(B)[:, None, None, None]
    gidx4 = jnp.arange(G)[None, :, None, None]
    j_slc = jnp.arange(n_slc)

    def step(args):
        qb, qd, qi, wi, qn, gt = args
        t = qb * Q_BLOCK + jnp.arange(Q_BLOCK, dtype=jnp.int32)

        idx_score = jnp.einsum('bqhs,bqh->bqs',
                               jax.nn.relu(jnp.einsum('bqhd,bsd->bqhs', qi, k_i)), wi).astype(jnp.float32)
        idx_score = jnp.where(pos[None, None, :] <= t[None, :, None], idx_score, -jnp.inf)
        _, sel = lax.top_k(idx_score, k_dsa)
        kg = k_d[bidx3, sel]
        vg = v_d[bidx3, sel]
        s = jnp.einsum('bqhd,bqkd->bhqk', qd, kg).astype(jnp.float32) * ATTN_SCALE
        p = _masked_softmax(s, (sel <= t[None, :, None])[:, None])
        o_dsa = jnp.einsum('bhqk,bqkd->bqhd', p.astype(vg.dtype), vg)

        qg = qn.reshape(B, Q_BLOCK, G, R, D)
        s = jnp.einsum('bqgrd,bngd->bgrqn', qg, k_c).astype(jnp.float32) * ATTN_SCALE
        p_cmp = _masked_softmax(s, cmp_end[None, :] <= t[:, None])
        o_cmp = jnp.einsum('bgrqn,bngd->bqgrd', p_cmp.astype(v_c.dtype), v_c)
        blk_score = jnp.einsum('bgrqn,nj->bgqj', p_cmp, overlap)
        tb = t // SLC_BLOCK
        forced = (j_slc[None, :] == 0) | (j_slc[None, :] == tb[:, None]) | (j_slc[None, :] == tb[:, None] - 1)
        admissible = j_slc[None, :] * SLC_BLOCK <= t[:, None]
        blk_score = jnp.where(admissible, blk_score + jnp.where(forced, FORCE_BONUS, 0.0), -jnp.inf)
        _, sel_blk = lax.top_k(blk_score, n_sel)
        kb = k_slc_blk[bidx4, gidx4, sel_blk].reshape(B, G, Q_BLOCK, n_sel * SLC_BLOCK, D)
        vb = v_slc_blk[bidx4, gidx4, sel_blk].reshape(B, G, Q_BLOCK, n_sel * SLC_BLOCK, D)
        kpos = (sel_blk[..., None] * SLC_BLOCK + jnp.arange(SLC_BLOCK)).reshape(B, G, Q_BLOCK, n_sel * SLC_BLOCK)
        s = jnp.einsum('bqgrd,bgqkd->bgrqk', qg, kb).astype(jnp.float32) * ATTN_SCALE
        p = _masked_softmax(s, (kpos <= t[None, None, :, None])[:, :, None])
        o_slc = jnp.einsum('bgrqk,bgqkd->bqgrd', p.astype(vb.dtype), vb)
        kw = lax.dynamic_slice_in_dim(k_win_pad, qb * Q_BLOCK, WINDOW_2 + Q_BLOCK, axis=1)
        vw = lax.dynamic_slice_in_dim(v_win_pad, qb * Q_BLOCK, WINDOW_2 + Q_BLOCK, axis=1)
        wpos = qb * Q_BLOCK - WINDOW_2 + jnp.arange(WINDOW_2 + Q_BLOCK, dtype=jnp.int32)
        wmask = (wpos[None, :] <= t[:, None]) & (wpos[None, :] > t[:, None] - WINDOW_2) & (wpos[None, :] >= 0)
        s = jnp.einsum('bqgrd,bkgd->bgrqk', qg, kw).astype(jnp.float32) * ATTN_SCALE
        p = _masked_softmax(s, wmask)
        o_win = jnp.einsum('bgrqk,bkgd->bqgrd', p.astype(vw.dtype), vw)
        gt = gt.reshape(B, Q_BLOCK, G, R, 3)
        o_nsa = o_cmp * gt[..., 0:1] + o_slc * gt[..., 1:2] + o_win * gt[..., 2:3]

        return jnp.concatenate([o_dsa.reshape(B, Q_BLOCK, -1), o_nsa.reshape(B, Q_BLOCK, -1)], axis=-1)

    xs = (jnp.arange(n_qb, dtype=jnp.int32), blocks(q_d), blocks(q_i), blocks(w_i), blocks(q_n), blocks(gates))
    o = lax.map(step, xs)
    o = jnp.moveaxis(o, 0, 1).reshape(B, L, MIX_WIDTH)
    return o @ w_out

def _memory_xattn(h, mem, mem_norm_g, w_xq, w_xk, w_xv, xq_norm_g, xk_norm_g, w_xo):
    B, L, _ = h.shape
    M = mem.shape[1]
    m = _rms_norm(mem, mem_norm_g)
    q = _rms_norm((h @ w_xq).reshape(B, L, XATTN_HEADS, XATTN_HEAD_DIM), xq_norm_g)
    k = _rms_norm((m @ w_xk).reshape(B, M, XATTN_HEADS, XATTN_HEAD_DIM), xk_norm_g)
    v = (m @ w_xv).reshape(B, M, XATTN_HEADS, XATTN_HEAD_DIM)
    s = jnp.einsum('bqhd,bmhd->bhqm', q, k).astype(jnp.float32) * (XATTN_HEAD_DIM ** -0.5)
    p = jax.nn.softmax(s, axis=-1).astype(v.dtype)
    o = jnp.einsum('bhqm,bmhd->bqhd', p, v).reshape(B, L, XATTN_HEADS * XATTN_HEAD_DIM)
    return o @ w_xo

def _sq_relu_mlp(h, w_ff_in, w_ff_out):
    return jnp.square(jax.nn.relu(h @ w_ff_in)) @ w_ff_out

def second_inputs(seed: int = 0) -> dict:
    key = jax.random.key(seed)
    D = HEAD_DIM
    specs = [
        ("norm1_g", (D_MODEL,), "g", 1),
        ("w_in", (D_MODEL, IN_WIDTH), "w", D_MODEL),
        ("dsa_cq_g", (DSA_Q_RANK,), "g", 1),
        ("dsa_ckv_g", (DSA_KV_RANK,), "g", 1),
        ("w_dsa_uq", (DSA_Q_RANK, DSA_HEADS * D), "w", DSA_Q_RANK),
        ("w_dsa_ukv", (DSA_KV_RANK, 2 * D), "w", DSA_KV_RANK),
        ("w_idx_q", (DSA_Q_RANK, IDX_HEADS * IDX_DIM), "w", DSA_Q_RANK),
        ("idx_k_ln_g", (IDX_DIM,), "g", 1),
        ("idx_k_ln_b", (IDX_DIM,), "b", 1),
        ("dsa_qn_g", (D,), "g", 1),
        ("dsa_kn_g", (D,), "g", 1),
        ("nsa_cmp_pe", (2, CMP_BLOCK, D), "b", 1),
        ("w_nsa_cmp", (2, CMP_BLOCK, D, D), "w", CMP_BLOCK * D),
        ("nsa_qn_g", (D,), "g", 1),
        ("nsa_kn_g", (3, D), "g", 1),
        ("w_out", (MIX_WIDTH, D_MODEL), "w", MIX_WIDTH),
        ("norm2_g", (D_MODEL,), "g", 1),
        ("mem_norm_g", (D_MODEL,), "g", 1),
        ("w_xq", (D_MODEL, XATTN_HEADS * XATTN_HEAD_DIM), "w", D_MODEL),
        ("w_xk", (D_MODEL, XATTN_HEADS * XATTN_HEAD_DIM), "w", D_MODEL),
        ("w_xv", (D_MODEL, XATTN_HEADS * XATTN_HEAD_DIM), "w", D_MODEL),
        ("xq_norm_g", (XATTN_HEAD_DIM,), "g", 1),
        ("xk_norm_g", (XATTN_HEAD_DIM,), "g", 1),
        ("w_xo", (XATTN_HEADS * XATTN_HEAD_DIM, D_MODEL), "w", XATTN_HEADS * XATTN_HEAD_DIM),
        ("norm3_g", (D_MODEL,), "g", 1),
        ("w_ff_in", (D_MODEL, D_FF), "w", D_MODEL),
        ("w_ff_out", (D_FF, D_MODEL), "w", D_FF),
    ]
    keys = jax.random.split(key, len(specs) + 2)
    out = {
        "x": jax.random.normal(keys[0], (BATCH, SEQ, D_MODEL), jnp.float32),
        "mem": jax.random.normal(keys[1], (BATCH, MEM_LEN, D_MODEL), jnp.float32),
    }
    for k, (name, shape, kind, fan) in zip(keys[2:], specs):
        z = jax.random.normal(k, (DEPTH_2,) + shape, jnp.float32)
        if kind == "w":
            out[name] = z * (fan ** -0.5)
        elif kind == "g":
            out[name] = 1.0 + 0.02 * z
        else:
            out[name] = 0.02 * z
    return out

def second_block(x, mem, norm1_g, w_in, dsa_cq_g, dsa_ckv_g, w_dsa_uq, w_dsa_ukv, w_idx_q, idx_k_ln_g, idx_k_ln_b,
              dsa_qn_g, dsa_kn_g, nsa_cmp_pe, w_nsa_cmp, nsa_qn_g, nsa_kn_g, w_out, norm2_g, mem_norm_g,
              w_xq, w_xk, w_xv, xq_norm_g, xk_norm_g, w_xo, norm3_g, w_ff_in, w_ff_out):
    for l in range(DEPTH_2):
        x = x + _hybrid_mixer(_rms_norm(x, norm1_g[l]), w_in[l], dsa_cq_g[l], dsa_ckv_g[l], w_dsa_uq[l],
                              w_dsa_ukv[l], w_idx_q[l], idx_k_ln_g[l], idx_k_ln_b[l], dsa_qn_g[l], dsa_kn_g[l],
                              nsa_cmp_pe[l], w_nsa_cmp[l], nsa_qn_g[l], nsa_kn_g[l], w_out[l])
        x = x + _memory_xattn(_rms_norm(x, norm2_g[l]), mem, mem_norm_g[l], w_xq[l], w_xk[l], w_xv[l],
                              xq_norm_g[l], xk_norm_g[l], w_xo[l])
        x = x + _sq_relu_mlp(_rms_norm(x, norm3_g[l]), w_ff_in[l], w_ff_out[l])
    return x


def setup_inputs(seed=0):
    out = dict(first_inputs(seed))
    for name, value in second_inputs(seed + 1).items():
        if name != "x":
            out[name + "_2"] = value
    return out


def reference(
    x, norm_mix, w_in, b_gate, attn_sinks, w_attn_o, conv_w, w_conv_o, ssm_a_re, ssm_a_im,
    ssm_b_re, ssm_b_im, ssm_c_re, ssm_c_im, ssm_d, ssm_log_dt, w_ssm_glu, w_ssm_o, w_mix_o,
    norm_ffn, w_ffn_in, w_ffn_out, norm_final, mem_2, norm1_g_2, w_in_2, dsa_cq_g_2,
    dsa_ckv_g_2, w_dsa_uq_2, w_dsa_ukv_2, w_idx_q_2, idx_k_ln_g_2, idx_k_ln_b_2, dsa_qn_g_2,
    dsa_kn_g_2, nsa_cmp_pe_2, w_nsa_cmp_2, nsa_qn_g_2, nsa_kn_g_2, w_out_2, norm2_g_2,
    mem_norm_g_2, w_xq_2, w_xk_2, w_xv_2, xq_norm_g_2, xk_norm_g_2, w_xo_2, norm3_g_2,
    w_ff_in_2, w_ff_out_2,
):
    x = first_block(
        x, norm_mix, w_in, b_gate, attn_sinks, w_attn_o, conv_w, w_conv_o, ssm_a_re, ssm_a_im,
        ssm_b_re, ssm_b_im, ssm_c_re, ssm_c_im, ssm_d, ssm_log_dt, w_ssm_glu, w_ssm_o, w_mix_o,
        norm_ffn, w_ffn_in, w_ffn_out, norm_final,
    )
    return second_block(
        x, mem_2, norm1_g_2, w_in_2, dsa_cq_g_2, dsa_ckv_g_2, w_dsa_uq_2, w_dsa_ukv_2,
        w_idx_q_2, idx_k_ln_g_2, idx_k_ln_b_2, dsa_qn_g_2, dsa_kn_g_2, nsa_cmp_pe_2,
        w_nsa_cmp_2, nsa_qn_g_2, nsa_kn_g_2, w_out_2, norm2_g_2, mem_norm_g_2, w_xq_2, w_xk_2,
        w_xv_2, xq_norm_g_2, xk_norm_g_2, w_xo_2, norm3_g_2, w_ff_in_2, w_ff_out_2,
    )


_drawn_inputs = setup_inputs


def setup_inputs(seed=0):
    import zlib

    import numpy as np

    out = dict(_drawn_inputs(seed))
    spreads = {}
    factors = {'b_gate': 5.421,
     'attn_sinks': 5.668,
     'ssm_a_re': 8.0,
     'ssm_b_re': 3.407,
     'ssm_b_im': 3.439,
     'ssm_c_re': 3.399,
     'ssm_c_im': 3.379,
     'ssm_log_dt': 2.7,
     'norm1_g_2': 3.794,
     'dsa_cq_g_2': 5.085,
     'dsa_ckv_g_2': 8.0,
     'idx_k_ln_g_2': 5.493,
     'idx_k_ln_b_2': 6.147,
     'dsa_qn_g_2': 8.0,
     'dsa_kn_g_2': 8.0,
     'nsa_cmp_pe_2': 8.0,
     'nsa_qn_g_2': 8.0,
     'nsa_kn_g_2': 8.0,
     'norm2_g_2': 8.0,
     'mem_norm_g_2': 8.0,
     'xq_norm_g_2': 8.0,
     'xk_norm_g_2': 8.0,
     'norm3_g_2': 9.64}
    for name, (base, spread) in spreads.items():
        noise = np.random.default_rng([zlib.crc32(name.encode()), seed]).standard_normal(out[name].shape)
        drawn = base * np.exp(spread * noise) if base else spread * noise
        out[name] = __import__('jax').numpy.asarray(drawn.astype(out[name].dtype))
    for name, factor in factors.items():
        out[name] = (out[name] * factor).astype(out[name].dtype)
    return out
```

```python
import math
from contextlib import ExitStack

import concourse.bass as bass
import numpy as np
from concourse import mybir

F32 = mybir.dt.float32
F32R = mybir.dt.float32r
ALU = mybir.AluOpType
ACT = mybir.ActivationFunctionType
AX_X = mybir.AxisListType.X

P = 128
SEQ = 512
NB = SEQ // P
D_MODEL = 1024
KD = D_MODEL // P
DEPTH = 2
HEAD = 64
HALF = 4
W_IN_COLS = dict(q=0, k=512, v=640, cb=768, cc=1280, cx=1792, u=2304, g=2816)
FFN_TILES = 22
FFN_CHUNKS = [(0, 8), (8, 8), (16, 6)]
FF2_CHUNKS = [(0, 8), (8, 8), (16, 8), (24, 8)]
EPS = 1e-6
NEG = -1e30
TAKEN = -3e38

SSM_STATE = 64
SSM_H = 16
SSM_T = 8
SSM_C = SEQ // SSM_T
SSM_G = P // SSM_H
SSM_PARAMS = 3 * SSM_G + 4 * SSM_G * SSM_H

CMP_N, CMP_L, CMP_STRIDE = 31, 32, 16
TOPK = 128
IDX_SCALE = 8 ** -0.5 * 64 ** -0.5
MEM = 256
XHEADS = 4

RAW_SLOTS = 4
SPLIT_SLOTS = 3
GEMM_BANKS = 3



def job_plan():
    jobs = []
    for l in range(DEPTH):
        jobs += [(("u", l, i), 8, SEQ, "act") for i in range(4)]
        jobs += [(("glu", l, i), 4, SEQ, "act") for i in range(4)]
        jobs += [(("q", l, i), 8, SEQ, "act") for i in range(4)]
        jobs += [(("k", l, 0), 8, SEQ, "act"), (("v", l, 0), 8, SEQ, "act")]
        for i in range(4):
            jobs += [(("cc", l, i), 8, SEQ, "act"), (("cx", l, i), 8, SEQ, "dve"), (("cb", l, i), 8, SEQ, "dve")]
        for i in range(KD):
            jobs += [(("g0", l, i), 8, SEQ, "act"), (("ao", l, i), 4, SEQ, "dve"),
                     (("g1", l, i), 8, SEQ, "act"), (("co", l, i), 4, SEQ, "dve"),
                     (("g2", l, i), 8, SEQ, "act"), (("so", l, i), 4, SEQ, "dve")]
        jobs += [(("mix", l, i), 8, SEQ, "dve") for i in range(KD)]
        for c, (t0, nt) in enumerate(FFN_CHUNKS):
            for t in range(t0, t0 + nt):
                jobs += [(("gt", l, t), 8, SEQ, "act"), (("up", l, t), 8, SEQ, "dve")]
            jobs += [(("fo", l, c, i), nt, SEQ, "dve") for i in range(KD)]
    for name in ("kc", "vc", "cq0", "cq1", "ckv", "wg"):
        jobs.append((("p2", name), 8, SEQ, "act"))
    for name in ("vs", "vw", "ki", "ks", "kw", "qn0", "qn1", "qn2", "qn3"):
        jobs.append((("p2", name), 8, SEQ, "act"))
    jobs += [(("kvd",), 1, SEQ, "act"), (("kd",), 1, SEQ, "act")]
    jobs += [(("iq", i), 2, SEQ, "act") for i in range(4)]
    jobs += [(("uq", i), 2, SEQ, "act") for i in range(4)]
    jobs += [(("out2", i), 8, SEQ, "dve") for i in range(KD)]
    jobs += [(("xk", i), 8, MEM, "act") for i in range(XHEADS)]
    jobs += [(("xv", i), 8, MEM, "act") for i in range(XHEADS)]
    jobs += [(("xq", i), 8, SEQ, "act") for i in range(XHEADS)]
    jobs += [(("xo", i), 4, SEQ, "dve") for i in range(KD)]
    for c, (t0, nt) in enumerate(FF2_CHUNKS):
        jobs += [(("fi", t), 8, SEQ, "act") for t in range(t0, t0 + nt)]
        jobs += [(("fo2", c, i), nt, SEQ, "dve") for i in range(KD)]
    return jobs


def weight_tile(w, key):
    kind = key[0]
    cols = lambda a, c, n=P: a[:, c:c + n]
    both = lambda a, c0, c1: np.concatenate([a[:, c0:c0 + HEAD], a[:, c1:c1 + HEAD]], 1)
    pairs = lambda a: np.concatenate(
        [np.concatenate([a[j * HEAD:(j + 1) * HEAD], a[(j + 4) * HEAD:(j + 5) * HEAD]]) for j in range(4)])
    if kind in ("u", "k", "v", "cc", "cx", "cb"):
        return cols(w["w_in"][key[1]], W_IN_COLS[kind] + P * key[2])
    if kind in ("g0", "g1", "g2"):
        return cols(w["w_in"][key[1]], W_IN_COLS["g"] + D_MODEL * int(kind[1]) + P * key[2])
    if kind == "q":
        return both(w["w_in"][key[1]], key[2] * HEAD, (key[2] + 4) * HEAD)
    if kind == "glu":
        return cols(w["w_ssm_glu"][key[1]], P * key[2])
    if kind == "ao":
        return cols(pairs(w["w_attn_o"][key[1]]), P * key[2])
    if kind == "co":
        return cols(w["w_conv_o"][key[1]], P * key[2])
    if kind == "so":
        return cols(w["w_ssm_o"][key[1]], P * key[2])
    if kind == "mix":
        return cols(w["w_mix_o"][key[1]], P * key[2])
    if kind in ("gt", "up"):
        return cols(w["w_ffn_in"][key[1]], P * key[2] + (FFN_TILES * P if kind == "up" else 0))
    if kind == "fo":
        t0, nt = FFN_CHUNKS[key[2]]
        return cols(w["w_ffn_out"][key[1]][t0 * P:(t0 + nt) * P], P * key[3])
    if kind == "p2":
        a, name = w["w_in_2"][0], key[1]
        if name in ("cq0", "cq1", "ckv"):
            return cols(a, {"cq0": 0, "cq1": 128, "ckv": 256}[name])
        if name == "ki":
            return both(a, 384, 384)
        if name == "wg":
            return np.concatenate([a[:, 448:456], a[:, 1640:1760]], 1)
        if name[:2] == "qn":
            j = int(name[2])
            return both(a, 456 + j * HEAD, 456 + (j + 4) * HEAD)
        return cols(a, 968 + {"kc": 0, "vc": 1, "ks": 2, "vs": 3, "kw": 4, "vw": 5}[name] * P)
    if kind == "kvd":
        return w["w_dsa_ukv_2"][0]
    if kind == "kd":
        return both(w["w_dsa_ukv_2"][0], 0, 0)
    if kind == "iq":
        return cols(w["w_idx_q_2"][0], P * key[1])
    if kind == "uq":
        return cols(w["w_dsa_uq_2"][0], P * key[1])
    if kind == "out2":
        a = w["w_out_2"][0]
        return cols(np.concatenate([a[:512], pairs(a[512:])]), P * key[1])
    if kind in ("xk", "xv", "xq", "xo"):
        return cols(w["w_" + kind + "_2"][0], P * key[1])
    if kind == "fi":
        return cols(w["w_ff_in_2"][0], P * key[1])
    if kind == "fo2":
        t0, nt = FF2_CHUNKS[key[1]]
        return cols(w["w_ff_out_2"][0][t0 * P:(t0 + nt) * P], P * key[2])
    raise KeyError(key)




def param_columns():
    at, n = {}, 0
    for l in range(DEPTH):
        for name, c in (("norm_mix", 8), ("norm_ffn", 8), ("b_gate", 24), ("sinks", 8), ("conv", 12), ("ssm_d", 4)):
            at[name, l] = (n, c)
            n += c
    for name, c in (("norm_final", 8), ("norm1", 8), ("norm2", 8), ("norm3", 8), ("mem_norm", 8), ("cq", 2),
                    ("ckv", 1), ("lng", 1), ("lnb", 1), ("dqn", 1), ("dkn", 1), ("nqn", 1), ("nkn", 3),
                    ("xqn", 1), ("xkn", 1), ("pe", 64)):
        at[name] = (n, c)
        n += c
    return at, n


def pack_params(w):
    at, n = param_columns()
    out = np.zeros((P, n), np.float32)

    def put(key, a):
        c, m = at[key]
        out[:, c:c + m] = a

    feat = lambda v: np.asarray(v).reshape(-1, P).T
    twice = lambda v: np.concatenate([v, v])
    for l in range(DEPTH):
        put(("norm_mix", l), feat(w["norm_mix"][l]))
        put(("norm_ffn", l), feat(w["norm_ffn"][l]))
        put(("b_gate", l), feat(w["b_gate"][l]))
        put(("sinks", l), np.broadcast_to(w["attn_sinks"][l], (P, 8)))
        put(("conv", l), feat(w["conv_w"][l].reshape(-1)))
        put(("ssm_d", l), feat(w["ssm_d"][l]))
    put("norm_final", feat(w["norm_final"]))
    put("norm1", feat(w["norm1_g_2"][0]))
    put("norm2", feat(w["norm2_g_2"][0]))
    put("norm3", feat(w["norm3_g_2"][0]))
    put("mem_norm", feat(w["mem_norm_g_2"][0]))
    put("cq", feat(w["dsa_cq_g_2"][0]))
    put("ckv", feat(w["dsa_ckv_g_2"][0]))
    put("lng", twice(w["idx_k_ln_g_2"][0])[:, None])
    put("lnb", twice(w["idx_k_ln_b_2"][0])[:, None])
    put("dqn", twice(w["dsa_qn_g_2"][0])[:, None])
    put("dkn", twice(w["dsa_kn_g_2"][0])[:, None])
    put("nqn", twice(w["nsa_qn_g_2"][0])[:, None])
    put("nkn", twice(w["nsa_kn_g_2"][0].T))
    put("xqn", w["xq_norm_g_2"][0][:, None])
    put("xkn", w["xk_norm_g_2"][0][:, None])
    pe = w["nsa_cmp_pe_2"][0]
    put("pe", twice(pe.transpose(2, 0, 1).reshape(HEAD, 64)))
    return out


def pack_ssm(w):
    out = np.zeros((DEPTH * 4, P, SSM_PARAMS), np.float32)
    for l in range(DEPTH):
        for ft in range(4):
            g = slice(ft * SSM_G, (ft + 1) * SSM_G)
            re, im = w["ssm_a_re"][l, g].T, w["ssm_a_im"][l, g].T
            br = w["ssm_b_re"][l, g].transpose(1, 0, 2).reshape(SSM_STATE, -1)
            bi = w["ssm_b_im"][l, g].transpose(1, 0, 2).reshape(SSM_STATE, -1)
            cr = w["ssm_c_re"][l, g].transpose(2, 0, 1).reshape(SSM_STATE, -1)
            ci = w["ssm_c_im"][l, g].transpose(2, 0, 1).reshape(SSM_STATE, -1)
            dt = np.broadcast_to(w["ssm_log_dt"][l, g], (SSM_STATE, SSM_G))
            top = np.concatenate([re, im, dt, br, bi, cr, ci], 1)
            low = np.concatenate([re, im, dt, bi, br, ci, cr], 1)
            out[l * 4 + ft] = np.concatenate([top, low])
    return out




CONST_MATS = ("ident", "ones", "blk", "rot1", "rot2")
CONST_AT = {n: i * P for i, n in enumerate(CONST_MATS)}
_n = len(CONST_MATS) * P
for _name, _c in (("C1", SEQ), ("S1", SEQ), ("C2", SEQ), ("S2", SEQ), ("sw", 2 * P), ("mk", SEQ),
                  ("cmp_add", NB * CMP_N), ("cmp_mul", NB * CMP_N), ("J", 9), ("eps", 1), ("sgn", 1), ("neg", 1)):
    CONST_AT[_name] = _n
    _n += _c
CONST_N = _n


def constants():
    c = np.zeros((P, CONST_N), np.float32)

    def put(name, a):
        a = np.asarray(a, np.float32).reshape(P, -1)
        c[:, CONST_AT[name]:CONST_AT[name] + a.shape[1]] = a

    put("ident", np.eye(P))
    put("ones", np.full((P, P), 1.0 / D_MODEL))
    put("blk", np.kron(np.eye(2), np.full((HEAD, HEAD), 1.0 / HEAD)))

    def rotation(half):
        r = np.zeros((P, P))
        for base in (0, HEAD):
            for d in range(half):
                r[base + d + half, base + d] = -1.0
                r[base + d, base + d + half] = 1.0
        return r

    put("rot1", rotation(8))
    put("rot2", rotation(32))

    def tables(theta, half, width):
        pos = np.arange(SEQ, dtype=np.float32)
        inv = np.float32(theta) ** (-np.arange(half, dtype=np.float32) / np.float32(half))
        if width == 16:
            inv = np.float32(theta) ** (-np.arange(0, 16, 2, dtype=np.float32) / np.float32(16))
        ang = (pos[:, None] * inv.astype(np.float32)[None, :]).astype(np.float32).astype(np.float64)
        co, si = np.cos(ang).T, np.sin(ang).T
        ct, st = np.ones((HEAD, SEQ)), np.zeros((HEAD, SEQ))
        ct[:half], ct[half:2 * half] = co, co
        st[:half], st[half:2 * half] = si, si
        return np.concatenate([ct, ct]), np.concatenate([st, st])

    a, b = tables(500000.0, 8, 16)
    put("C1", a)
    put("S1", b)
    a, b = tables(10000.0, 32, 64)
    put("C2", a)
    put("S2", b)
    qi, kj = np.arange(P)[:, None], np.arange(2 * P)[None, :]
    delta = qi + P - kj
    put("sw", np.where((delta >= 0) & (delta < P), 0.0, NEG))
    mk = np.zeros((P, SEQ))
    mk[:, SEQ - P:] = np.where(np.arange(P)[None, :] <= qi, 0.0, NEG)
    put("mk", mk)
    t = np.arange(NB)[None, :, None] * P + np.arange(P)[:, None, None]
    ok = np.arange(CMP_N)[None, None, :] * CMP_STRIDE + CMP_L - 1 <= t
    put("cmp_add", np.where(ok, 0.0, NEG))
    put("cmp_mul", ok)
    put("J", np.broadcast_to(np.arange(9), (P, 9)))
    put("eps", np.full(P, EPS))
    put("sgn", np.where(np.arange(P) < HEAD, 1.0, -1.0))
    put("neg", np.full(P, -1.0))
    return c




def units_sw(l):
    out = []
    for b in range(NB):
        for j in range(4):
            out.append(dict(kind="sw", l=l, b=b, j=j, W=P if b == 0 else 2 * P, k0=0 if b == 0 else (b - 1) * P,
                            first=True, last=True))
    return out


def units_dsa(b):
    return [dict(kind="dsa", b=b, j=j, W=(b + 1) * P, k0=0, first=True, last=True) for j in range(4)]


def units_nsa(b):
    out = []
    for j in range(4):
        out.append(dict(kind="cmp", b=b, j=j, W=CMP_N, k0=0, first=True, last=False))
        out.append(dict(kind="slc", b=b, j=j, W=(b + 1) * P, k0=0, first=False, last=False))
        out.append(dict(kind="win", b=b, j=j, W=(b + 1) * P, k0=0, first=False, last=True))
    return out


def units_x():
    return [dict(kind="x", b=b, j=j, W=MEM, k0=0, first=True, last=True) for b in range(NB) for j in range(2)]


def all_units():
    lists = {"sw0": units_sw(0), "sw1": units_sw(1)}
    for b in range(NB):
        lists["dsa", b] = units_dsa(b)
        lists["nsa", b] = units_nsa(b)
    lists["x"] = units_x()
    n = g = 0
    for us in lists.values():
        for u in us:
            u["n"], u["group"] = n, g
            n += 1
            g += u["last"]
    return lists


class Line:

    def __init__(self, eng, chain):
        self.eng, self.chain, self.count = eng, chain, {}

    def done(self, ins, sem=None):
        sem = sem or self.chain
        ins.then_inc(sem, 1)
        self.count[sem.name] = self.count.get(sem.name, 0) + 1
        self.eng.wait_ge(sem, self.count[sem.name])


def block_program(nc, wstream, params, ssmp, cmpw, consts, xT, memT, outT):
    jobs = job_plan()
    offset, number, taken = {}, {}, {}
    at = 0
    free_count = {"act": 0, "dve": 0}
    for n, (key, K, N, who) in enumerate(jobs):
        offset[key], number[key] = at, n
        at += K * P * P
        free_count[who] += 1
        taken[key] = (who, free_count[who])
    units = all_units()
    pcol, npar = param_columns()

    ctx = ExitStack()
    with ctx:
        def sem(name):
            return ctx.enter_context(nc.semaphore(name))

        base = (nc.sbuf_base + 63) // 64 * 64
        cursor = [base]

        def place(name, shape, dt, at=None):
            size = 4 * int(np.prod(shape[1:]))
            off = cursor[0] if at is None else at
            if at is None:
                cursor[0] += (size + 31) // 32 * 32
            return nc.alloc_sbuf_tensor_at(name, shape, dt, offset=off), off

        X, _ = place("x", [P, KD, SEQ], F32)
        Hh, _ = place("h_hi", [P, KD, SEQ], F32R)
        Hl, _ = place("h_lo", [P, KD, SEQ], F32R)
        Mh, m_at = place("m_hi", [P, KD, SEQ], F32R)
        Ml, _ = place("m_lo", [P, KD, SEQ], F32R)
        Bh, b_at = place("b_hi", [P, 12, SEQ], F32R)
        Bl, _ = place("b_lo", [P, 12, SEQ], F32R)
        R, _ = place("work_m", [P, 2 * KD * SEQ], F32, at=m_at)
        R2, _ = place("work_b", [P, 24 * SEQ], F32, at=b_at)
        raw, _ = place("w_raw", [P, RAW_SLOTS, 8 * P], F32)
        Wh, _ = place("w_hi", [P, SPLIT_SLOTS, 8, P], F32R)
        Wl, _ = place("w_lo", [P, SPLIT_SLOTS, 8, P], F32R)
        CON, _ = place("consts", [P, CONST_N], F32)
        PAR, _ = place("params", [P, npar], F32)
        acc, _ = place("square_sum", [P, SEQ], F32)
        rinv, _ = place("rinv", [P, SEQ], F32)
        tmp, _ = place("tmp", [P, 3, SEQ], F32)
        rawt, _ = place("raw_tile", [P, 2, SEQ], F32)
        stat, _ = place("stats", [P, 2, 24], F32)
        gtok, _ = place("gate_tok", [P, NB, 24], F32)
        wtok, _ = place("widx_tok", [P, NB, 8], F32)
        m8, _ = place("max8", [P, 8], F32)
        TS, _ = place("small_work", [P, 2400], F32)
        assert cursor[0] <= nc.sbuf_usable_end, (cursor[0], nc.sbuf_usable_end)

        psG = ctx.enter_context(nc.psum_tensor("psG", [P, GEMM_BANKS, SEQ], F32))
        psS = ctx.enter_context(nc.psum_tensor("psS", [P, 2, SEQ], F32))
        psT = ctx.enter_context(nc.psum_tensor("psT", [P, 2, SEQ], F32))
        psO = ctx.enter_context(nc.psum_tensor("psO", [P, SEQ], F32))

        def con(name, n, rows=P):
            return CON[0:rows, CONST_AT[name]:CONST_AT[name] + n]

        ident, ones, blk = con("ident", P), con("ones", P), con("blk", P)
        rots = {1: con("rot1", P), 2: con("rot2", P)}
        tabs = {1: (con("C1", SEQ), con("S1", SEQ)), 2: (con("C2", SEQ), con("S2", SEQ))}
        eps = con("eps", 1)

        def par(key, i=0, n=1):
            c, _ = pcol[key]
            return PAR[:, c + i:c + i + n]

        s_raw = [sem(f"weights_landed{i}") for i in range(RAW_SLOTS)]
        s_hi = sem("weights_hi")
        s_split = sem("weights_split")
        s_job = sem("product_done")
        s_took = {"act": sem("product_taken_act"), "dve": sem("product_taken_dve")}
        s_in = sem("inputs_landed")
        s_mem = sem("memory_landed")
        s_ssmp = [sem("ssm_params_landed0"), sem("ssm_params_landed1")]
        s_toep = sem("toeplitz_landed")
        s_cw = sem("cmp_weights_landed")
        s_out = sem("out_landed")
        c_act, c_dve = sem("act_chain"), sem("dve_chain")
        s_ssq, s_ms, s_sd, s_h = sem("squares_summed"), sem("mean_square"), sem("norm_root"), sem("h_ready")
        s_y = sem("final_x_ready")
        names = ("par_ready y1 args sincos consts_ready wb w12 x1 g_out g_pad wbt wbt_sb u2 u2_sb ug ug_sb e z yc yc_sb yt "
                 "ypre ys ysplit glu_sig glu_out").split()
        v = {n: sem("ssm_" + n) for n in names}
        s_rawt, s_rot, s_rope = sem("rope_in"), sem("rotated"), sem("roped")
        s_vraw, s_vt, s_vtok = sem("v_raw"), sem("v_transposed"), sem("v_tok")
        s_cc, s_cy = sem("conv_cc"), sem("conv_y")
        s_sig, s_merged = sem("gate_sigmoid"), sem("merged")
        s_silu, s_hid = sem("silu"), sem("hidden")
        s_sc, s_masked, s_neg, s_exp = sem("scores"), sem("masked"), sem("neg_max"), sem("exped")
        s_prob, s_tr, s_pt, s_pv, s_oe = (sem(x) for x in ("probs", "probs_t", "probs_t_sb", "pv", "attn_out"))
        s_is, s_ir, s_ia, s_sel = sem("idx_scores"), sem("idx_relu"), sem("idx_added"), sem("selected")
        s_p = {n: sem("post_" + n) for n in ("raw", "cmean", "cen", "sq", "mean", "sd", "qn", "rot", "out", "tok", "toksb")}
        s_cmpin, s_cmpo, s_relu2 = sem("cmp_in"), sem("cmp_out"), sem("relu")

        block = ctx.enter_context(nc.Block())

        def work(t, off, shape):
            n = int(np.prod(shape[1:]))
            a = t[0:shape[0], off:off + n]
            if len(shape) == 3:
                a = a.rearrange("p (a b) -> p a b", b=shape[2])
            elif len(shape) == 4:
                a = a.rearrange("p (a b c) -> p a b c", b=shape[2], c=shape[3])
            return a

        uT = work(R, 0, [P, 4, SEQ])
        ysf = work(R, 2048, [P, 4, SEQ])
        U2 = work(R, 4096, [SSM_C, SSM_G, P])
        UG = work(R, 5120, [P, SSM_G, SSM_C])
        zb = [work(R, 5632 + 512 * i, [P, SSM_G, SSM_C]) for i in range(3)]
        Y2 = work(R, 7168, [SSM_C, SSM_T, P])
        qT1, kT1, vt1 = work(R, 0, [P, 4, SEQ]), work(R, 4096, [P, SEQ]), work(R, 4608, [P, NB, P])
        sp = [work(R2, SSM_PARAMS * i, [P, SSM_PARAMS]) for i in range(2)]
        o = 2 * SSM_PARAMS
        WbE = work(R2, o, [P, SSM_G, SSM_T, SSM_H])
        WbI = work(R2, o + 1024, [P, SSM_G, SSM_T, SSM_H])
        W1 = work(R2, o + 2048, [P, SSM_G, SSM_T + 1, SSM_H])
        W2 = work(R2, o + 3200, [P, SSM_G, SSM_T, SSM_H])
        TO = work(R2, o + 4224, [P, SSM_G, P])
        WT = work(R2, o + 5248, [P, SSM_G, P])
        WTI = work(R2, o + 6272, [P, SSM_G, P])
        rotC = work(R2, o + 7296, [P, SSM_G, SSM_C])
        rotS = work(R2, o + 7808, [P, SSM_G, SSM_C])
        Gp = work(R2, o + 8320, [SSM_H, SSM_G, 15 * SSM_H])
        X1 = work(R2, o + 10240, [P, SSM_G, SSM_H])
        acoef = work(R2, o + 10368, [P, SSM_G, SSM_C])
        assert o + 10880 <= 24 * SEQ
        NJ = 9 + 8 + 8
        arg = work(TS, 0, [P, SSM_G, NJ])
        arg2 = work(TS, 200, [P, SSM_G, NJ])
        sn = work(TS, 400, [P, SSM_G, NJ])
        cs = work(TS, 600, [P, SSM_G, NJ])
        red = work(TS, 800, [P, SSM_G, NJ])
        mag = work(TS, 1000, [P, SSM_G, 9])
        Lr = work(TS, 1072, [P, SSM_G, 9])
        Li = work(TS, 1144, [P, SSM_G, 9])
        Lcr = work(TS, 1216, [P, SSM_G, 8])
        Lci = work(TS, 1280, [P, SSM_G, 8])
        sm = work(TS, 1344, [P, 16, SSM_G])
        Z1 = work(TS, 1472, [P, SSM_G, SSM_H])
        Z2 = work(TS, 1600, [P, SSM_G, SSM_H])
        Y1n = work(TS, 1728, [P, SSM_G, SSM_H])
        pwork = tmp[:, :, :].rearrange("p a b -> p (a b)")[:, 0:1152]
        zc = work(TS, 0, [P, SEQ + 2])
        ycv = work(TS, 514, [P, SEQ])
        qn, qd, qi = (work(R, 2048 * i, [P, 4, SEQ]) for i in range(3))
        kd, ki, ks, kw = (work(R, 6144 + 512 * i, [P, SEQ]) for i in range(4))
        vd, vs, vw = work(R2, 0, [P, NB, HEAD]), work(R2, 256, [P, NB, P]), work(R2, 768, [P, NB, P])
        vc, kc = work(R2, 1280, [P, P]), work(R2, 1408, [P, CMP_N])
        iacc, iwork, selm = work(R2, 1536, [P, SEQ]), work(R2, 2048, [P, SEQ]), work(R2, 2560, [P, SEQ])
        irelu = work(R2, 3072, [P, 2, SEQ])
        cmpW = work(R2, 6144, [P, 2, CMP_L, HEAD])
        cmpin = work(TS, 0, [P, CMP_L, CMP_N])
        cmpt = work(TS, 1000, [P, 2, CMP_N])
        cqf = work(TS, 0, [P, 3, SEQ])
        qx, kx, vx = work(R, 0, [P, 4, SEQ]), work(R, 2048, [P, XHEADS, MEM]), work(R, 3072, [P, 2, XHEADS * P])
        memf = work(R, 4096, [P, KD, MEM])
        mH = Bh[:, 0:4, :].rearrange("p a b -> p (a b)").rearrange("p (k n) -> p k n", n=MEM)
        mL = Bl[:, 0:4, :].rearrange("p a b -> p (a b)").rearrange("p (k n) -> p k n", n=MEM)

        def probs(u):
            i, W = u["n"] % 2, u["W"]
            if u["kind"] == "sw":
                p = work(R, 5120 + 1024 * i, [P, 2, 2 * P])
                t = work(R, 7168 + 512 * i, [P, 2, 2, P])
            else:
                p = work(R2, 4096 + 1024 * i, [P, 2, SEQ])
                t = work(R2, 6144 + 1024 * i, [P, 2, NB, P])
            return p[:, :, 0:W], t

        def key_blocks(u):
            return [(0, u["W"])] if u["kind"] == "cmp" else [(i, P) for i in range(u["W"] // P)]

        def moving(key, k):
            kind = key[0]
            if kind == "glu":
                return Bh[:, 4 + k, :], Bl[:, 4 + k, :]
            if kind == "ao":
                return Bh[:, k, :], Bl[:, k, :]
            if kind == "co":
                return Bh[:, 4 + k, :], Bl[:, 4 + k, :]
            if kind == "so":
                return Bh[:, 8 + k, :], Bl[:, 8 + k, :]
            if kind in ("mix", "fo", "fo2"):
                return Mh[:, k, :], Ml[:, k, :]
            if kind in ("iq", "uq"):
                return Bh[:, 8 + k, :], Bl[:, 8 + k, :]
            if kind in ("kd", "kvd"):
                return Bh[:, 10, :], Bl[:, 10, :]
            if kind in ("xk", "xv"):
                return mH[:, k, :], mL[:, k, :]
            return Hh[:, k, :], Hl[:, k, :]

        NORMS = {"mix0": 0, "ffn0": 1, "mix1": 2, "ffn1": 3, "final": 4, "norm1": 5, "mem": 6, "norm2": 7, "norm3": 8}
        h_tiles, n = {}, 0
        for name in NORMS:
            if name != "final":
                h_tiles[name] = n
                n += KD
        POST = [("cq0", "cq"), ("cq1", "cq"), ("ckv", "ckv")]

        posts = []
        for key, kind, gain, dest in (
            [(("p2", "kc"), "cmpk", "nkn", None), (("p2", "vc"), "cmpv", None, None)]
            + [(("p2", "cq0"), "lat", None, 0), (("p2", "cq1"), "lat2", None, 1), (("p2", "ckv"), "lat1", None, 2)]
            + [(("p2", "wg"), "tokwg", None, None), (("p2", "vs"), "tok", None, "vs"), (("p2", "vw"), "tok", None, "vw")]
            + [(("p2", "ki"), "ln", None, ki)]
            + [(("p2", "ks"), "rms", ("nkn", 1), ks), (("p2", "kw"), "rms", ("nkn", 2), kw)]
            + [(("p2", f"qn{j}"), "rms", ("nqn", 0), qn[:, j]) for j in range(4)]
            + [(("kvd",), "tokd", None, "vd"), (("kd",), "rms", ("dkn", 0), kd)]
            + [(("iq", j), "rope", None, qi[:, j]) for j in range(4)]
            + [(("uq", j), "rms", ("dqn", 0), qd[:, j]) for j in range(4)]
            + [(("xk", j), "xrms", ("xkn", 0), kx[:, j]) for j in range(4)]
            + [(("xv", j), "tokx", None, j) for j in range(4)]
            + [(("xq", j), "xrms", ("xqn", 0), qx[:, j]) for j in range(4)]
        ):
            posts.append(dict(key=key, kind=kind, gain=gain, dest=dest, i=len(posts)))
        STEPS = {"cmpk": "raw cen sq mean sd qn rot out", "cmpv": "raw cen tok toksb", "lat": "raw sq", "lat2": "raw sq mean sd out",
                 "lat1": "raw sq mean sd out", "tokwg": "raw tok toksb", "tok": "raw tok toksb", "tokd": "raw tok toksb",
                 "tokx": "raw tok toksb", "ln": "raw cmean cen sq mean sd qn rot out", "rms": "raw sq mean sd qn rot out",
                 "rope": "raw rot out", "xrms": "raw sq mean sd out"}
        tally = {n: 0 for n in s_p}
        for p in posts:
            for n in STEPS[p["kind"]].split():
                tally[n] += 1
                p[n] = tally[n]
            p["last"] = dict(tally)
        by_kind = {p["key"]: p for p in posts}
        block2_posts = [p for p in posts if p["key"][0] not in ("xk", "xv", "xq")]
        x_posts = [p for p in posts if p["key"][0] in ("xk", "xv", "xq")]

        def post_cols(p):
            return MEM if p["key"][0] in ("xk", "xv") else SEQ

        @block.sync
        def _(sp_eng):
            for n, (key, K, N, who) in enumerate(jobs):
                if n >= RAW_SLOTS:
                    sp_eng.wait_ge(s_split, n - RAW_SLOTS + 1)
                src = wstream[offset[key]:offset[key] + K * P * P].rearrange("(p f) -> p f", p=P)
                sp_eng.dma_start(raw[:, n % RAW_SLOTS, 0:K * P], src).then_inc(s_raw[n % RAW_SLOTS], 16)
            sp_eng.wait_ge(s_y, 1)
            sp_eng.dma_start(outT, X[:, :, :]).then_inc(s_out, 16)
            sp_eng.wait_ge(s_out, 16)

        @block.gpsimd
        def _(pool):
            for n, (key, K, N, who) in enumerate(jobs):
                pool.wait_ge(s_raw[n % RAW_SLOTS], 16 * (n // RAW_SLOTS + 1))
                if n >= SPLIT_SLOTS:
                    pool.wait_ge(s_job, n - SPLIT_SLOTS + 1)
                w = raw[:, n % RAW_SLOTS, 0:K * P]
                hi = Wh[:, n % SPLIT_SLOTS, 0:K, :].rearrange("p k n -> p (k n)")
                lo = Wl[:, n % SPLIT_SLOTS, 0:K, :].rearrange("p k n -> p (k n)")
                pool.tensor_scalar(hi, w, 1.0, 0.0, ALU.mult, ALU.add).then_inc(s_hi, 1)
                pool.wait_ge(s_hi, n + 1)
                pool.tensor_tensor(lo, w, hi.bitcast(F32), ALU.subtract).then_inc(s_split, 1)

        group_total = {"nsa": units["nsa", NB - 1][-1]["group"] + 1, "x": units["x"][-1]["group"] + 1}

        @block.tensor
        def _(pe):
            def product(key):
                n = number[key]
                _, K, N, who = jobs[n]
                pe.wait_ge(s_split, n + 1)
                if n >= GEMM_BANKS:
                    who0, count = taken[jobs[n - GEMM_BANKS][0]]
                    pe.wait_ge(s_took[who0], count)
                out = psG[:, n % GEMM_BANKS, 0:N]
                for k in range(K):
                    hi, lo = moving(key, k)
                    need = h_need(key, k)
                    if need:
                        pe.wait_ge(*need)
                    whi, wlo = Wh[:, n % SPLIT_SLOTS, k, :], Wl[:, n % SPLIT_SLOTS, k, :]
                    pe.matmul(out, whi, hi, start=(k == 0), stop=False)
                    pe.matmul(out, whi, lo, start=False, stop=False)
                    ins = pe.matmul(out, wlo, hi, start=False, stop=(k == K - 1))
                ins.then_inc(s_job, 1)

            def h_need(key, k):
                kind = key[0]
                if kind == "u":
                    return (s_h, h_tiles[f"mix{key[1]}"] + k + 1) if key[2] == 0 else None
                if kind == "gt" and key[2] == 0:
                    return s_h, h_tiles[f"ffn{key[1]}"] + k + 1
                if kind == "p2" and key[1] == "kc":
                    return s_h, h_tiles["norm1"] + k + 1
                if kind == "xk" and key[1] == 0:
                    return s_h, h_tiles["mem"] + k + 1
                if kind == "xq" and key[1] == 0:
                    return s_h, h_tiles["norm2"] + k + 1
                if kind == "fi" and key[1] == 0:
                    return s_h, h_tiles["norm3"] + k + 1
                if kind == "glu" and key[2] == 0:
                    return v["ysplit"], key[1] * 4 + k + 1
                if kind == "ao" and key[2] == 0:
                    return s_oe, 16 * (key[1] + 1)
                if kind == "co" and key[2] == 0:
                    return s_cy, 4 * (key[1] + 1)
                if kind == "so" and key[2] == 0:
                    return v["glu_out"], 4 * (key[1] + 1)
                if kind == "mix" and key[2] == 0:
                    return s_merged, 8 * key[1] + k + 1
                if kind == "fo" and key[3] == 0:
                    return s_hid, FFN_TILES * key[1] + FFN_CHUNKS[key[2]][0] + k + 1
                if kind == "fo2" and key[2] == 0:
                    return s_hid, FFN_TILES * DEPTH + FF2_CHUNKS[key[1]][0] + k + 1
                if kind in ("kvd", "iq") and key in (("kvd",), ("iq", 0)):
                    p = by_kind["p2", "ckv" if kind == "kvd" else "cq1"]
                    return s_p["out"], p["out"]
                if kind == "out2" and key[1] == 0:
                    return s_oe, group_total["nsa"]
                if kind == "xo" and key[1] == 0:
                    return s_oe, group_total["x"]
                return None

            def mean_square(name, cols=SEQ):
                pe.wait_ge(s_ssq, NORMS[name] + 1)
                pe.matmul(psO[:, 0:cols], ones, acc[:, 0:cols], start=True, stop=True).then_inc(s_ms, 1)

            def ssm(l, ft):
                f = l * 4 + ft
                pe.wait_ge(v["w12"], f + 1)
                for g in range(SSM_G):
                    ins = pe.matmul(psS[0:SSM_H, g // 4, (g % 4) * P:(g % 4 + 1) * P], X1[:, g],
                                    W1[:, g, 0:SSM_T, :], start=True, stop=True)
                ins.then_inc(v["g_out"], 1)
                pe.wait_ge(v["wb"], f + 1)
                for g in range(SSM_G):
                    ins = pe.transpose(psT[:, g // 4, (g % 4) * P:(g % 4 + 1) * P],
                                       WbE[:, g].rearrange("p a b -> p (a b)"), ident)
                ins.then_inc(v["wbt"], 1)
                pe.wait_ge(v["g_pad"], f + 1)
                for g in range(SSM_G):
                    ins = pe.transpose(psS[:, g // 4, (g % 4) * P:(g % 4 + 1) * P],
                                       WbI[:, g].rearrange("p a b -> p (a b)"), ident)
                ins.then_inc(v["wbt"], 1)
                pe.wait_ge(s_took["act"], taken["u", l, ft][1])
                pe.wait_ge(v["wbt_sb"], 2 * f + 1)
                for j in range(SSM_T):
                    ins = pe.transpose(psT[0:SSM_C, j // 4, (j % 4) * P:(j % 4 + 1) * P], uT[:, ft, j::SSM_T], ident)
                ins.then_inc(v["u2"], 1)
                pe.wait_ge(v["u2_sb"], f + 1)
                for g in range(SSM_G):
                    ins = pe.transpose(psO[:, g * SSM_C:(g + 1) * SSM_C], U2[:, g],
                                       ident[0:SSM_C, 0:SSM_C])
                ins.then_inc(v["ug"], 1)
                pe.wait_ge(v["ug_sb"], f + 1)
                pe.wait_ge(v["wbt_sb"], 2 * f + 2)
                for g in range(SSM_G):
                    pe.matmul(psS[:, 0, g * SSM_C:(g + 1) * SSM_C], WT[:, g], UG[:, g], start=True, stop=True)
                    ins = pe.matmul(psS[:, 1, g * SSM_C:(g + 1) * SSM_C], WTI[:, g], UG[:, g], start=True, stop=True)
                ins.then_inc(v["e"], 1)
                pe.wait_ge(v["z"], f + 1)
                pe.wait_ge(s_toep, 16 * SSM_T * (f + 1))
                for g in range(SSM_G):
                    o = psT[0:SSM_C, g // 4, (g % 4) * P:(g % 4 + 1) * P]
                    pe.matmul(o, UG[:, g], TO[:, g], start=True, stop=False)
                    pe.matmul(o, zb[1][:, g], W1[:, g, 1:SSM_T + 1, :], start=False, stop=False)
                    ins = pe.matmul(o, zb[2][:, g], W2[:, g], start=False, stop=True)
                ins.then_inc(v["yc"], 1)
                pe.wait_ge(v["yc_sb"], f + 1)
                for j in range(SSM_T):
                    ins = pe.transpose(psO[:, j * SSM_C:(j + 1) * SSM_C], Y2[:, j],
                                       ident[0:SSM_C, 0:SSM_C])
                ins.then_inc(v["yt"], 1)

            def unit_scores(u):
                n, kind, b, j = u["n"], u["kind"], u["b"], u["j"]
                if n:
                    pe.wait_ge(s_masked, n)
                for a in range(2):
                    h = slice(64 * a, 64 * a + 64)
                    q = slice(b * P, (b + 1) * P)
                    k = slice(u["k0"], u["k0"] + u["W"])
                    if kind == "sw":
                        lhs, rhs = qT1[h, j, q], kT1[h, k]
                    elif kind == "dsa":
                        lhs, rhs = qd[h, j, q], kd[h, k]
                    elif kind == "x":
                        lhs, rhs = qx[:, 2 * j + a, q], kx[:, 2 * j + a, :]
                    else:
                        lhs, rhs = qn[h, j, q], {"cmp": kc[h, :], "slc": ks[h, k], "win": kw[h, k]}[kind]
                    ins = pe.matmul(psS[:, a, 0:u["W"]], lhs, rhs, start=True, stop=True)
                ins.then_inc(s_sc, 1)

            def unit_transpose(u):
                n = u["n"]
                pe.wait_ge(s_prob, n + 1)
                if n:
                    pe.wait_ge(s_pt, n)
                p, _ = probs(u)
                for a in range(2):
                    for i, m in key_blocks(u):
                        ins = pe.transpose(psT[0:m, a, i * P:(i + 1) * P], p[:, a, i * P:i * P + m], ident)
                ins.then_inc(s_tr, 1)

            def unit_pv(u):
                n, kind, b, j = u["n"], u["kind"], u["b"], u["j"]
                pe.wait_ge(s_pt, n + 1)
                if u["first"] and u["group"]:
                    pe.wait_ge(s_oe, u["group"])
                _, t = probs(u)
                for a in range(2):
                    h = slice(64 * a, 64 * a + 64)
                    blocks = key_blocks(u)
                    for i, m in blocks:
                        kb = u["k0"] // P + i
                        if kind == "x":
                            o, lhs = psO[:, a * P:(a + 1) * P], vx[:, i, (2 * j + a) * P:(2 * j + a + 1) * P]
                        else:
                            o = psO[h, 0:P]
                            lhs = {"sw": lambda: vt1[:, kb, h], "dsa": lambda: vd[:, kb, :], "cmp": lambda: vc[0:m, h],
                                   "slc": lambda: vs[:, kb, h], "win": lambda: vw[:, kb, h]}[kind]()
                        ins = pe.matmul(o, lhs, t[0:m, a, i, :], start=(u["first"] and i == 0),
                                        stop=(u["last"] and i == blocks[-1][0]))
                ins.then_inc(s_pv, 1)

            def attention(us):
                unit_scores(us[0])
                for i, u in enumerate(us):
                    if i + 1 < len(us):
                        unit_scores(us[i + 1])
                    unit_transpose(u)
                    if i:
                        unit_pv(us[i - 1])
                unit_pv(us[-1])

            def rotate(r, which, src):
                pe.wait_ge(s_rawt, r + 1)
                if r:
                    pe.wait_ge(s_rope, r)
                pe.matmul(psS[:, 1, :], rots[which], src, start=True, stop=True).then_inc(s_rot, 1)

            def post(p):
                kind, N = p["kind"], post_cols(p)
                rt = rawt[:, p["i"] % 2, 0:N]
                if kind == "cmpk" or kind == "cmpv":
                    i = 0 if kind == "cmpk" else 1
                    pe.wait_ge(s_cmpin, i + 1)
                    pe.wait_ge(s_cw, 32)
                    for a in range(2):
                        h = slice(64 * a, 64 * a + 64)
                        for t in range(CMP_L):
                            ins = pe.matmul(psT[h, 0, 0:CMP_N], cmpW[h, i, t, :], cmpin[h, t, :],
                                            start=(t == 0), stop=(t == CMP_L - 1))
                    ins.then_inc(s_cmpo, 1)
                    rt = cmpt[:, i]
                    N = CMP_N
                if kind == "ln":
                    pe.wait_ge(s_p["raw"], p["raw"])
                    pe.matmul(psT[:, 1, 0:N], blk, rt, start=True, stop=True).then_inc(s_p["cmean"], 1)
                if "mean" in p:
                    pe.wait_ge(s_p["sq"], p["sq"])
                    if kind == "lat2":
                        pe.matmul(psT[:, 1, 0:N], ones, tmp[:, 0, 0:N], start=True, stop=False)
                        pe.matmul(psT[:, 1, 0:N], ones, tmp[:, 1, 0:N], start=False, stop=True).then_inc(s_p["mean"], 1)
                    else:
                        m = ones if kind in ("lat1", "xrms") else blk
                        pe.matmul(psT[:, 1, 0:N], m, tmp[:, 0, 0:N], start=True, stop=True).then_inc(s_p["mean"], 1)
                if "rot" in p:
                    if kind == "rope":
                        pe.wait_ge(s_p["raw"], p["raw"])
                        if p["out"] > 1:
                            pe.wait_ge(s_p["out"], p["out"] - 1)
                    else:
                        pe.wait_ge(s_p["qn"], p["qn"])
                    pe.matmul(psS[:, 1, 0:N], rots[2], rt, start=True, stop=True).then_inc(s_p["rot"], 1)
                if "tok" in p:
                    pe.wait_ge(s_p["cen" if kind == "cmpv" else "raw"], p["cen" if kind == "cmpv" else "raw"])
                    if p["toksb"] > 1:
                        pe.wait_ge(s_p["toksb"], p["toksb"] - 1)
                    if kind == "cmpv":
                        ins = pe.transpose(psS[0:CMP_N, 0, 0:P], rt, ident)
                    else:
                        for i in range(N // P):
                            ins = pe.transpose(psS[:, 0, i * P:(i + 1) * P], rt[:, i * P:(i + 1) * P], ident)
                    ins.then_inc(s_p["tok"], 1)

            pe.wait_ge(s_in, 48)
            for l in range(DEPTH):
                mean_square(f"mix{l}")
                for i in range(4):
                    product(("u", l, i))
                for ft in range(4):
                    ssm(l, ft)
                for i in range(4):
                    product(("glu", l, i))
                for i in range(4):
                    product(("q", l, i))
                    if i:
                        rotate(l * 5 + i - 1, 1, rawt[:, (l * 5 + i - 1) % 2, :])
                product(("k", l, 0))
                rotate(l * 5 + 3, 1, rawt[:, (l * 5 + 3) % 2, :])
                product(("v", l, 0))
                rotate(l * 5 + 4, 1, rawt[:, (l * 5 + 4) % 2, :])
                pe.wait_ge(s_vraw, l + 1)
                for b in range(NB):
                    ins = pe.transpose(psT[:, 0, b * P:(b + 1) * P], tmp[:, 2, b * P:(b + 1) * P], ident)
                ins.then_inc(s_vt, 1)
                pe.wait_ge(s_vtok, l + 1)
                pe.wait_ge(s_rope, 5 * (l + 1))
                attention(units[f"sw{l}"])
                for i in range(4):
                    for kind in ("cc", "cx", "cb"):
                        product((kind, l, i))
                for i in range(KD):
                    for kind in ("g0", "ao", "g1", "co", "g2", "so"):
                        product((kind, l, i))
                for i in range(KD):
                    product(("mix", l, i))
                mean_square(f"ffn{l}")
                for c, (t0, nt) in enumerate(FFN_CHUNKS):
                    for t in range(t0, t0 + nt):
                        product(("gt", l, t))
                        product(("up", l, t))
                    for i in range(KD):
                        product(("fo", l, c, i))
            mean_square("final")
            mean_square("norm1")
            for p in block2_posts:
                product(p["key"])
                post(p)
            pe.wait_ge(s_p["out"], block2_posts[-1]["last"]["out"])
            pe.wait_ge(s_p["toksb"], block2_posts[-1]["last"]["toksb"])
            for b in range(NB):
                if b:
                    W = (b + 1) * P
                    for h in range(8):
                        hh = slice(64 * (h % 2), 64 * (h % 2) + 64)
                        n = (b - 1) * 8 + h
                        if n >= 2:
                            pe.wait_ge(s_ir, n - 1)
                        pe.matmul(psT[:, h % 2, 0:W], qi[hh, h // 2, b * P:(b + 1) * P], ki[hh, 0:W],
                                  start=True, stop=True).then_inc(s_is, 1)
                    pe.wait_ge(s_ir, b * 8)
                attention(units["dsa", b])
                attention(units["nsa", b])
            for i in range(KD):
                product(("out2", i))
            mean_square("mem", MEM)
            mean_square("norm2")
            for p in x_posts:
                product(p["key"])
                post(p)
            pe.wait_ge(s_p["out"], x_posts[-1]["last"]["out"])
            pe.wait_ge(s_p["toksb"], x_posts[-1]["last"]["toksb"])
            attention(units["x"])
            for i in range(KD):
                product(("xo", i))
            mean_square("norm3")
            for c, (t0, nt) in enumerate(FF2_CHUNKS):
                for t in range(t0, t0 + nt):
                    product(("fi", t))
                for i in range(KD):
                    product(("fo2", c, i))

        @block.scalar
        def _(act):
            line = Line(act, c_act)
            do = line.done
            act.dma_start(CON[:, :], consts).then_inc(s_in, 16)
            act.dma_start(PAR[:, :], params).then_inc(s_in, 16)
            act.dma_start(X[:, :, :], xT).then_inc(s_in, 16)
            act.wait_ge(s_in, 48)

            def from_bank(key):
                n = number[key]
                act.wait_ge(s_job, n + 1)
                return psG[:, n % GEMM_BANKS, 0:jobs[n][2]]

            def root(name, cols=SEQ):
                act.wait_ge(s_ms, NORMS[name] + 1)
                do(act.activation(rinv[:, 0:cols], psO[:, 0:cols], ACT.Sqrt, bias=eps), s_sd)

            def ssm(l, ft):
                f = l * 4 + ft
                s = sp[f % 2]
                act.wait_ge(s_ssmp[f % 2], 16 * (f // 2 + 1))
                if f:
                    act.wait_ge(v["w12"], f)
                do(act.activation(sm[:, 0], s[:, 2 * SSM_G:3 * SSM_G], ACT.Exp), v["y1"])
                act.wait_ge(v["args"], 2 * f + 1)
                do(act.activation(mag, mag, ACT.Exp), v["sincos"])
                act.wait_ge(v["args"], 2 * f + 2)
                do(act.activation(sn, arg, ACT.Sin))
                do(act.activation(cs, arg2, ACT.Sin), v["sincos"])
                if f:
                    act.wait_ge(s_toep, 16 * SSM_T * f)
                act.wait_ge(v["g_out"], f + 1)
                for i in range(2):
                    ins = act.activation(Gp[:, 4 * i:4 * i + 4, 7 * SSM_H:],
                                         psS[0:SSM_H, i, :].rearrange("p (g x) -> p g x", g=4), ACT.Copy)
                    do(ins) if i == 0 else do(ins, v["g_pad"])
                if f:
                    act.wait_ge(v["yc"], f)
                for j in range(SSM_T):
                    act.dma_start(TO[j * SSM_H:(j + 1) * SSM_H, :, :],
                                  Gp[:, :, (7 - j) * SSM_H:(7 - j) * SSM_H + P]).then_inc(s_toep, 16)
                for k, (dst, src) in enumerate(((WT, psT), (WTI, psS))):
                    act.wait_ge(v["wbt"], 2 * f + k + 1)
                    do(act.activation(dst[:, 0:4].rearrange("p a b -> p (a b)"), src[:, 0, :], ACT.Copy))
                    do(act.activation(dst[:, 4:8].rearrange("p a b -> p (a b)"), src[:, 1, :], ACT.Copy), v["wbt_sb"])
                act.wait_ge(v["u2"], f + 1)
                by_position = U2.rearrange("c g (j h) -> c j g h", h=SSM_H)
                for i, s_i in ((0, None), (1, v["u2_sb"])):
                    do(act.activation(by_position[:, 4 * i:4 * i + 4],
                                      psT[0:SSM_C, i, :].rearrange("c (j g h) -> c j g h", g=SSM_G, h=SSM_H), ACT.Copy), s_i)
                act.wait_ge(v["ug"], f + 1)
                do(act.activation(UG[:, :, :].rearrange("p a b -> p (a b)"), psO[:, :], ACT.Copy), v["ug_sb"])
                act.wait_ge(v["yc"], f + 1)
                by_group = Y2.rearrange("c j (g h) -> c g j h", h=SSM_H)
                for i, s_i in ((0, None), (1, v["yc_sb"])):
                    do(act.activation(by_group[:, 4 * i:4 * i + 4],
                                      psT[0:SSM_C, i, :].rearrange("c (g j h) -> c g j h", j=SSM_T, h=SSM_H), ACT.Copy), s_i)
                act.wait_ge(v["ypre"], f + 1)
                do(act.activation(ysf[:, ft], ysf[:, ft], ACT.Gelu_apprx_tanh), v["ys"])
                if ft < 2:
                    act.dma_start(s, ssmp[f + 2]).then_inc(s_ssmp[f % 2], 16)

            def unit_exp(u):
                n, kind = u["n"], u["kind"]
                st = stat[:, n % 2]
                p, _ = probs(u)
                act.wait_ge(s_neg, n + 1)
                scale = {"sw": 1.0, "x": P ** -0.5}.get(kind, HEAD ** -0.5)
                do(act.activation(p[:, 0], p[:, 0], ACT.Exp, bias=st[:, 2:3], scale=scale, accum_out=st[:, 4:5]))
                ins = act.activation(p[:, 1], p[:, 1], ACT.Exp, bias=st[:, 3:4], scale=scale, accum_out=st[:, 5:6])
                if kind == "sw":
                    do(ins)
                    ins = act.activation(st[:, 6:8], st[:, 6:8], ACT.Exp)
                do(ins, s_exp)

            def unit_copy(u):
                n = u["n"]
                act.wait_ge(s_tr, n + 1)
                if n >= 2:
                    act.wait_ge(s_pv, n - 1)
                _, t = probs(u)
                m, w = (CMP_N, 1) if u["kind"] == "cmp" else (P, u["W"] // P)
                src = psT[0:m, :, 0:w * P].rearrange("p a (b c) -> p a b c", c=P)
                do(act.activation(t[0:m, 0, 0:w, :], src[:, 0], ACT.Copy))
                do(act.activation(t[0:m, 1, 0:w, :], src[:, 1], ACT.Copy), s_pt)

            def attention(us):
                unit_exp(us[0])
                for i, u in enumerate(us):
                    if i + 1 < len(us):
                        unit_exp(us[i + 1])
                    unit_copy(u)

            def post(p):
                kind, N = p["kind"], post_cols(p)
                rt = rawt[:, p["i"] % 2, 0:N]
                bank = from_bank(p["key"])
                prev = posts[p["i"] - (1 if kind == "lat1" else 2)] if p["i"] >= 2 else None
                if prev:
                    for n in ("out", "toksb", "cen"):
                        if prev["last"][n]:
                            act.wait_ge(s_p[n], prev["last"][n])
                do(act.activation(rt, bank, ACT.Copy), s_took["act"])
                act.sem_inc(s_p["raw"], 1) if hasattr(act, "sem_inc") else None
                if "sd" in p:
                    act.wait_ge(s_p["mean"], p["mean"])
                    if kind == "cmpk":
                        N = CMP_N
                    scale = {"lat2": 4.0, "lat1": 8.0, "xrms": 8.0}.get(kind, 1.0)
                    do(act.activation(rinv[:, 0:N], psT[:, 1, 0:N], ACT.Sqrt, bias=eps, scale=scale), s_p["sd"])
                if "toksb" in p:
                    act.wait_ge(s_p["tok"], p["tok"])
                    t = psS[:, 0, :].rearrange("p (b c) -> p b c", c=P)
                    if kind == "tok":
                        do(act.activation({"vs": vs, "vw": vw}[p["dest"]], t, ACT.Copy), s_p["toksb"])
                    elif kind == "tokd":
                        do(act.activation(vd, t[:, :, HEAD:P], ACT.Copy), s_p["toksb"])
                    elif kind == "tokwg":
                        do(act.activation(wtok[:, :, :], t[:, :, 0:8], ACT.Copy, scale=IDX_SCALE))
                        do(act.activation(gtok[:, :, :], t[:, :, 104:128], ACT.Sigmoid), s_p["toksb"])
                    elif kind == "tokx":
                        i = p["dest"]
                        do(act.activation(vx[:, :, i * P:(i + 1) * P], t[:, 0:2, :], ACT.Copy), s_p["toksb"])
                    elif kind == "cmpv":
                        do(act.activation(vc[0:CMP_N, :], psS[0:CMP_N, 0, 0:P], ACT.Copy), s_p["toksb"])

            for l in range(DEPTH):
                for i in range(2):
                    act.dma_start(sp[i], ssmp[4 * l + i]).then_inc(s_ssmp[i], 16)
                root(f"mix{l}")
                for i in range(4):
                    do(act.activation(uT[:, i], from_bank(("u", l, i)), ACT.Copy), s_took["act"])
                for ft in range(4):
                    ssm(l, ft)
                for i in range(4):
                    bank = from_bank(("glu", l, i))
                    act.wait_ge(v["glu_out"], 4 * l + i) if 4 * l + i else None
                    do(act.activation(tmp[:, 0, :], bank, ACT.Sigmoid), s_took["act"])
                for i in range(4):
                    r = l * 5 + i
                    bank = from_bank(("q", l, i))
                    if r >= 2:
                        act.wait_ge(s_rope, r - 1)
                    do(act.activation(rawt[:, r % 2, :], bank, ACT.Copy, scale=HEAD ** -0.5), s_took["act"])
                    act.sem_inc(s_rawt, 1)
                r = l * 5 + 4
                bank = from_bank(("k", l, 0))
                act.wait_ge(s_rope, r - 1)
                do(act.activation(rawt[:, r % 2, :], bank, ACT.Copy), s_took["act"])
                act.sem_inc(s_rawt, 1)
                bank = from_bank(("v", l, 0))
                act.wait_ge(s_rope, r)
                do(act.activation(tmp[:, 2, :], bank, ACT.Copy), s_took["act"])
                act.sem_inc(s_vraw, 1)
                act.wait_ge(s_vt, l + 1)
                do(act.activation(vt1[:, :, :].rearrange("p a b -> p (a b)"), psT[:, 0, :], ACT.Copy), s_vtok)
                attention(units[f"sw{l}"])
                for i in range(4):
                    bank = from_bank(("cc", l, i))
                    act.wait_ge(s_cy, 4 * l + i) if 4 * l + i else None
                    do(act.activation(tmp[:, 0, :], bank, ACT.Copy), s_took["act"])
                for i in range(KD):
                    for br, g in enumerate(("g0", "g1", "g2")):
                        bank = from_bank((g, l, i))
                        n = 24 * l + 3 * i + br
                        if n >= 2:
                            act.wait_ge(s_sig, n - 1)
                        do(act.activation(rawt[:, n % 2, :], bank, ACT.Sigmoid, bias=par(("b_gate", l), br * KD + i)),
                           s_took["act"])
                root(f"ffn{l}")
                for t in range(FFN_TILES):
                    bank = from_bank(("gt", l, t))
                    n = FFN_TILES * l + t
                    if n >= 2:
                        act.wait_ge(s_hid, n - 1)
                    do(act.activation(rawt[:, n % 2, :], bank, ACT.Silu), s_took["act"])
            root("final")
            root("norm1")
            for i in range(2):
                act.dma_start(cmpW[:, i].rearrange("p a b -> p (a b)"), cmpw[i]).then_inc(s_cw, 16)
            for p in block2_posts:
                post(p)
            for b in range(NB):
                if b:
                    W = (b + 1) * P
                    for h in range(8):
                        n = (b - 1) * 8 + h
                        act.wait_ge(s_is, n + 1)
                        if n >= 2:
                            act.wait_ge(s_ia, n - 1)
                        do(act.activation(irelu[:, h % 2, 0:W], psT[:, h % 2, 0:W], ACT.Relu), s_ir)
                attention(units["dsa", b])
                attention(units["nsa", b])
            act.wait_ge(s_pv, units["nsa", NB - 1][-1]["n"] + 1)
            act.dma_start(memf, memT).then_inc(s_mem, 16)
            root("mem", MEM)
            root("norm2")
            for p in x_posts:
                post(p)
            attention(units["x"])
            root("norm3")
            for t in range(32):
                bank = from_bank(("fi", t))
                n = FFN_TILES * DEPTH + t
                act.wait_ge(s_hid, n - 1)
                do(act.activation(rawt[:, n % 2, :], bank, ACT.Relu), s_took["act"])

        @block.vector
        def _(dve):
            line = Line(dve, c_dve)
            do = line.done

            def from_bank(key):
                n = number[key]
                dve.wait_ge(s_job, n + 1)
                return psG[:, n % GEMM_BANKS, 0:jobs[n][2]]

            def tt(out, a, b, op, s=None):
                do(dve.tensor_tensor(out, a, b, op), s)

            def stt(out, a, s_, b, op0, op1, s=None):
                do(dve.scalar_tensor_tensor(out, a, s_, b, op0, op1), s)

            def ts(out, a, s1, s2, op0, op1=None, s=None):
                do(dve.tensor_scalar(out, a, s1, s2, op0, op1) if op1 is not None
                   else dve.tensor_scalar(out, a, s1, None, op0), s)

            def split(hi, lo, src, s):
                do(dve.tensor_copy(hi, src))
                tt(lo, src, hi.bitcast(F32), ALU.subtract, s)

            def add_square(k, src, n=SEQ):
                if k == 0:
                    tt(acc[:, 0:n], src, src, ALU.mult)
                else:
                    tt(tmp[:, 0, 0:n], src, src, ALU.mult)
                    tt(acc[:, 0:n], acc[:, 0:n], tmp[:, 0, 0:n], ALU.add, s_ssq if k == KD - 1 else None)

            def normalise(name, gain, src=None, hi=Hh, lo=Hl, n=SEQ):
                src = X if src is None else src
                dve.wait_ge(s_sd, NORMS[name] + 1)
                do(dve.reciprocal(rinv[:, 0:n], rinv[:, 0:n]))
                for k in range(KD):
                    if name == "final":
                        stt(X[:, k], X[:, k], par(gain, k), rinv[:, :], ALU.mult, ALU.mult)
                    else:
                        t = tmp[:, 1, 0:n]
                        stt(t, src[:, k], par(gain, k), rinv[:, 0:n], ALU.mult, ALU.mult)
                        split(hi[:, k], lo[:, k], t, s_h)

            def residual(key, i, square):
                bank = from_bank(key)
                tt(X[:, i], X[:, i], bank, ALU.add, s_took["dve"])
                if square:
                    add_square(i, X[:, i])

            def reduce_angle(a):
                big = 1.5 * 2.0 ** 23
                ts(red, a, 1.0 / (2 * math.pi), big, ALU.mult, ALU.add)
                ts(red, red, big, None, ALU.subtract)
                for c in (6.28125, 1.93500518798828125e-3, 3.01991598195675286e-7):
                    stt(a, red, -c, a, ALU.mult, ALU.add)
                ts(a, a, 3.1415925, -3.1415925, ALU.min, ALU.max)

            def reduce_small(a):
                big = 1.5 * 2.0 ** 23
                t = sm[:, 15]
                ts(t, a, 1.0 / (2 * math.pi), big, ALU.mult, ALU.add)
                ts(t, t, big, None, ALU.subtract)
                for c in (6.28125, 1.93500518798828125e-3, 3.01991598195675286e-7):
                    stt(a, t, -c, a, ALU.mult, ALU.add)

            def ssm(l, ft):
                f = l * 4 + ft
                s = sp[f % 2]
                G = SSM_G
                are, aim = s[:, 0:G], s[:, G:2 * G]
                o = 3 * G
                gh = G * SSM_H
                y1, y2, c1, c2 = (s[:, o + gh * i:o + gh * (i + 1)].rearrange("p (g h) -> p g h", g=G) for i in range(4))
                J = con("J", 9)
                dve.wait_ge(s_ssmp[f % 2], 16 * (f // 2 + 1))
                dve.wait_ge(v["y1"], f + 1)
                dt, ar, th, t8, t64, inv, cr, ci, ta, tb = (sm[:, i] for i in range(10))
                tt(ar, are, dt, ALU.mult)
                tt(th, aim, dt, ALU.mult)
                tt(mag, ar.unsqueeze(2).to_broadcast([P, G, 9]), J.unsqueeze(1).to_broadcast([P, G, 9]), ALU.mult, v["args"])
                reduce_small(th)
                ts(t8, th, 8.0, None, ALU.mult)
                reduce_small(t8)
                ts(t64, t8, 8.0, None, ALU.mult)
                reduce_small(t64)
                for a, n, c in ((th, 9, 0), (t8, 8, 9), (t64, 8, 17)):
                    tt(arg[:, :, c:c + n], a.unsqueeze(2).to_broadcast([P, G, n]),
                       J[:, 0:n].unsqueeze(1).to_broadcast([P, G, n]), ALU.mult)
                reduce_angle(arg)
                ts(arg2, arg, math.pi / 2, None, ALU.add)
                reduce_angle(arg2)
                ts(Y1n, y2, con("sgn", 1), -1.0, ALU.mult, ALU.mult)
                ts(Z1, c1, con("sgn", 1), None, ALU.mult)
                ts(Z2, c2, -1.0, None, ALU.mult, None, v["args"])
                dve.wait_ge(v["sincos"], 2 * f + 2)
                tt(Lr, mag, cs[:, :, 0:9], ALU.mult)
                tt(Li, mag, sn[:, :, 0:9], ALU.mult)
                tt(ta, are, are, ALU.mult)
                tt(tb, aim, aim, ALU.mult)
                tt(ta, ta, tb, ALU.add)
                do(dve.reciprocal(inv, ta))
                nr, ni = sm[:, 10], Li[:, :, 1]
                ts(nr, Lr[:, :, 1], -1.0, None, ALU.add)
                tt(cr, nr, are, ALU.mult)
                tt(ta, ni, aim, ALU.mult)
                tt(cr, cr, ta, ALU.add)
                tt(cr, cr, inv, ALU.mult)
                tt(ci, ni, are, ALU.mult)
                tt(ta, nr, aim, ALU.mult)
                tt(ci, ci, ta, ALU.subtract)
                tt(ci, ci, inv, ALU.mult)
                bc = lambda a, n: a.unsqueeze(2).to_broadcast([P, G, n])
                rev = lambda a: a[:, :, 7::-1]
                t3 = work(TS, 1856, [P, G, 8])
                tt(Lcr, rev(Lr), bc(cr, 8), ALU.mult)
                tt(t3, rev(Li), bc(ci, 8), ALU.mult)
                tt(Lcr, Lcr, t3, ALU.subtract)
                tt(Lci, rev(Lr), bc(ci, 8), ALU.mult)
                tt(t3, rev(Li), bc(cr, 8), ALU.mult)
                tt(Lci, Lci, t3, ALU.add)
                t4 = work(TS, 1920, [P, G, SSM_H])
                tt(X1, y1, bc(cr, SSM_H), ALU.mult)
                tt(t4, Y1n, bc(ci, SSM_H), ALU.mult)
                tt(X1, X1, t4, ALU.add)
                jh = lambda a, n: a.unsqueeze(3).to_broadcast([P, G, n, SSM_H])
                hj = lambda a, n: a.unsqueeze(2).to_broadcast([P, G, n, SSM_H])
                pw = lambda n: pwork[:, 0:G * n * SSM_H].rearrange("p (g j h) -> p g j h", g=G, j=n)
                if f:
                    dve.wait_ge(v["yc"], f)
                tt(W1, jh(Lr, 9), hj(Z1, 9), ALU.mult)
                tt(pw(9), jh(Li, 9), hj(Z2, 9), ALU.mult)
                tt(W1, W1, pw(9), ALU.add)
                tt(W2, jh(Lr[:, :, 1:9], 8), hj(Z2, 8), ALU.mult)
                tt(pw(8), jh(Li[:, :, 1:9], 8), hj(Z1, 8), ALU.mult)
                tt(W2, W2, pw(8), ALU.subtract, v["w12"])
                tt(WbE, jh(Lcr, 8), hj(y1, 8), ALU.mult)
                tt(pw(8), jh(Lci, 8), hj(Y1n, 8), ALU.mult)
                tt(WbE, WbE, pw(8), ALU.add)
                tt(WbI, jh(Lci, 8), hj(y1, 8), ALU.mult)
                tt(pw(8), jh(Lcr, 8), hj(Y1n, 8), ALU.mult)
                tt(WbI, WbI, pw(8), ALU.subtract, v["wb"])
                ab = lambda a: a.rearrange("p g (a b) -> p g a b", b=8)
                ea = lambda a: a[:, :, 17:25].unsqueeze(3).to_broadcast([P, G, 8, 8])
                eb = lambda a: a[:, :, 9:17].unsqueeze(2).to_broadcast([P, G, 8, 8])
                pt = pwork[:, 0:G * 64].rearrange("p (g a b) -> p g a b", g=G, a=8)
                tt(ab(rotC), ea(cs), eb(cs), ALU.mult)
                tt(pt, ea(sn), eb(sn), ALU.mult)
                tt(ab(rotC), ab(rotC), pt, ALU.subtract)
                tt(ab(rotS), ea(sn), eb(cs), ALU.mult)
                tt(pt, ea(cs), eb(sn), ALU.mult)
                tt(ab(rotS), ab(rotS), pt, ALU.add)
                do(dve.tensor_copy(acoef, mag[:, :, 8:9].to_broadcast([P, G, SSM_C])))
                do(dve.memset(acoef[:, :, 0:1], 0.0))
                if f == 0:
                    do(dve.memset(zb[1][:, :, 0:1], 0.0))
                    do(dve.memset(zb[2][:, :, 0:1], 0.0))
                dve.wait_ge(v["e"], f + 1)
                e0 = psS[:, 0, :].rearrange("p (g c) -> p g c", g=G)
                e1 = psS[:, 1, :].rearrange("p (g c) -> p g c", g=G)
                zt = pwork[:, 0:512].rearrange("p (g c) -> p g c", g=G)
                tt(zb[0], e0, rotC, ALU.mult)
                tt(zt, e1, rotS, ALU.mult)
                tt(zb[0], zb[0], zt, ALU.add)
                fl = lambda a: a.rearrange("p g c -> p (g c)")
                do(dve.tensor_tensor_scan(fl(zt), fl(acoef), fl(zb[0]), 0.0, ALU.mult, ALU.add))
                tt(zb[1][:, :, 1:], zt[:, :, :-1], rotC[:, :, :-1], ALU.mult)
                tt(zb[2][:, :, 1:], zt[:, :, :-1], rotS[:, :, :-1], ALU.mult, v["z"])
                dve.wait_ge(v["yt"], f + 1)
                stt(ysf[:, ft].rearrange("p (c j) -> p c j", j=SSM_T), uT[:, ft].rearrange("p (c j) -> p c j", j=SSM_T),
                    par(("ssm_d", l), ft), psO[:, :].rearrange("p (j c) -> p c j", j=SSM_T), ALU.mult, ALU.add, v["ypre"])

            def unit_max(u):
                n, kind, b, W = u["n"], u["kind"], u["b"], u["W"]
                st = stat[:, n % 2]
                p, _ = probs(u)
                dve.wait_ge(s_sc, n + 1)
                if n >= 2:
                    dve.wait_ge(s_tr, n - 1)
                src = psS[:, :, 0:W]
                if kind == "sw":
                    mask = con("sw", 2 * P)[:, 2 * P - W:]
                elif kind == "dsa":
                    mask = selm[:, 0:W]
                elif kind == "cmp":
                    mask = con("cmp_add", NB * CMP_N)[:, b * CMP_N:(b + 1) * CMP_N]
                else:
                    mask = con("mk", SEQ)[:, SEQ - W:]
                if kind == "x":
                    do(dve.tensor_copy(p, src), s_masked)
                else:
                    tt(p, src, mask.unsqueeze(1).to_broadcast([P, 2, W]), ALU.add, s_masked)
                do(dve.tensor_reduce(st[:, 0:2], p, AX_X, ALU.max))
                scale = {"sw": 1.0, "x": P ** -0.5}.get(kind, HEAD ** -0.5)
                if kind == "sw":
                    snk = par(("sinks", u["l"]), 0, 8)[:, u["j"]::4]
                    tt(st[:, 0:2], st[:, 0:2], snk, ALU.max)
                    tt(st[:, 6:8], snk, st[:, 0:2], ALU.subtract)
                ts(st[:, 2:4], st[:, 0:2], -scale, None, ALU.mult, None, s_neg)

            def unit_scale(u):
                n, kind, b, j = u["n"], u["kind"], u["b"], u["j"]
                st = stat[:, n % 2]
                p, _ = probs(u)
                dve.wait_ge(s_exp, n + 1)
                den = st[:, 4:6]
                if kind == "sw":
                    tt(den, den, st[:, 6:8], ALU.add)
                if kind == "cmp":
                    mul = con("cmp_mul", NB * CMP_N)[:, b * CMP_N:(b + 1) * CMP_N]
                    tt(p, p, mul.unsqueeze(1).to_broadcast([P, 2, CMP_N]), ALU.mult)
                    do(dve.tensor_reduce(den, p, AX_X, ALU.add))
                    ts(den, den, 1e-30, None, ALU.max)
                do(dve.reciprocal(st[:, 8:10], den))
                if kind in ("cmp", "slc", "win"):
                    br = ("cmp", "slc", "win").index(kind)
                    tt(st[:, 8:10], st[:, 8:10], gtok[:, b, 3 * j + br::12], ALU.mult)
                ts(p[:, 0], p[:, 0], st[:, 8:9], None, ALU.mult)
                ts(p[:, 1], p[:, 1], st[:, 9:10], None, ALU.mult, None, s_prob)

            def unit_out(u):
                if not u["last"]:
                    return
                kind, b, j = u["kind"], u["b"], u["j"]
                dve.wait_ge(s_pv, u["n"] + 1)
                q = slice(b * P, (b + 1) * P)
                if kind == "x":
                    for a in range(2):
                        o = psO[:, a * P:(a + 1) * P]
                        t = 2 * j + a
                        do(dve.tensor_copy(Hh[:, t, q], o))
                        tt(Hl[:, t, q], o, Hh[:, t, q].bitcast(F32), ALU.subtract, s_oe if a else None)
                    return
                hi, lo, t = {"sw": (Bh, Bl, j), "dsa": (Hh, Hl, j)}.get(kind, (Hh, Hl, 4 + j))
                do(dve.tensor_copy(hi[:, t, q], psO[:, 0:P]))
                tt(lo[:, t, q], psO[:, 0:P], hi[:, t, q].bitcast(F32), ALU.subtract, s_oe)

            def attention(us):
                unit_max(us[0])
                for i, u in enumerate(us):
                    if i + 1 < len(us):
                        unit_max(us[i + 1])
                    unit_scale(u)
                    if i:
                        unit_out(us[i - 1])
                unit_out(us[-1])

            def post(p):
                kind, N = p["kind"], post_cols(p)
                rt = rawt[:, p["i"] % 2, 0:N]
                dve.wait_ge(s_p["raw"], p["raw"])
                if kind in ("cmpk", "cmpv"):
                    i = 0 if kind == "cmpk" else 1
                    if i:
                        dve.wait_ge(s_cmpo, i)
                    for l0 in (0, CMP_STRIDE):
                        src = rt[:, l0:l0 + CMP_STRIDE * CMP_N].rearrange("p (n l) -> p l n", l=CMP_STRIDE)
                        pe_ = par("pe", CMP_L * i + l0, CMP_STRIDE).unsqueeze(2).to_broadcast([P, CMP_STRIDE, CMP_N])
                        tt(cmpin[:, l0:l0 + CMP_STRIDE], src, pe_, ALU.add, s_cmpin if l0 else None)
                    dve.wait_ge(s_cmpo, i + 1)
                    rt = cmpt[:, i]
                    do(dve.tensor_copy(rt, psT[:, 0, 0:CMP_N]), s_p["cen"])
                    N = CMP_N
                if kind == "ln":
                    dve.wait_ge(s_p["cmean"], p["cmean"])
                    tt(rt, rt, psT[:, 1, 0:N], ALU.subtract, s_p["cen"])
                if "sq" in p:
                    tt(tmp[:, 1 if kind == "lat2" else 0, 0:N], rt, rt, ALU.mult, s_p["sq"])
                    if kind == "lat":
                        return
                    dve.wait_ge(s_p["sd"], p["sd"])
                    do(dve.reciprocal(rinv[:, 0:N], rinv[:, 0:N]))
                    if kind in ("lat1", "lat2"):
                        tiles = [(0, posts[p["i"] - 1]), (1, p)] if kind == "lat2" else [(2, p)]
                        for n, (i, q) in enumerate(tiles):
                            gain = par("cq", i) if kind == "lat2" else par("ckv")
                            stt(tmp[:, 2, :], rawt[:, q["i"] % 2, :], gain, rinv[:, :], ALU.mult, ALU.mult)
                            split(Bh[:, 8 + i], Bl[:, 8 + i], tmp[:, 2, :], s_p["out"] if n == len(tiles) - 1 else None)
                        return
                    if kind == "ln":
                        tt(rt, rt, rinv[:, 0:N], ALU.mult)
                        ts(rt, rt, par("lng"), par("lnb"), ALU.mult, ALU.add, s_p["qn"])
                    elif kind == "xrms":
                        stt(p["dest"], rt, par(*p["gain"]), rinv[:, 0:N], ALU.mult, ALU.mult, s_p["out"])
                        return
                    else:
                        gain = par("nkn", 0) if kind == "cmpk" else par(*p["gain"])
                        stt(rt, rt, gain, rinv[:, 0:N], ALU.mult, ALU.mult, s_p["qn"])
                if "rot" in p:
                    C, S = tabs[2]
                    dest = p["dest"]
                    if kind == "cmpk":
                        C, S = (a[:, CMP_L - 1::CMP_STRIDE] for a in (C, S))
                        dest = kc
                    dve.wait_ge(s_p["rot"], p["rot"])
                    tt(tmp[:, 2, 0:N], psS[:, 1, 0:N], S, ALU.mult)
                    tt(dest, rt, C, ALU.mult)
                    tt(dest, dest, tmp[:, 2, 0:N], ALU.add, s_p["out"])

            dve.wait_ge(s_in, 48)
            do(dve.memset(zc[:, 0:2], 0.0))
            for k in range(KD):
                add_square(k, X[:, k])
            for l in range(DEPTH):
                normalise(f"mix{l}", ("norm_mix", l))
                do(dve.memset(Gp[:, :, 0:7 * SSM_H], 0.0), v["consts_ready"])
                do(dve.memset(zb[1][:, :, 0:1], 0.0))
                do(dve.memset(zb[2][:, :, 0:1], 0.0))
                for ft in range(4):
                    ssm(l, ft)
                for ft in range(4):
                    dve.wait_ge(v["ys"], l * 4 + ft + 1)
                    split(Bh[:, 4 + ft], Bl[:, 4 + ft], ysf[:, ft], v["ysplit"])
                for i in range(4):
                    dve.wait_ge(s_took["act"], taken["glu", l, i][1])
                    tt(tmp[:, 1, :], tmp[:, 0, :], ysf[:, i], ALU.mult)
                    split(Bh[:, 8 + i], Bl[:, 8 + i], tmp[:, 1, :], v["glu_out"])
                for i in range(5):
                    r = l * 5 + i
                    dve.wait_ge(s_rot, r + 1)
                    dest = qT1[:, i] if i < 4 else kT1
                    tt(tmp[:, 0, :], psS[:, 1, :], tabs[1][1], ALU.mult)
                    tt(tmp[:, 1, :], rawt[:, r % 2, :], tabs[1][0], ALU.mult)
                    tt(dest, tmp[:, 0, :], tmp[:, 1, :], ALU.add, s_rope)
                attention(units[f"sw{l}"])
                do(dve.memset(zc[:, 0:2], 0.0))
                for i in range(4):
                    dve.wait_ge(s_took["act"], taken["cc", l, i][1])
                    bank = from_bank(("cx", l, i))
                    tt(zc[:, 2:], bank, tmp[:, 0, :], ALU.mult, s_took["dve"])
                    ts(ycv, zc[:, 0:SEQ], par(("conv", l), i), None, ALU.mult)
                    stt(ycv, zc[:, 1:SEQ + 1], par(("conv", l), 4 + i), ycv, ALU.mult, ALU.add)
                    stt(ycv, zc[:, 2:SEQ + 2], par(("conv", l), 8 + i), ycv, ALU.mult, ALU.add)
                    bank = from_bank(("cb", l, i))
                    tt(ycv, bank, ycv, ALU.mult, s_took["dve"])
                    split(Bh[:, 4 + i], Bl[:, 4 + i], ycv, s_cy)
                for i in range(KD):
                    for br, kind in enumerate(("ao", "co", "so")):
                        n = 24 * l + 3 * i + br
                        bank = from_bank((kind, l, i))
                        dve.wait_ge(s_took["act"], taken["g" + str(br), l, i][1])
                        gate = rawt[:, n % 2, :]
                        if br == 0:
                            tt(tmp[:, 0, :], bank, gate, ALU.mult, s_took["dve"])
                        else:
                            tt(tmp[:, 1, :], bank, gate, ALU.mult, s_took["dve"])
                            tt(tmp[:, 0, :], tmp[:, 0, :], tmp[:, 1, :], ALU.add)
                        dve.sem_inc(s_sig, 1)
                    split(Mh[:, i], Ml[:, i], tmp[:, 0, :], s_merged)
                for i in range(KD):
                    residual(("mix", l, i), i, True)
                normalise(f"ffn{l}", ("norm_ffn", l))
                for c, (t0, nt) in enumerate(FFN_CHUNKS):
                    for t in range(t0, t0 + nt):
                        n = FFN_TILES * l + t
                        bank = from_bank(("up", l, t))
                        dve.wait_ge(s_took["act"], taken["gt", l, t][1])
                        tt(tmp[:, 1, :], bank, rawt[:, n % 2, :], ALU.mult, s_took["dve"])
                        split(Mh[:, t - t0], Ml[:, t - t0], tmp[:, 1, :], s_hid)
                    for i in range(KD):
                        residual(("fo", l, c, i), i, c == len(FFN_CHUNKS) - 1)
            normalise("final", "norm_final")
            for k in range(KD):
                add_square(k, X[:, k])
            normalise("norm1", "norm1")
            for p in block2_posts:
                post(p)
            for b in range(NB):
                W = (b + 1) * P
                mk = con("mk", SEQ)[:, SEQ - W:]
                if b == 0:
                    do(dve.tensor_copy(selm[:, 0:W], mk))
                else:
                    for h in range(8):
                        n = (b - 1) * 8 + h
                        dve.wait_ge(s_ir, n + 1)
                        w = wtok[:, b, h:h + 1]
                        if h == 0:
                            ts(iacc[:, 0:W], irelu[:, 0, 0:W], w, None, ALU.mult, None, s_ia)
                        else:
                            stt(iacc[:, 0:W], irelu[:, h % 2, 0:W], w, iacc[:, 0:W], ALU.mult, ALU.add, s_ia)
                    tt(iwork[:, 0:W], iacc[:, 0:W], mk, ALU.add)
                    for _ in range(TOPK // 8):
                        do(dve.max(m8[:, :], iwork[:, 0:W]))
                        do(dve.match_replace(iwork[:, 0:W], m8[:, :], iwork[:, 0:W], TAKEN))
                    ts(selm[:, 0:W], iwork[:, 0:W], TAKEN / 2, NEG, ALU.is_gt, ALU.mult)
                attention(units["dsa", b])
                attention(units["nsa", b])
            for i in range(KD):
                residual(("out2", i), i, False)
            dve.wait_ge(s_mem, 16)
            for k in range(KD):
                add_square(k, memf[:, k], MEM)
            normalise("mem", "mem_norm", memf, mH, mL, MEM)
            for k in range(KD):
                add_square(k, X[:, k])
            normalise("norm2", "norm2")
            for p in x_posts:
                post(p)
            attention(units["x"])
            for i in range(KD):
                residual(("xo", i), i, True)
            normalise("norm3", "norm3")
            for c, (t0, nt) in enumerate(FF2_CHUNKS):
                for t in range(t0, t0 + nt):
                    n = FFN_TILES * DEPTH + t
                    dve.wait_ge(s_took["act"], taken["fi", t][1])
                    tt(tmp[:, 1, :], rawt[:, n % 2, :], rawt[:, n % 2, :], ALU.mult)
                    split(Mh[:, t - t0], Ml[:, t - t0], tmp[:, 1, :], s_hid)
                for i in range(KD):
                    residual(("fo2", c, i), i, False)
            dve.sem_inc(s_y, 1)


def kernel(**inputs):
    import concourse.bacc as bacc
    from concourse.bass_utils import run_bass_kernel_spmd

    w = {k: np.asarray(a) for k, a in inputs.items()}
    parts = []
    for key, K, _, _ in job_plan():
        a = weight_tile(w, key)
        parts.append(a.reshape(K, P, P).transpose(1, 0, 2).reshape(-1))
    arrays = {
        "wstream": np.concatenate(parts),
        "params": pack_params(w),
        "ssmp": pack_ssm(w),
        "cmpw": np.tile(w["w_nsa_cmp_2"][0].transpose(0, 2, 1, 3), (1, 2, 1, 1)).reshape(2, P, CMP_L * HEAD),
        "consts": constants(),
        "xT": np.ascontiguousarray(w["x"][0].T.reshape(KD, P, SEQ).transpose(1, 0, 2)),
        "memT": np.ascontiguousarray(w["mem_2"][0].T.reshape(KD, P, MEM).transpose(1, 0, 2)),
    }
    nc = bacc.Bacc("TRN2", target_bir_lowering=False, num_devices=1)
    args = [nc.dram_tensor(n, a.shape, F32, kind="ExternalInput").ap() for n, a in arrays.items()]
    out = nc.dram_tensor("outT", (P, KD, SEQ), F32, kind="ExternalOutput").ap()
    block_program(nc, *args, out)
    r = run_bass_kernel_spmd(nc, [arrays], core_ids=[0])
    o = r.results[0]["outT"]
    return np.ascontiguousarray(o.transpose(1, 0, 2).reshape(D_MODEL, SEQ).T)[None]
```

```python
import math
from contextlib import ExitStack

import concourse.bass as bass
import numpy as np
from concourse import mybir

F32 = mybir.dt.float32
F32R = mybir.dt.float32r
ALU = mybir.AluOpType
ACT = mybir.ActivationFunctionType
AX_X = mybir.AxisListType.X

P = 128
SEQ = 512
NB = SEQ // P
D_MODEL = 1024
KD = D_MODEL // P
DEPTH = 2
HEAD = 64
HALF = 4
W_IN_COLS = dict(q=0, k=512, v=640, cb=768, cc=1280, cx=1792, u=2304, g=2816)
FFN_TILES = 22
FFN_CHUNKS = [(0, 8), (8, 8), (16, 6)]
FF2_CHUNKS = [(0, 8), (8, 8), (16, 8), (24, 8)]
EPS = 1e-6
NEG = -1e30
TAKEN = -3e38

SSM_STATE = 64
SSM_H = 16
SSM_T = 8
SSM_C = SEQ // SSM_T
SSM_G = P // SSM_H
SSM_PARAMS = 3 * SSM_G + 4 * SSM_G * SSM_H

CMP_N, CMP_L, CMP_STRIDE = 31, 32, 16
TOPK = 128
IDX_SCALE = 8 ** -0.5 * 64 ** -0.5
MEM = 256
XHEADS = 4

RAW_SLOTS = 3
SPLIT_SLOTS = 3
GEMM_BANKS = 3



PROJECTIONS = [("p2", n) for n in ("cq0", "cq1", "ckv", "kc", "vc", "wg", "ki")] + [
    ("kvd",), ("p2", "ks"), ("kd",), ("p2", "kw"), ("iq", 0), ("p2", "vs"), ("iq", 1), ("p2", "vw"), ("iq", 2),
    ("p2", "qn0"), ("iq", 3), ("p2", "qn1"), ("uq", 0), ("p2", "qn2"), ("uq", 1), ("p2", "qn3"), ("uq", 2), ("uq", 3)]


def job_plan():
    jobs = []
    for l in range(DEPTH):
        jobs += [(("u", l, i), 8, SEQ, "act") for i in range(4)]
        jobs += [(("glu", l, i), 4, SEQ, "act") for i in range(4)]
        jobs += [(("q", l, i), 8, SEQ, "act") for i in range(4)]
        jobs += [(("k", l, 0), 8, SEQ, "act"), (("v", l, 0), 8, SEQ, "act")]
        for i in range(4):
            jobs += [(("cc", l, i), 8, SEQ, "act"), (("cx", l, i), 8, SEQ, "dve"), (("cb", l, i), 8, SEQ, "dve")]
        for i in range(KD):
            jobs += [(("g0", l, i), 8, SEQ, "act"), (("ao", l, i), 4, SEQ, "dve"),
                     (("g1", l, i), 8, SEQ, "act"), (("co", l, i), 4, SEQ, "dve"),
                     (("g2", l, i), 8, SEQ, "act"), (("so", l, i), 4, SEQ, "dve")]
        jobs += [(("mix", l, i), 8, SEQ, "dve") for i in range(KD)]
        for c, (t0, nt) in enumerate(FFN_CHUNKS):
            for t in range(t0, t0 + nt):
                jobs += [(("gt", l, t), 8, SEQ, "act"), (("up", l, t), 8, SEQ, "dve")]
            jobs += [(("fo", l, c, i), nt, SEQ, "dve") for i in range(KD)]
    jobs += [(("xk", i), 8, MEM, "act") for i in range(XHEADS)]
    jobs += [(("xv", i), 8, MEM, "act") for i in range(XHEADS)]
    for key in PROJECTIONS:
        K = {"kvd": 1, "kd": 1, "iq": 2, "uq": 2}.get(key[0], 8)
        jobs.append((key, K, SEQ, "act"))
    jobs += [(("out2", i), 8, SEQ, "dve") for i in range(KD)]
    jobs += [(("xq", i), 8, SEQ, "act") for i in range(XHEADS)]
    jobs += [(("xo", i), 4, SEQ, "dve") for i in range(KD)]
    for c, (t0, nt) in enumerate(FF2_CHUNKS):
        jobs += [(("fi", t), 8, SEQ, "act") for t in range(t0, t0 + nt)]
        jobs += [(("fo2", c, i), nt, SEQ, "dve") for i in range(KD)]
    return jobs


def weight_tile(w, key):
    kind = key[0]
    cols = lambda a, c, n=P: a[:, c:c + n]
    both = lambda a, c0, c1: np.concatenate([a[:, c0:c0 + HEAD], a[:, c1:c1 + HEAD]], 1)
    pairs = lambda a: np.concatenate(
        [np.concatenate([a[j * HEAD:(j + 1) * HEAD], a[(j + 4) * HEAD:(j + 5) * HEAD]]) for j in range(4)])
    if kind in ("u", "k", "v", "cc", "cx", "cb"):
        return cols(w["w_in"][key[1]], W_IN_COLS[kind] + P * key[2])
    if kind in ("g0", "g1", "g2"):
        return cols(w["w_in"][key[1]], W_IN_COLS["g"] + D_MODEL * int(kind[1]) + P * key[2])
    if kind == "q":
        return both(w["w_in"][key[1]], key[2] * HEAD, (key[2] + 4) * HEAD)
    if kind == "glu":
        return cols(w["w_ssm_glu"][key[1]], P * key[2])
    if kind == "ao":
        return cols(pairs(w["w_attn_o"][key[1]]), P * key[2])
    if kind == "co":
        return cols(w["w_conv_o"][key[1]], P * key[2])
    if kind == "so":
        return cols(w["w_ssm_o"][key[1]], P * key[2])
    if kind == "mix":
        return cols(w["w_mix_o"][key[1]], P * key[2])
    if kind in ("gt", "up"):
        return cols(w["w_ffn_in"][key[1]], P * key[2] + (FFN_TILES * P if kind == "up" else 0))
    if kind == "fo":
        t0, nt = FFN_CHUNKS[key[2]]
        return cols(w["w_ffn_out"][key[1]][t0 * P:(t0 + nt) * P], P * key[3])
    if kind == "p2":
        a, name = w["w_in_2"][0], key[1]
        if name in ("cq0", "cq1", "ckv"):
            return cols(a, {"cq0": 0, "cq1": 128, "ckv": 256}[name])
        if name == "ki":
            return both(a, 384, 384)
        if name == "wg":
            return np.concatenate([a[:, 448:456], a[:, 1640:1760]], 1)
        if name[:2] == "qn":
            j = int(name[2])
            return both(a, 456 + j * HEAD, 456 + (j + 4) * HEAD)
        return cols(a, 968 + {"kc": 0, "vc": 1, "ks": 2, "vs": 3, "kw": 4, "vw": 5}[name] * P)
    if kind == "kvd":
        return w["w_dsa_ukv_2"][0]
    if kind == "kd":
        return both(w["w_dsa_ukv_2"][0], 0, 0)
    if kind == "iq":
        return cols(w["w_idx_q_2"][0], P * key[1])
    if kind == "uq":
        return cols(w["w_dsa_uq_2"][0], P * key[1])
    if kind == "out2":
        a = w["w_out_2"][0]
        return cols(np.concatenate([a[:512], pairs(a[512:])]), P * key[1])
    if kind in ("xk", "xv", "xq", "xo"):
        return cols(w["w_" + kind + "_2"][0], P * key[1])
    if kind == "fi":
        return cols(w["w_ff_in_2"][0], P * key[1])
    if kind == "fo2":
        t0, nt = FF2_CHUNKS[key[1]]
        return cols(w["w_ff_out_2"][0][t0 * P:(t0 + nt) * P], P * key[2])
    raise KeyError(key)




def param_columns():
    at, n = {}, 0
    for l in range(DEPTH):
        for name, c in (("norm_mix", 8), ("norm_ffn", 8), ("b_gate", 24), ("sinks", 8), ("conv", 12), ("ssm_d", 4)):
            at[name, l] = (n, c)
            n += c
    for name, c in (("norm_final", 8), ("norm1", 8), ("norm2", 8), ("norm3", 8), ("mem_norm", 8), ("cq", 2),
                    ("ckv", 1), ("lng", 1), ("lnb", 1), ("dqn", 1), ("dkn", 1), ("nqn", 1), ("nkn", 3),
                    ("xqn", 1), ("xkn", 1), ("pe", 64)):
        at[name] = (n, c)
        n += c
    return at, n


def pack_params(w):
    at, n = param_columns()
    out = np.zeros((P, n), np.float32)

    def put(key, a):
        c, m = at[key]
        out[:, c:c + m] = a

    feat = lambda v: np.asarray(v).reshape(-1, P).T
    twice = lambda v: np.concatenate([v, v])
    for l in range(DEPTH):
        put(("norm_mix", l), feat(w["norm_mix"][l]))
        put(("norm_ffn", l), feat(w["norm_ffn"][l]))
        put(("b_gate", l), feat(w["b_gate"][l]))
        put(("sinks", l), np.broadcast_to(w["attn_sinks"][l], (P, 8)))
        put(("conv", l), feat(w["conv_w"][l].reshape(-1)))
        put(("ssm_d", l), feat(w["ssm_d"][l]))
    put("norm_final", feat(w["norm_final"]))
    put("norm1", feat(w["norm1_g_2"][0]))
    put("norm2", feat(w["norm2_g_2"][0]))
    put("norm3", feat(w["norm3_g_2"][0]))
    put("mem_norm", feat(w["mem_norm_g_2"][0]))
    put("cq", feat(w["dsa_cq_g_2"][0]))
    put("ckv", feat(w["dsa_ckv_g_2"][0]))
    put("lng", twice(w["idx_k_ln_g_2"][0])[:, None])
    put("lnb", twice(w["idx_k_ln_b_2"][0])[:, None])
    put("dqn", twice(w["dsa_qn_g_2"][0])[:, None])
    put("dkn", twice(w["dsa_kn_g_2"][0])[:, None])
    put("nqn", twice(w["nsa_qn_g_2"][0])[:, None])
    put("nkn", twice(w["nsa_kn_g_2"][0].T))
    put("xqn", w["xq_norm_g_2"][0][:, None])
    put("xkn", w["xk_norm_g_2"][0][:, None])
    pe = w["nsa_cmp_pe_2"][0]
    put("pe", twice(pe.transpose(2, 0, 1).reshape(HEAD, 64)))
    return out


def pack_ssm(w):
    out = np.zeros((DEPTH * 4, P, SSM_PARAMS), np.float32)
    for l in range(DEPTH):
        for ft in range(4):
            g = slice(ft * SSM_G, (ft + 1) * SSM_G)
            re, im = w["ssm_a_re"][l, g].T, w["ssm_a_im"][l, g].T
            br = w["ssm_b_re"][l, g].transpose(1, 0, 2).reshape(SSM_STATE, -1)
            bi = w["ssm_b_im"][l, g].transpose(1, 0, 2).reshape(SSM_STATE, -1)
            cr = w["ssm_c_re"][l, g].transpose(2, 0, 1).reshape(SSM_STATE, -1)
            ci = w["ssm_c_im"][l, g].transpose(2, 0, 1).reshape(SSM_STATE, -1)
            dt = np.broadcast_to(w["ssm_log_dt"][l, g], (SSM_STATE, SSM_G))
            top = np.concatenate([re, im, dt, br, bi, cr, ci], 1)
            low = np.concatenate([re, im, dt, bi, br, ci, cr], 1)
            out[l * 4 + ft] = np.concatenate([top, low])
    return out




CONST_MATS = ("ident", "ones", "blk", "rot1", "rot2")
CONST_AT = {n: i * P for i, n in enumerate(CONST_MATS)}
_n = len(CONST_MATS) * P
for _name, _c in (("C1", SEQ), ("S1", SEQ), ("C2", SEQ), ("S2", SEQ), ("sw", 2 * P), ("mk", SEQ),
                  ("cmp_add", NB * CMP_N), ("cmp_mul", NB * CMP_N), ("J", 9), ("eps", 1), ("sgn", 1), ("neg", 1)):
    CONST_AT[_name] = _n
    _n += _c
CONST_N = _n


def constants():
    c = np.zeros((P, CONST_N), np.float32)

    def put(name, a):
        a = np.asarray(a, np.float32).reshape(P, -1)
        c[:, CONST_AT[name]:CONST_AT[name] + a.shape[1]] = a

    put("ident", np.eye(P))
    put("ones", np.full((P, P), 1.0 / D_MODEL))
    put("blk", np.kron(np.eye(2), np.full((HEAD, HEAD), 1.0 / HEAD)))

    def rotation(half):
        r = np.zeros((P, P))
        for base in (0, HEAD):
            for d in range(half):
                r[base + d + half, base + d] = -1.0
                r[base + d, base + d + half] = 1.0
        return r

    put("rot1", rotation(8))
    put("rot2", rotation(32))

    def tables(theta, half, width):
        pos = np.arange(SEQ, dtype=np.float32)
        inv = np.float32(theta) ** (-np.arange(half, dtype=np.float32) / np.float32(half))
        if width == 16:
            inv = np.float32(theta) ** (-np.arange(0, 16, 2, dtype=np.float32) / np.float32(16))
        ang = (pos[:, None] * inv.astype(np.float32)[None, :]).astype(np.float32).astype(np.float64)
        co, si = np.cos(ang).T, np.sin(ang).T
        ct, st = np.ones((HEAD, SEQ)), np.zeros((HEAD, SEQ))
        ct[:half], ct[half:2 * half] = co, co
        st[:half], st[half:2 * half] = si, si
        return np.concatenate([ct, ct]), np.concatenate([st, st])

    a, b = tables(500000.0, 8, 16)
    put("C1", a)
    put("S1", b)
    a, b = tables(10000.0, 32, 64)
    put("C2", a)
    put("S2", b)
    qi, kj = np.arange(P)[:, None], np.arange(2 * P)[None, :]
    delta = qi + P - kj
    put("sw", np.where((delta >= 0) & (delta < P), 0.0, NEG))
    mk = np.zeros((P, SEQ))
    mk[:, SEQ - P:] = np.where(np.arange(P)[None, :] <= qi, 0.0, NEG)
    put("mk", mk)
    t = np.arange(NB)[None, :, None] * P + np.arange(P)[:, None, None]
    ok = np.arange(CMP_N)[None, None, :] * CMP_STRIDE + CMP_L - 1 <= t
    put("cmp_add", np.where(ok, 0.0, NEG))
    put("cmp_mul", ok)
    put("J", np.broadcast_to(np.arange(9), (P, 9)))
    put("eps", np.full(P, EPS))
    put("sgn", np.where(np.arange(P) < HEAD, 1.0, -1.0))
    put("neg", np.full(P, -1.0))
    return c




def units_sw(l):
    out = []
    for b in range(NB):
        for j in range(4):
            out.append(dict(kind="sw", l=l, b=b, j=j, W=P if b == 0 else 2 * P, k0=0 if b == 0 else (b - 1) * P,
                            first=True, last=True))
    return out


def units_dsa(b):
    return [dict(kind="dsa", b=b, j=j, W=(b + 1) * P, k0=0, first=True, last=True) for j in range(4)]


def units_nsa(b):
    out = []
    for j in range(4):
        out.append(dict(kind="cmp", b=b, j=j, W=CMP_N, k0=0, first=True, last=False))
        out.append(dict(kind="slc", b=b, j=j, W=(b + 1) * P, k0=0, first=False, last=False))
        out.append(dict(kind="win", b=b, j=j, W=(b + 1) * P, k0=0, first=False, last=True))
    return out


def units_x():
    return [dict(kind="x", b=b, j=j, W=MEM, k0=0, first=True, last=True) for b in range(NB) for j in range(2)]


def all_units():
    lists = {"sw0": units_sw(0), "sw1": units_sw(1)}
    for b in range(NB):
        lists["dsa", b] = units_dsa(b)
        lists["nsa", b] = units_nsa(b)
    lists["x"] = units_x()
    n = g = 0
    for us in lists.values():
        for u in us:
            u["n"], u["group"] = n, g
            n += 1
            g += u["last"]
    return lists


class Line:

    def __init__(self, eng, chain):
        self.eng, self.chain, self.count = eng, chain, {}

    def done(self, ins, sem=None):
        sem = sem or self.chain
        ins.then_inc(sem, 1)
        self.count[sem.name] = self.count.get(sem.name, 0) + 1
        self.eng.wait_ge(sem, self.count[sem.name])


def block_program(nc, wstream, params, ssmp, cmpw, consts, xT, memT, outT):
    jobs = job_plan()
    offset, number, taken = {}, {}, {}
    at = 0
    free_count = {"act": 0, "dve": 0}
    for n, (key, K, N, who) in enumerate(jobs):
        offset[key], number[key] = at, n
        at += K * P * P
        free_count[who] += 1
        taken[key] = (who, free_count[who])
    units = all_units()
    units2 = [u for b in range(NB) for u in units["dsa", b] + units["nsa", b]]
    pcol, npar = param_columns()

    ctx = ExitStack()
    with ctx:
        def sem(name):
            return ctx.enter_context(nc.semaphore(name))

        base = (nc.sbuf_base + 63) // 64 * 64
        cursor = [base]

        def place(name, shape, dt, at=None):
            size = 4 * int(np.prod(shape[1:]))
            off = cursor[0] if at is None else at
            if at is None:
                cursor[0] += (size + 31) // 32 * 32
            return nc.alloc_sbuf_tensor_at(name, shape, dt, offset=off), off

        X, _ = place("x", [P, KD, SEQ], F32)
        Hh, _ = place("h_hi", [P, KD, SEQ], F32R)
        Hl, _ = place("h_lo", [P, KD, SEQ], F32R)
        Mh, m_at = place("m_hi", [P, KD, SEQ], F32R)
        Ml, _ = place("m_lo", [P, KD, SEQ], F32R)
        Bh, b_at = place("b_hi", [P, 12, SEQ], F32R)
        Bl, _ = place("b_lo", [P, 12, SEQ], F32R)
        R, _ = place("work_m", [P, 2 * KD * SEQ], F32, at=m_at)
        R2, _ = place("work_b", [P, 24 * SEQ], F32, at=b_at)
        raw, _ = place("w_raw", [P, RAW_SLOTS, 8 * P], F32)
        Wh, _ = place("w_hi", [P, SPLIT_SLOTS, 8, P], F32R)
        Wl, _ = place("w_lo", [P, SPLIT_SLOTS, 8, P], F32R)
        CON, _ = place("consts", [P, CONST_N], F32)
        PAR, _ = place("params", [P, npar], F32)
        acc, _ = place("square_sum", [P, SEQ], F32)
        rinv, _ = place("rinv", [P, SEQ], F32)
        tmp, _ = place("tmp", [P, 3, SEQ], F32)
        rawt, _ = place("raw_tile", [P, 2, SEQ], F32)
        stat, _ = place("stats", [P, 3, 12], F32)
        VX, _ = place("memory_values", [P, 2, XHEADS * P], F32)
        gtok, _ = place("gate_tok", [P, NB, 24], F32)
        wtok, _ = place("widx_tok", [P, NB, 8], F32)
        m8, _ = place("max8", [P, 8], F32)
        TS, _ = place("small_work", [P, 2400], F32)
        assert cursor[0] <= nc.sbuf_usable_end, (cursor[0], nc.sbuf_usable_end)

        psG = ctx.enter_context(nc.psum_tensor("psG", [P, GEMM_BANKS, SEQ], F32))
        psS = ctx.enter_context(nc.psum_tensor("psS", [P, 2, SEQ], F32))
        psT = ctx.enter_context(nc.psum_tensor("psT", [P, 2, SEQ], F32))
        psO = ctx.enter_context(nc.psum_tensor("psO", [P, SEQ], F32))

        def con(name, n, rows=P):
            return CON[0:rows, CONST_AT[name]:CONST_AT[name] + n]

        ident, ones, blk = con("ident", P), con("ones", P), con("blk", P)
        rots = {1: con("rot1", P), 2: con("rot2", P)}
        tabs = {1: (con("C1", SEQ), con("S1", SEQ)), 2: (con("C2", SEQ), con("S2", SEQ))}
        eps = con("eps", 1)

        def par(key, i=0, n=1):
            c, _ = pcol[key]
            return PAR[:, c + i:c + i + n]

        s_raw = [sem(f"weights_landed{i}") for i in range(RAW_SLOTS)]
        s_hi = sem("weights_hi")
        s_split = sem("weights_split")
        s_job = sem("product_done")
        s_took = {"act": sem("product_taken_act"), "dve": sem("product_taken_dve")}
        s_in = sem("inputs_landed")
        s_mem = sem("memory_landed")
        s_ssmp = [sem("ssm_params_landed0"), sem("ssm_params_landed1")]
        s_toep = sem("toeplitz_landed")
        s_cw = sem("cmp_weights_landed")
        s_out = sem("out_landed")
        c_act, c_dve, c_pool = sem("act_chain"), sem("dve_chain"), sem("pool_chain")
        s_ssq, s_ms, s_sd = sem("squares_summed"), sem("mean_square"), sem("norm_root")
        s_xs, s_hh, s_h, s_hp = sem("x_scaled"), sem("h_hi_ready"), sem("h_lo_ready_dve"), sem("h_lo_ready_pool")
        s_m, s_kx, s_kxsq, s_kxms, s_xtr, s_vx = (sem("mem_" + n) for n in (
            "h_ready", "keys_raw", "keys_squared", "keys_mean", "values_transposed", "values_ready"))
        s_xtr_in = sem("mem_values_raw")
        s_kxsd, s_kxn, s_norm = sem("mem_keys_root"), sem("mem_keys_ready"), sem("prob_factor")
        s_y, s_fin = sem("final_x_ready"), sem("final_norm")
        names = ("par_ready y1 args sincos consts_ready wb w12 x1 g_out g_pad wbt wbt_sb u2 u2_sb ug ug_sb e z yc yc_sb yt "
                 "ypre ys ysplit glu_sig glu_out").split()
        v = {n: sem("ssm_" + n) for n in names}
        s_rawt, s_rot, s_rope = sem("rope_in"), sem("rotated"), sem("roped")
        s_vraw, s_vt, s_vtok = sem("v_raw"), sem("v_transposed"), sem("v_tok")
        s_cc, s_cy = sem("conv_cc"), sem("conv_y")
        s_sig, s_merged = sem("gate_sigmoid"), sem("merged")
        s_silu, s_hid = sem("silu"), sem("hidden")
        s_sc, s_masked, s_neg, s_exp = sem("scores"), sem("masked"), sem("neg_max"), sem("exped")
        s_prob, s_tr, s_pt, s_pv, s_oe = (sem(x) for x in ("probs", "probs_t", "probs_t_sb", "pv", "attn_out"))
        s_is, s_ir, s_ia, s_sel = sem("idx_scores"), sem("idx_relu"), sem("idx_added"), sem("selected")
        s_p = {n: sem("post_" + n) for n in ("raw", "cmpin", "cmpo", "cmean", "cen", "sqa", "sqd", "mean", "sd",
                                          "qn", "rot", "rotd", "out", "tok", "toksb")}

        block = ctx.enter_context(nc.Block())

        def work(t, off, shape):
            n = int(np.prod(shape[1:]))
            a = t[0:shape[0], off:off + n]
            if len(shape) == 3:
                a = a.rearrange("p (a b) -> p a b", b=shape[2])
            elif len(shape) == 4:
                a = a.rearrange("p (a b c) -> p a b c", b=shape[2], c=shape[3])
            return a

        uT = work(R, 0, [P, 4, SEQ])
        ysf = work(R, 2048, [P, 4, SEQ])
        U2 = work(R, 4096, [SSM_C, SSM_G, P])
        UG = work(R, 5120, [P, SSM_G, SSM_C])
        zb = [work(R, 5632 + 512 * i, [P, SSM_G, SSM_C]) for i in range(3)]
        Y2 = work(R, 7168, [SSM_C, SSM_T, P])
        qT1, kT1, vt1 = work(R, 0, [P, 4, SEQ]), work(R, 4096, [P, SEQ]), work(R, 4608, [P, NB, P])
        sp = [work(R2, SSM_PARAMS * i, [P, SSM_PARAMS]) for i in range(2)]
        o = 2 * SSM_PARAMS
        WbE = work(R2, o, [P, SSM_G, SSM_T, SSM_H])
        WbI = work(R2, o + 1024, [P, SSM_G, SSM_T, SSM_H])
        W1 = work(R2, o + 2048, [P, SSM_G, SSM_T + 1, SSM_H])
        W2 = work(R2, o + 3200, [P, SSM_G, SSM_T, SSM_H])
        TO = work(R2, o + 4224, [P, SSM_G, P])
        WT = work(R2, o + 5248, [P, SSM_G, P])
        WTI = work(R2, o + 6272, [P, SSM_G, P])
        rotC = work(R2, o + 7296, [P, SSM_G, SSM_C])
        rotS = work(R2, o + 7808, [P, SSM_G, SSM_C])
        Gp = work(R2, o + 8320, [SSM_H, SSM_G, 15 * SSM_H])
        X1 = work(R2, o + 10240, [P, SSM_G, SSM_H])
        acoef = work(R2, o + 10368, [P, SSM_G, SSM_C])
        assert o + 10880 <= 24 * SEQ
        NJ = 9 + 8 + 8
        arg = work(TS, 0, [P, SSM_G, NJ])
        arg2 = work(TS, 200, [P, SSM_G, NJ])
        sn = work(TS, 400, [P, SSM_G, NJ])
        cs = work(TS, 600, [P, SSM_G, NJ])
        red = work(TS, 800, [P, SSM_G, NJ])
        mag = work(TS, 1000, [P, SSM_G, 9])
        Lr = work(TS, 1072, [P, SSM_G, 9])
        Li = work(TS, 1144, [P, SSM_G, 9])
        Lcr = work(TS, 1216, [P, SSM_G, 8])
        Lci = work(TS, 1280, [P, SSM_G, 8])
        sm = work(TS, 1344, [P, 16, SSM_G])
        Z1 = work(TS, 1472, [P, SSM_G, SSM_H])
        Z2 = work(TS, 1600, [P, SSM_G, SSM_H])
        Y1n = work(TS, 1728, [P, SSM_G, SSM_H])
        pwork = tmp[:, :, :].rearrange("p a b -> p (a b)")[:, 0:1152]
        zc = work(TS, 0, [P, SEQ + 2])
        ycv = work(TS, 514, [P, SEQ])
        qn, qd, qi = (work(R, 2048 * i, [P, 4, SEQ]) for i in range(3))
        kd, ki, ks, kw = (work(R, 6144 + 512 * i, [P, SEQ]) for i in range(4))
        vd, vs, vw = work(R2, 0, [P, NB, HEAD]), work(R2, 256, [P, NB, P]), work(R2, 768, [P, NB, P])
        vc, kc = work(R2, 1280, [P, P]), work(R2, 1408, [P, CMP_N])
        iacc, iwork, selm = work(R2, 1536, [P, SEQ]), work(R2, 2048, [P, SEQ]), work(R2, 2560, [P, SEQ])
        irelu = work(R2, 3072, [P, 2, SEQ])
        cmpW = work(R2, 6144, [P, 2, CMP_L, HEAD])
        cmpin = work(TS, 0, [P, CMP_L, CMP_N])
        cmpt = work(TS, 1000, [P, 2, CMP_N])
        cqf = work(TS, 0, [P, 3, SEQ])
        raws = [rawt[:, 0, :], rawt[:, 1, :], work(R2, 11 * SEQ, [P, SEQ]), work(R2, 23 * SEQ, [P, SEQ])]
        qx, kx, vx = work(R, 0, [P, 4, SEQ]), work(TS, 1100, [P, XHEADS, MEM]), VX
        memf = work(R2, 8192, [P, KD, MEM])
        xsq = work(R2, 2048, [P, 2, MEM])
        xsd = work(R2, 2560, [P, XHEADS, MEM])
        xraw = work(R2, 3584, [P, 2, MEM])
        mH = Bh[:, 0:4, :].rearrange("p a b -> p (a b)").rearrange("p (k n) -> p k n", n=MEM)
        mL = Bl[:, 0:4, :].rearrange("p a b -> p (a b)").rearrange("p (k n) -> p k n", n=MEM)

        def probs(u):
            n, W = u["n"], u["W"]
            if u["kind"] == "sw":
                p = work(R, 5120 + 1024 * (n % 2), [P, 2, 2 * P])
                t = work(R, 7168 + 512 * (n % 2), [P, 2, 2, P])
            else:
                p = work(R2, 4096 + 1024 * (n % 3), [P, 2, SEQ])
                t = work(R2, 7168 + 1024 * (n % 2), [P, 2, NB, P])
            return p[:, :, 0:W], t

        def narrow(u):
            return u["kind"] in ("sw", "x")

        def ahead(u):
            return 1 if u["kind"] == "sw" else 2

        def stats(u):
            return stat[:, u["n"] % 3]

        def score_banks(u):
            return psG[:, 0:2, 0:u["W"]] if u["n"] % 2 else psS[:, :, 0:u["W"]]

        def transpose_banks(u):
            n = u["n"]
            if narrow(u):
                return psT[:, n % 2, :].rearrange("p (a w) -> p a w", a=2)
            return psT[:, :, :]

        def key_blocks(u):
            return [(0, u["W"])] if u["kind"] == "cmp" else [(i, P) for i in range(u["W"] // P)]

        def moving(key, k):
            kind = key[0]
            if kind == "glu":
                return Bh[:, 4 + k, :], Bl[:, 4 + k, :]
            if kind == "ao":
                return Bh[:, k, :], Bl[:, k, :]
            if kind == "co":
                return Bh[:, 4 + k, :], Bl[:, 4 + k, :]
            if kind == "so":
                return Bh[:, 8 + k, :], Bl[:, 8 + k, :]
            if kind in ("mix", "fo", "fo2"):
                return Mh[:, k, :], Ml[:, k, :]
            if kind in ("iq", "uq"):
                return Bh[:, 8 + k, :], Bl[:, 8 + k, :]
            if kind in ("kd", "kvd"):
                return Bh[:, 10, :], Bl[:, 10, :]
            if kind in ("xk", "xv"):
                return mH[:, k, :], mL[:, k, :]
            return Hh[:, k, :], Hl[:, k, :]

        NORMS = {"mix0": 0, "ffn0": 1, "mix1": 2, "ffn1": 3, "mem": 4, "final": 5, "norm1": 6, "norm2": 7, "norm3": 8}
        h_norm = {name: i for i, name in enumerate(n for n in NORMS if n not in ("final", "mem"))}
        first_job = {"mix0": ("u", 0, 0), "ffn0": ("gt", 0, 0), "mix1": ("u", 1, 0), "ffn1": ("gt", 1, 0),
                     "norm1": PROJECTIONS[0], "norm2": ("xq", 0), "norm3": ("fi", 0)}
        norm_before = {number[key] + SPLIT_SLOTS: name for name, key in first_job.items()}

        roots = (rinv, acc)
        def description(key):
            kind, name = key[0], key[1] if len(key) > 1 else None
            if kind == "p2":
                return {"kc": ("cmpk", ("nkn", 0), kc), "vc": ("cmpv", None, None), "cq0": ("lat", None, 0),
                        "cq1": ("lat2", None, 1), "ckv": ("lat1", None, 2), "wg": ("tokwg", None, None),
                        "vs": ("tok", None, vs), "vw": ("tok", None, vw), "ki": ("ln", None, ki),
                        "ks": ("rms", ("nkn", 1), ks), "kw": ("rms", ("nkn", 2), kw),
                        }.get(name) or ("rms", ("nqn", 0), qn[:, int(name[2])])
            return {"kvd": lambda: ("tokd", None, None), "kd": lambda: ("rms", ("dkn", 0), kd),
                    "iq": lambda: ("rope", None, qi[:, name]), "uq": lambda: ("rms", ("dqn", 0), qd[:, name]),
                    "xq": lambda: ("xrms", ("xqn", 0), qx[:, name])}[kind]()

        PHASES = {"cmpk": ("", "cmp", "mean", "rot"), "cmpv": ("", "cmp", "tok"), "lat": ("",), "lat2": ("", "mean"),
                  "lat1": ("", "mean"), "tokwg": ("", "tok"), "tok": ("", "tok"), "tokd": ("", "tok"),
                  "ln": ("", "cmean", "mean", "rot"), "rms": ("", "mean", "rot"), "rope": ("", "rot"), "xrms": ("", "mean")}
        posts = []
        for key in PROJECTIONS + [("xq", j) for j in range(4)]:
            kind, gain, dest = description(key)
            posts.append(dict(key=key, kind=kind, gain=gain, dest=dest, i=len(posts)))
        by_key = {p["key"]: p for p in posts}
        block2_posts, x_posts = posts[:len(PROJECTIONS)], posts[len(PROJECTIONS):]

        def waves(ps):
            for s_ in range(len(ps) + 3):
                old = [(ps[s_ - f], PHASES[ps[s_ - f]["kind"]][f]) for f in (3, 2, 1)
                       if 0 <= s_ - f < len(ps) and f < len(PHASES[ps[s_ - f]["kind"]])]
                yield (ps[s_] if s_ < len(ps) else None), old

        tally = {n: 0 for n in s_p}
        square_reader = [None, None]

        def step(p, *names_):
            for n_ in names_:
                tally[n_] += 1
                p[n_] = tally[n_]

        def square_place(p):
            i_ = (tally["sqa"] + tally["sqd"]) % 2
            p["sq_at"], p["sq_wait"] = i_, square_reader[i_]
            square_reader[i_] = posts[p["i"] + 1] if p["kind"] == "lat" else p

        for ps in (block2_posts, x_posts):
            for new, old in waves(ps):
                if new:
                    step(new, "raw")
                    if new["kind"] in ("lat", "lat2", "lat1", "rms", "xrms"):
                        square_place(new)
                        step(new, "sqa")
                for p, phase in old:
                    if phase in ("cmp", "cmean"):
                        step(p, "cmpo" if phase == "cmp" else "cmean", "cen")
                        if p["kind"] != "cmpv":
                            square_place(p)
                            step(p, "sqd")
                    elif phase == "mean":
                        step(p, "mean", "sd", "qn" if "rot" in PHASES[p["kind"]] else "out")
                    elif phase == "rot":
                        step(p, "rot", "rotd", "out")
                    elif phase == "tok":
                        step(p, "tok", "toksb")
                if new and new["kind"] in ("cmpk", "cmpv"):
                    step(new, "cmpin")
        all_done = dict(tally)
        block2_done = {n_: max(p.get(n_, 0) for p in block2_posts) for n_ in s_p}

        @block.sync
        def _(sp_eng):
            for n, (key, K, N, who) in enumerate(jobs):
                if n >= RAW_SLOTS:
                    sp_eng.wait_ge(s_split, n - RAW_SLOTS + 1)
                src = wstream[offset[key]:offset[key] + K * P * P].rearrange("(p f) -> p f", p=P)
                sp_eng.dma_start(raw[:, n % RAW_SLOTS, 0:K * P], src).then_inc(s_raw[n % RAW_SLOTS], 16)
            sp_eng.wait_ge(s_y, 1)
            sp_eng.dma_start(outT, X[:, :, :]).then_inc(s_out, 16)
            sp_eng.wait_ge(s_out, 16)

        @block.gpsimd
        def _(pool):
            def split_weights(n):
                key, K, N, who = jobs[n]
                pool.wait_ge(s_raw[n % RAW_SLOTS], 16 * (n // RAW_SLOTS + 1))
                if n >= SPLIT_SLOTS:
                    pool.wait_ge(s_job, n - SPLIT_SLOTS + 1)
                w = raw[:, n % RAW_SLOTS, 0:K * P]
                hi = Wh[:, n % SPLIT_SLOTS, 0:K, :].rearrange("p k n -> p (k n)")
                lo = Wl[:, n % SPLIT_SLOTS, 0:K, :].rearrange("p k n -> p (k n)")
                pool.tensor_scalar(hi, w, 1.0, 0.0, ALU.mult, ALU.add).then_inc(s_hi, 1)
                pool.wait_ge(s_hi, n + 1)
                pool.tensor_tensor(lo, w, hi.bitcast(F32), ALU.subtract).then_inc(s_split, 1)

            def norm_low_parts(name):
                for k in range(1, KD, 2):
                    pool.wait_ge(s_hh, KD * h_norm[name] + k + 1)
                    pool.tensor_tensor(Hl[:, k], tmp[:, k % 3, :], Hh[:, k].bitcast(F32), ALU.subtract).then_inc(s_hp, 1)

            def scale_probs(u):
                n = u["n"]
                p, _ = probs(u)
                st = stats(u)
                pool.wait_ge(s_norm, n - units["dsa", 0][0]["n"] + 1)
                for a in range(2):
                    ins = pool.tensor_scalar(p[:, a], p[:, a], st[:, 8 + a:9 + a], 1.0, ALU.mult, ALU.mult)
                    ins.then_inc(s_prob if a else c_pool, 1)

            for n in range(len(jobs)):
                if n in norm_before:
                    norm_low_parts(norm_before[n])
                if n == number["out2", 0] + SPLIT_SLOTS:
                    for u in units2:
                        scale_probs(u)
                split_weights(n)

        group_total = {"nsa": units["nsa", NB - 1][-1]["group"] + 1, "x": units["x"][-1]["group"] + 1}

        @block.tensor
        def _(pe):
            def product(key):
                n = number[key]
                _, K, N, who = jobs[n]
                pe.wait_ge(s_split, n + 1)
                if n >= GEMM_BANKS:
                    who0, count = taken[jobs[n - GEMM_BANKS][0]]
                    pe.wait_ge(s_took[who0], count)
                out = psG[:, n % GEMM_BANKS, 0:N]
                for k in range(K):
                    hi, lo = moving(key, k)
                    for need in h_need(key, k):
                        pe.wait_ge(*need)
                    whi, wlo = Wh[:, n % SPLIT_SLOTS, k, :], Wl[:, n % SPLIT_SLOTS, k, :]
                    pe.matmul(out, whi, hi, start=(k == 0), stop=False)
                    pe.matmul(out, whi, lo, start=False, stop=False)
                    ins = pe.matmul(out, wlo, hi, start=False, stop=(k == K - 1))
                ins.then_inc(s_job, 1)

            def h_need(key, k):
                kind = key[0]
                for name, first in first_job.items():
                    if key == first:
                        n_ = KD // 2 * h_norm[name] + k // 2 + 1
                        return [(s_hp if k % 2 else s_h, n_)]
                if kind == "xk" and key[1] == 0:
                    return [(s_m, k + 1)]
                if kind == "glu" and key[2] == 0:
                    return [(v["ysplit"], key[1] * 4 + k + 1)]
                if kind == "ao" and key[2] == 0:
                    return [(s_oe, 16 * (key[1] + 1))]
                if kind == "co" and key[2] == 0:
                    return [(s_cy, 4 * (key[1] + 1))]
                if kind == "so" and key[2] == 0:
                    return [(v["glu_out"], 4 * (key[1] + 1))]
                if kind == "mix" and key[2] == 0:
                    return [(s_merged, 8 * key[1] + k + 1)]
                if kind == "fo" and key[3] == 0:
                    return [(s_hid, FFN_TILES * key[1] + FFN_CHUNKS[key[2]][0] + k + 1)]
                if kind == "fo2" and key[2] == 0:
                    return [(s_hid, FFN_TILES * DEPTH + FF2_CHUNKS[key[1]][0] + k + 1)]
                if kind == "kvd":
                    return [(s_p["out"], by_key["p2", "ckv"]["out"])]
                if key == ("iq", 0):
                    return [(s_p["out"], by_key["p2", "cq1"]["out"])]
                if kind == "out2" and key[1] == 0:
                    return [(s_oe, group_total["nsa"])]
                if kind == "xo" and key[1] == 0:
                    return [(s_oe, group_total["x"])]
                return []

            def mean_square(name, cols=SEQ):
                pe.wait_ge(s_ssq, NORMS[name] + 1)
                pe.matmul(psO[:, 0:cols], ones, acc[:, 0:cols], start=True, stop=True).then_inc(s_ms, 1)

            def ssm(l, ft):
                f = l * 4 + ft
                pe.wait_ge(v["w12"], f + 1)
                for g in range(SSM_G):
                    ins = pe.matmul(psS[0:SSM_H, g // 4, (g % 4) * P:(g % 4 + 1) * P], X1[:, g],
                                    W1[:, g, 0:SSM_T, :], start=True, stop=True)
                ins.then_inc(v["g_out"], 1)
                pe.wait_ge(v["wb"], f + 1)
                for g in range(SSM_G):
                    ins = pe.transpose(psT[:, g // 4, (g % 4) * P:(g % 4 + 1) * P],
                                       WbE[:, g].rearrange("p a b -> p (a b)"), ident)
                ins.then_inc(v["wbt"], 1)
                pe.wait_ge(v["g_pad"], f + 1)
                for g in range(SSM_G):
                    ins = pe.transpose(psS[:, g // 4, (g % 4) * P:(g % 4 + 1) * P],
                                       WbI[:, g].rearrange("p a b -> p (a b)"), ident)
                ins.then_inc(v["wbt"], 1)
                pe.wait_ge(s_took["act"], taken["u", l, ft][1])
                pe.wait_ge(v["wbt_sb"], 2 * f + 1)
                for j in range(SSM_T):
                    ins = pe.transpose(psT[0:SSM_C, j // 4, (j % 4) * P:(j % 4 + 1) * P], uT[:, ft, j::SSM_T], ident)
                ins.then_inc(v["u2"], 1)
                pe.wait_ge(v["u2_sb"], f + 1)
                for g in range(SSM_G):
                    ins = pe.transpose(psO[:, g * SSM_C:(g + 1) * SSM_C], U2[:, g],
                                       ident[0:SSM_C, 0:SSM_C])
                ins.then_inc(v["ug"], 1)
                pe.wait_ge(v["ug_sb"], f + 1)
                pe.wait_ge(v["wbt_sb"], 2 * f + 2)
                for g in range(SSM_G):
                    pe.matmul(psS[:, 0, g * SSM_C:(g + 1) * SSM_C], WT[:, g], UG[:, g], start=True, stop=True)
                    ins = pe.matmul(psS[:, 1, g * SSM_C:(g + 1) * SSM_C], WTI[:, g], UG[:, g], start=True, stop=True)
                ins.then_inc(v["e"], 1)
                pe.wait_ge(v["z"], f + 1)
                pe.wait_ge(s_toep, 16 * SSM_T * (f + 1))
                for g in range(SSM_G):
                    o = psT[0:SSM_C, g // 4, (g % 4) * P:(g % 4 + 1) * P]
                    pe.matmul(o, UG[:, g], TO[:, g], start=True, stop=False)
                    pe.matmul(o, zb[1][:, g], W1[:, g, 1:SSM_T + 1, :], start=False, stop=False)
                    ins = pe.matmul(o, zb[2][:, g], W2[:, g], start=False, stop=True)
                ins.then_inc(v["yc"], 1)
                pe.wait_ge(v["yc_sb"], f + 1)
                for j in range(SSM_T):
                    ins = pe.transpose(psO[:, j * SSM_C:(j + 1) * SSM_C], Y2[:, j],
                                       ident[0:SSM_C, 0:SSM_C])
                ins.then_inc(v["yt"], 1)

            def unit_scores(u):
                n, kind, b, j = u["n"], u["kind"], u["b"], u["j"]
                if n >= 2:
                    pe.wait_ge(s_masked, n - 1)
                out = score_banks(u)
                for a in range(2):
                    h = slice(64 * a, 64 * a + 64)
                    q = slice(b * P, (b + 1) * P)
                    k = slice(u["k0"], u["k0"] + u["W"])
                    if kind == "sw":
                        lhs, rhs = qT1[h, j, q], kT1[h, k]
                    elif kind == "dsa":
                        lhs, rhs = qd[h, j, q], kd[h, k]
                    elif kind == "x":
                        lhs, rhs = qx[:, 2 * j + a, q], kx[:, 2 * j + a, :]
                    else:
                        lhs, rhs = qn[h, j, q], {"cmp": kc[h, :], "slc": ks[h, k], "win": kw[h, k]}[kind]
                    ins = pe.matmul(out[:, a], lhs, rhs, start=True, stop=True)
                ins.then_inc(s_sc, 1)

            def unit_transpose(u):
                n = u["n"]
                pe.wait_ge(s_prob, n + 1)
                before = n - 1 if narrow(u) else n
                if before > 0:
                    pe.wait_ge(s_pt, before)
                p, _ = probs(u)
                out = transpose_banks(u)
                for a in range(2):
                    for i, m in key_blocks(u):
                        ins = pe.transpose(out[0:m, a, i * P:(i + 1) * P], p[:, a, i * P:i * P + m], ident)
                ins.then_inc(s_tr, 1)

            def unit_pv(u):
                n, kind, b, j = u["n"], u["kind"], u["b"], u["j"]
                pe.wait_ge(s_pt, n + 1)
                if u["first"] and u["group"]:
                    pe.wait_ge(s_oe, u["group"])
                _, t = probs(u)
                for a in range(2):
                    h = slice(64 * a, 64 * a + 64)
                    blocks = key_blocks(u)
                    for i, m in blocks:
                        kb = u["k0"] // P + i
                        if kind == "x":
                            o, lhs = psO[:, a * P:(a + 1) * P], vx[:, i, (2 * j + a) * P:(2 * j + a + 1) * P]
                        else:
                            o = psO[h, 0:P]
                            lhs = {"sw": lambda: vt1[:, kb, h], "dsa": lambda: vd[:, kb, :], "cmp": lambda: vc[0:m, h],
                                   "slc": lambda: vs[:, kb, h], "win": lambda: vw[:, kb, h]}[kind]()
                        ins = pe.matmul(o, lhs, t[0:m, a, i, :], start=(u["first"] and i == 0),
                                        stop=(u["last"] and i == blocks[-1][0]))
                ins.then_inc(s_pv, 1)

            def indexer_head(b, h):
                n = (b - 1) * 8 + h
                W = (b + 1) * P
                hh = slice(64 * (h % 2), 64 * (h % 2) + 64)
                if n:
                    pe.wait_ge(s_ir, n)
                pe.matmul(psG[:, 2, 0:W], qi[hh, h // 2, b * P:(b + 1) * P], ki[hh, 0:W],
                          start=True, stop=True).then_inc(s_is, 1)

            def attention(us, side=None):
                la = ahead(us[0]) + 1
                for u in us[:la]:
                    unit_scores(u)
                for i, u in enumerate(us):
                    if i + la < len(us):
                        unit_scores(us[i + la])
                    if side:
                        side(i)
                    unit_transpose(u)
                    if i:
                        unit_pv(us[i - 1])
                unit_pv(us[-1])

            def rotate(r, which, src):
                pe.wait_ge(s_rawt, r + 1)
                if r:
                    pe.wait_ge(s_rope, r)
                pe.matmul(psS[:, 1, :], rots[which], src, start=True, stop=True).then_inc(s_rot, 1)

            def phase_of(p, phase):
                kind = p["kind"]
                N = CMP_N if kind == "cmpk" and phase != "cmp" else SEQ
                rt = cmpt[:, 0] if kind == "cmpk" else raws[p["i"] % 4][:, 0:N]
                sq = tmp[:, p.get("sq_at", 0), 0:N]
                if phase == "cmp":
                    i = 0 if kind == "cmpk" else 1
                    pe.wait_ge(s_p["cmpin"], i + 1)
                    pe.wait_ge(s_cw, 32)
                    if p["cen"] > 1:
                        pe.wait_ge(s_p["cen"], p["cen"] - 1)
                    for a in range(2):
                        h = slice(64 * a, 64 * a + 64)
                        for t in range(CMP_L):
                            ins = pe.matmul(psO[h, 0:CMP_N], cmpW[h, i, t, :], cmpin[h, t, :],
                                            start=(t == 0), stop=(t == CMP_L - 1))
                    ins.then_inc(s_p["cmpo"], 1)
                elif phase == "cmean":
                    pe.wait_ge(s_p["raw"], p["raw"])
                    pe.matmul(psT[:, 0, 0:N], blk, rt, start=True, stop=True).then_inc(s_p["cmean"], 1)
                elif phase == "mean":
                    if "sqa" in p:
                        pe.wait_ge(s_p["sqa"], p["sqa"])
                    else:
                        pe.wait_ge(s_p["sqd"], p["sqd"])
                    if p["sd"] > 1:
                        pe.wait_ge(s_p["sd"], p["sd"] - 1)
                    if kind == "lat2":
                        pe.matmul(psT[:, 1, 0:N], ones, tmp[:, posts[p["i"] - 1]["sq_at"], 0:N], start=True, stop=False)
                        pe.matmul(psT[:, 1, 0:N], ones, sq, start=False, stop=True).then_inc(s_p["mean"], 1)
                    else:
                        m = ones if kind in ("lat1", "xrms") else blk
                        pe.matmul(psT[:, 1, 0:N], m, sq, start=True, stop=True).then_inc(s_p["mean"], 1)
                elif phase == "rot":
                    if "qn" in p:
                        pe.wait_ge(s_p["qn"], p["qn"])
                    else:
                        pe.wait_ge(s_p["raw"], p["raw"])
                    if p["rotd"] > 1:
                        pe.wait_ge(s_p["rotd"], p["rotd"] - 1)
                    pe.matmul(psS[:, 1, 0:N], rots[2], rt, start=True, stop=True).then_inc(s_p["rot"], 1)
                elif phase == "tok":
                    if kind == "cmpv":
                        pe.wait_ge(s_p["cen"], p["cen"])
                    else:
                        pe.wait_ge(s_p["raw"], p["raw"])
                    if p["toksb"] > 1:
                        pe.wait_ge(s_p["toksb"], p["toksb"] - 1)
                    if kind == "cmpv":
                        ins = pe.transpose(psS[0:CMP_N, 0, 0:P], cmpt[:, 1], ident)
                    else:
                        for i in range(NB):
                            ins = pe.transpose(psS[:, 0, i * P:(i + 1) * P], rt[:, i * P:(i + 1) * P], ident)
                    ins.then_inc(s_p["tok"], 1)

            def project(ps):
                for new, old in waves(ps):
                    if new:
                        product(new["key"])
                    for p, phase in old:
                        phase_of(p, phase)

            def memory_keys_mean(j):
                pe.wait_ge(s_kxsq, j + 1)
                if j:
                    pe.wait_ge(s_kxsd, j)
                pe.matmul(psT[:, 0, 0:MEM], ones, xsq[:, j % 2], start=True,
                          stop=True).then_inc(s_kxms, 1)

            def memory_values_transpose(j):
                pe.wait_ge(s_xtr_in, j + 1)
                if j:
                    pe.wait_ge(s_vx, j)
                for i in range(2):
                    ins = pe.transpose(psT[:, 1, i * P:(i + 1) * P],
                                       xraw[:, j % 2, i * P:(i + 1) * P], ident)
                ins.then_inc(s_xtr, 1)

            pe.wait_ge(s_in, 48)
            for l in range(DEPTH):
                mean_square(f"mix{l}")
                for i in range(4):
                    product(("u", l, i))
                for ft in range(4):
                    ssm(l, ft)
                for i in range(4):
                    product(("glu", l, i))
                for i in range(4):
                    product(("q", l, i))
                    if i:
                        rotate(l * 5 + i - 1, 1, rawt[:, (l * 5 + i - 1) % 2, :])
                product(("k", l, 0))
                rotate(l * 5 + 3, 1, rawt[:, (l * 5 + 3) % 2, :])
                product(("v", l, 0))
                rotate(l * 5 + 4, 1, rawt[:, (l * 5 + 4) % 2, :])
                pe.wait_ge(s_vraw, l + 1)
                for b in range(NB):
                    ins = pe.transpose(psT[:, 0, b * P:(b + 1) * P], tmp[:, 2, b * P:(b + 1) * P], ident)
                ins.then_inc(s_vt, 1)
                pe.wait_ge(s_vtok, l + 1)
                pe.wait_ge(s_rope, 5 * (l + 1))
                attention(units[f"sw{l}"])
                for i in range(4):
                    for kind in ("cc", "cx", "cb"):
                        product((kind, l, i))
                for i in range(KD):
                    for kind in ("g0", "ao", "g1", "co", "g2", "so"):
                        product((kind, l, i))
                for i in range(KD):
                    product(("mix", l, i))
                mean_square(f"ffn{l}")
                for c, (t0, nt) in enumerate(FFN_CHUNKS):
                    if l == DEPTH - 1 and c == 1:
                        mean_square("mem", MEM)
                    for t in range(t0, t0 + nt):
                        product(("gt", l, t))
                        product(("up", l, t))
                    for i in range(KD):
                        product(("fo", l, c, i))
            product(("xk", 0))
            mean_square("final")
            for j in range(1, XHEADS):
                product(("xk", j))
                memory_keys_mean(j - 1)
            product(("xv", 0))
            memory_keys_mean(XHEADS - 1)
            for j in range(1, XHEADS):
                product(("xv", j))
                memory_values_transpose(j - 1)
            memory_values_transpose(XHEADS - 1)
            mean_square("norm1")
            project(block2_posts)
            pe.wait_ge(s_p["out"], block2_done["out"])
            pe.wait_ge(s_p["toksb"], block2_done["toksb"])
            attention(units2, lambda i: indexer_head(i // 16 + 1, i % 16) if i // 16 < NB - 1 and i % 16 < 8 else None)
            for i in range(KD):
                product(("out2", i))
            mean_square("norm2")
            project(x_posts)
            pe.wait_ge(s_p["out"], all_done["out"])
            pe.wait_ge(s_kxn, 1)
            attention(units["x"])
            for i in range(KD):
                product(("xo", i))
            mean_square("norm3")
            for c, (t0, nt) in enumerate(FF2_CHUNKS):
                for t in range(t0, t0 + nt):
                    product(("fi", t))
                for i in range(KD):
                    product(("fo2", c, i))

        @block.scalar
        def _(act):
            line = Line(act, c_act)
            do = line.done
            act.dma_start(CON[:, :], consts).then_inc(s_in, 16)
            act.dma_start(PAR[:, :], params).then_inc(s_in, 16)
            act.dma_start(X[:, :, :], xT).then_inc(s_in, 16)
            act.wait_ge(s_in, 48)

            def from_bank(key):
                n = number[key]
                act.wait_ge(s_job, n + 1)
                return psG[:, n % GEMM_BANKS, 0:jobs[n][2]]

            def root(name, cols=SEQ):
                act.wait_ge(s_ms, NORMS[name] + 1)
                do(act.activation(rinv[:, 0:cols], psO[:, 0:cols], ACT.Sqrt, bias=eps), s_sd)

            def high_parts(name):
                for k in range(KD):
                    n = KD * h_norm[name] + k + 1
                    act.wait_ge(s_xs, n)
                    act.activation(Hh[:, k], tmp[:, k % 3, :], ACT.Copy).then_inc(s_hh, 1)

            def ssm(l, ft):
                f = l * 4 + ft
                s = sp[f % 2]
                act.wait_ge(s_ssmp[f % 2], 16 * (f // 2 + 1))
                if f:
                    act.wait_ge(v["w12"], f)
                do(act.activation(sm[:, 0], s[:, 2 * SSM_G:3 * SSM_G], ACT.Exp), v["y1"])
                act.wait_ge(v["args"], 2 * f + 1)
                do(act.activation(mag, mag, ACT.Exp), v["sincos"])
                act.wait_ge(v["args"], 2 * f + 2)
                do(act.activation(sn, arg, ACT.Sin))
                do(act.activation(cs, arg2, ACT.Sin), v["sincos"])
                if f:
                    act.wait_ge(s_toep, 16 * SSM_T * f)
                act.wait_ge(v["g_out"], f + 1)
                for i in range(2):
                    ins = act.activation(Gp[:, 4 * i:4 * i + 4, 7 * SSM_H:],
                                         psS[0:SSM_H, i, :].rearrange("p (g x) -> p g x", g=4), ACT.Copy)
                    do(ins) if i == 0 else do(ins, v["g_pad"])
                if f:
                    act.wait_ge(v["yc"], f)
                for j in range(SSM_T):
                    act.dma_start(TO[j * SSM_H:(j + 1) * SSM_H, :, :],
                                  Gp[:, :, (7 - j) * SSM_H:(7 - j) * SSM_H + P]).then_inc(s_toep, 16)
                for k, (dst, src) in enumerate(((WT, psT), (WTI, psS))):
                    act.wait_ge(v["wbt"], 2 * f + k + 1)
                    do(act.activation(dst[:, 0:4].rearrange("p a b -> p (a b)"), src[:, 0, :], ACT.Copy))
                    do(act.activation(dst[:, 4:8].rearrange("p a b -> p (a b)"), src[:, 1, :], ACT.Copy), v["wbt_sb"])
                act.wait_ge(v["u2"], f + 1)
                by_position = U2.rearrange("c g (j h) -> c j g h", h=SSM_H)
                for i, s_i in ((0, None), (1, v["u2_sb"])):
                    do(act.activation(by_position[:, 4 * i:4 * i + 4],
                                      psT[0:SSM_C, i, :].rearrange("c (j g h) -> c j g h", g=SSM_G, h=SSM_H), ACT.Copy), s_i)
                act.wait_ge(v["ug"], f + 1)
                do(act.activation(UG[:, :, :].rearrange("p a b -> p (a b)"), psO[:, :], ACT.Copy), v["ug_sb"])
                act.wait_ge(v["yc"], f + 1)
                by_group = Y2.rearrange("c j (g h) -> c g j h", h=SSM_H)
                for i, s_i in ((0, None), (1, v["yc_sb"])):
                    do(act.activation(by_group[:, 4 * i:4 * i + 4],
                                      psT[0:SSM_C, i, :].rearrange("c (g j h) -> c g j h", j=SSM_T, h=SSM_H), ACT.Copy), s_i)
                act.wait_ge(v["ypre"], f + 1)
                do(act.activation(ysf[:, ft], ysf[:, ft], ACT.Gelu_apprx_tanh), v["ys"])
                if ft < 2:
                    act.dma_start(s, ssmp[f + 2]).then_inc(s_ssmp[f % 2], 16)

            def unit_exp(u):
                n, kind = u["n"], u["kind"]
                st = stats(u)
                p, _ = probs(u)
                act.wait_ge(s_neg, n + 1)
                scale = {"sw": 1.0, "x": P ** -0.5}.get(kind, HEAD ** -0.5)
                do(act.activation(p[:, 0], p[:, 0], ACT.Exp, bias=st[:, 2:3], scale=scale, accum_out=st[:, 4:5]))
                ins = act.activation(p[:, 1], p[:, 1], ACT.Exp, bias=st[:, 3:4], scale=scale, accum_out=st[:, 5:6])
                if kind == "sw":
                    do(ins)
                    ins = act.activation(st[:, 6:8], st[:, 6:8], ACT.Exp)
                do(ins, s_exp)

            def unit_copy(u):
                n = u["n"]
                act.wait_ge(s_tr, n + 1)
                if n >= 2:
                    act.wait_ge(s_pv, n - 1)
                _, t = probs(u)
                m, w = (CMP_N, 1) if u["kind"] == "cmp" else (P, u["W"] // P)
                src = transpose_banks(u)[0:m, :, 0:w * P].rearrange("p a (b c) -> p a b c", c=P)
                do(act.activation(t[0:m, 0, 0:w, :], src[:, 0], ACT.Copy))
                do(act.activation(t[0:m, 1, 0:w, :], src[:, 1], ACT.Copy), s_pt)

            def indexer_head(b, h):
                n = (b - 1) * 8 + h
                W = (b + 1) * P
                act.wait_ge(s_is, n + 1)
                if n >= 2:
                    act.wait_ge(s_ia, n - 1)
                do(act.activation(irelu[:, h % 2, 0:W], psG[:, 2, 0:W], ACT.Relu), s_ir)

            def attention(us, side=None):
                la = ahead(us[0])
                for u in us[:la]:
                    unit_exp(u)
                for i, u in enumerate(us):
                    if side:
                        side(i)
                    unit_copy(u)
                    if i + la < len(us):
                        unit_exp(us[i + la])

            def take(p):
                bank = from_bank(p["key"])
                rt = raws[p["i"] % 4]
                if p["i"] >= 4:
                    prev = posts[p["i"] - 4]
                    if prev["kind"] == "lat":
                        prev = posts[p["i"] - 3]
                    for n in ("out", "toksb", "cmpin"):
                        if n in prev:
                            act.wait_ge(s_p[n], prev[n])
                if "sqa" in p:
                    do(act.activation(rt, bank, ACT.Copy), s_p["raw"])
                    if p["sq_wait"]:
                        act.wait_ge(s_p["mean"], p["sq_wait"]["mean"])
                    do(act.activation(tmp[:, p["sq_at"], :], bank, ACT.Square), s_took["act"])
                    act.sem_inc(s_p["sqa"], 1)
                else:
                    do(act.activation(rt, bank, ACT.Copy), s_took["act"])
                    act.sem_inc(s_p["raw"], 1)

            def phase_of(p, phase):
                kind = p["kind"]
                N = CMP_N if kind == "cmpk" else SEQ
                if phase == "mean":
                    act.wait_ge(s_p["mean"], p["mean"])
                    if p["sd"] > 2:
                        q = next(q for q in posts if q.get("sd") == p["sd"] - 2)
                        act.wait_ge(s_p["qn" if "qn" in q else "out"], q["qn" if "qn" in q else "out"])
                    scale = {"lat2": 4.0, "lat1": 8.0, "xrms": 8.0}.get(kind, 1.0)
                    do(act.activation(roots[p["sd"] % 2][:, 0:N], psT[:, 1, 0:N], ACT.Sqrt, bias=eps, scale=scale), s_p["sd"])
                elif phase == "tok":
                    act.wait_ge(s_p["tok"], p["tok"])
                    t = psS[:, 0, :].rearrange("p (b c) -> p b c", c=P)
                    if kind == "tok":
                        do(act.activation(p["dest"], t, ACT.Copy), s_p["toksb"])
                    elif kind == "tokd":
                        do(act.activation(vd, t[:, :, HEAD:P], ACT.Copy), s_p["toksb"])
                    elif kind == "tokwg":
                        do(act.activation(wtok[:, :, :], t[:, :, 0:8], ACT.Copy, scale=IDX_SCALE))
                        do(act.activation(gtok[:, :, :], t[:, :, 104:128], ACT.Sigmoid), s_p["toksb"])
                    elif kind == "cmpv":
                        do(act.activation(vc[0:CMP_N, :], psS[0:CMP_N, 0, 0:P], ACT.Copy), s_p["toksb"])

            def project(ps):
                for new, old in waves(ps):
                    if new:
                        take(new)
                    for p, phase in old:
                        phase_of(p, phase)

            def memory_keys_take(j):
                bank = from_bank(("xk", j))
                do(act.activation(kx[:, j], bank, ACT.Copy), s_kx)
                if j >= 2:
                    act.wait_ge(s_kxms, j - 1)
                do(act.activation(xsq[:, j % 2], bank, ACT.Square), s_took["act"])
                act.sem_inc(s_kxsq, 1)

            def memory_keys_root(j):
                act.wait_ge(s_kxms, j + 1)
                do(act.activation(xsd[:, j], psT[:, 0, 0:MEM], ACT.Sqrt, bias=eps, scale=8.0), s_kxsd)

            def memory_values_take(j):
                bank = from_bank(("xv", j))
                if j >= 2:
                    act.wait_ge(s_xtr, j - 1)
                do(act.activation(xraw[:, j % 2], bank, ACT.Copy), s_took["act"])
                act.sem_inc(s_xtr_in, 1)

            def memory_values_copy(j):
                act.wait_ge(s_xtr, j + 1)
                src = psT[:, 1, 0:MEM].rearrange("p (b c) -> p b c", c=P)
                do(act.activation(vx[:, :, j * P:(j + 1) * P], src, ACT.Copy), s_vx)

            for l in range(DEPTH):
                for i in range(2):
                    act.dma_start(sp[i], ssmp[4 * l + i]).then_inc(s_ssmp[i], 16)
                root(f"mix{l}")
                high_parts(f"mix{l}")
                for i in range(4):
                    do(act.activation(uT[:, i], from_bank(("u", l, i)), ACT.Copy), s_took["act"])
                for ft in range(4):
                    ssm(l, ft)
                for i in range(4):
                    bank = from_bank(("glu", l, i))
                    act.wait_ge(v["glu_out"], 4 * l + i) if 4 * l + i else None
                    do(act.activation(tmp[:, 0, :], bank, ACT.Sigmoid), s_took["act"])
                for i in range(4):
                    r = l * 5 + i
                    bank = from_bank(("q", l, i))
                    if r >= 2:
                        act.wait_ge(s_rope, r - 1)
                    do(act.activation(rawt[:, r % 2, :], bank, ACT.Copy, scale=HEAD ** -0.5), s_took["act"])
                    act.sem_inc(s_rawt, 1)
                r = l * 5 + 4
                bank = from_bank(("k", l, 0))
                act.wait_ge(s_rope, r - 1)
                do(act.activation(rawt[:, r % 2, :], bank, ACT.Copy), s_took["act"])
                act.sem_inc(s_rawt, 1)
                bank = from_bank(("v", l, 0))
                act.wait_ge(s_rope, r)
                do(act.activation(tmp[:, 2, :], bank, ACT.Copy), s_took["act"])
                act.sem_inc(s_vraw, 1)
                act.wait_ge(s_vt, l + 1)
                do(act.activation(vt1[:, :, :].rearrange("p a b -> p (a b)"), psT[:, 0, :], ACT.Copy), s_vtok)
                attention(units[f"sw{l}"])
                for i in range(4):
                    bank = from_bank(("cc", l, i))
                    act.wait_ge(s_cy, 4 * l + i) if 4 * l + i else None
                    do(act.activation(tmp[:, 0, :], bank, ACT.Copy), s_took["act"])
                for i in range(KD):
                    for br, g in enumerate(("g0", "g1", "g2")):
                        bank = from_bank((g, l, i))
                        n = 24 * l + 3 * i + br
                        if n >= 2:
                            act.wait_ge(s_sig, n - 1)
                        do(act.activation(rawt[:, n % 2, :], bank, ACT.Sigmoid, bias=par(("b_gate", l), br * KD + i)),
                           s_took["act"])
                root(f"ffn{l}")
                high_parts(f"ffn{l}")
                if l == DEPTH - 1:
                    act.dma_start(memf, memT).then_inc(s_mem, 16)
                for t in range(FFN_TILES):
                    if l == DEPTH - 1 and t == FFN_CHUNKS[1][0]:
                        root("mem", MEM)
                    bank = from_bank(("gt", l, t))
                    n = FFN_TILES * l + t
                    if n >= 2:
                        act.wait_ge(s_hid, n - 1)
                    do(act.activation(rawt[:, n % 2, :], bank, ACT.Silu), s_took["act"])
            memory_keys_take(0)
            root("final")
            for j in range(1, XHEADS):
                memory_keys_take(j)
                memory_keys_root(j - 1)
            memory_values_take(0)
            memory_keys_root(XHEADS - 1)
            for j in range(1, XHEADS):
                memory_values_take(j)
                memory_values_copy(j - 1)
            memory_values_copy(XHEADS - 1)
            root("norm1")
            high_parts("norm1")
            for i in range(2):
                act.dma_start(cmpW[:, i].rearrange("p a b -> p (a b)"), cmpw[i]).then_inc(s_cw, 16)
            project(block2_posts)
            attention(units2, lambda i: indexer_head(i // 16 + 1, i % 16) if i // 16 < NB - 1 and i % 16 < 8 else None)
            root("norm2")
            high_parts("norm2")
            project(x_posts)
            attention(units["x"])
            root("norm3")
            high_parts("norm3")
            for t in range(32):
                bank = from_bank(("fi", t))
                n = FFN_TILES * DEPTH + t
                act.wait_ge(s_hid, n - 1)
                do(act.activation(rawt[:, n % 2, :], bank, ACT.Relu), s_took["act"])

        @block.vector
        def _(dve):
            line = Line(dve, c_dve)
            do = line.done

            def from_bank(key):
                n = number[key]
                dve.wait_ge(s_job, n + 1)
                return psG[:, n % GEMM_BANKS, 0:jobs[n][2]]

            def tt(out, a, b, op, s=None):
                do(dve.tensor_tensor(out, a, b, op), s)

            def stt(out, a, s_, b, op0, op1, s=None):
                do(dve.scalar_tensor_tensor(out, a, s_, b, op0, op1), s)

            def ts(out, a, s1, s2, op0, op1=None, s=None):
                do(dve.tensor_scalar(out, a, s1, s2, op0, op1) if op1 is not None
                   else dve.tensor_scalar(out, a, s1, None, op0), s)

            def split(hi, lo, src, s):
                do(dve.tensor_copy(hi, src))
                tt(lo, src, hi.bitcast(F32), ALU.subtract, s)

            def add_square(k, src, n=SEQ):
                if k == 0:
                    tt(acc[:, 0:n], src, src, ALU.mult)
                else:
                    tt(tmp[:, 0, 0:n], src, src, ALU.mult)
                    tt(acc[:, 0:n], acc[:, 0:n], tmp[:, 0, 0:n], ALU.add, s_ssq if k == KD - 1 else None)

            def normalise(name, gain):
                dve.wait_ge(s_sd, NORMS[name] + 1)
                do(dve.reciprocal(rinv[:, :], rinv[:, :]))
                if name == "final":
                    for k in range(KD):
                        dve.scalar_tensor_tensor(X[:, k], X[:, k], par(gain, k), rinv[:, :], ALU.mult, ALU.mult).then_inc(s_fin, 1)
                    return
                base = h_norm[name]

                def low_part(k):
                    dve.wait_ge(s_hh, KD * base + k + 1)
                    dve.tensor_tensor(Hl[:, k], tmp[:, k % 3, :], Hh[:, k].bitcast(F32), ALU.subtract).then_inc(s_h, 1)

                for k in range(KD):
                    if k >= 3:
                        dve.wait_ge(*((s_h, KD // 2 * base + (k - 3) // 2 + 1) if k % 2 else
                                      (s_hp, KD // 2 * base + (k - 3) // 2 + 1)))
                    dve.scalar_tensor_tensor(tmp[:, k % 3, :], X[:, k], par(gain, k), rinv[:, :],
                                             ALU.mult, ALU.mult).then_inc(s_xs, 1)
                    if k % 2:
                        low_part(k - 1)
                dve.wait_ge(s_h, KD // 2 * (base + 1))
                dve.wait_ge(s_hp, KD // 2 * (base + 1))
                dve.wait_ge(s_xs, KD * (base + 1))

            def memory_norm():
                dve.wait_ge(s_mem, 16)
                for k in range(KD):
                    add_square(k, memf[:, k], MEM)

            def memory_normalise():
                dve.wait_ge(s_sd, NORMS["mem"] + 1)
                do(dve.reciprocal(rinv[:, 0:MEM], rinv[:, 0:MEM]))
                for k in range(KD):
                    t = tmp[:, 1, 0:MEM]
                    stt(t, memf[:, k], par("mem_norm", k), rinv[:, 0:MEM], ALU.mult, ALU.mult)
                    split(mH[:, k], mL[:, k], t, s_m)

            def residual(key, i, square):
                bank = from_bank(key)
                tt(X[:, i], X[:, i], bank, ALU.add, s_took["dve"])
                if square:
                    add_square(i, X[:, i])

            def reduce_angle(a):
                big = 1.5 * 2.0 ** 23
                ts(red, a, 1.0 / (2 * math.pi), big, ALU.mult, ALU.add)
                ts(red, red, big, None, ALU.subtract)
                for c in (6.28125, 1.93500518798828125e-3, 3.01991598195675286e-7):
                    stt(a, red, -c, a, ALU.mult, ALU.add)
                ts(a, a, 3.1415925, -3.1415925, ALU.min, ALU.max)

            def reduce_small(a):
                big = 1.5 * 2.0 ** 23
                t = sm[:, 15]
                ts(t, a, 1.0 / (2 * math.pi), big, ALU.mult, ALU.add)
                ts(t, t, big, None, ALU.subtract)
                for c in (6.28125, 1.93500518798828125e-3, 3.01991598195675286e-7):
                    stt(a, t, -c, a, ALU.mult, ALU.add)

            def ssm(l, ft):
                f = l * 4 + ft
                s = sp[f % 2]
                G = SSM_G
                are, aim = s[:, 0:G], s[:, G:2 * G]
                o = 3 * G
                gh = G * SSM_H
                y1, y2, c1, c2 = (s[:, o + gh * i:o + gh * (i + 1)].rearrange("p (g h) -> p g h", g=G) for i in range(4))
                J = con("J", 9)
                dve.wait_ge(s_ssmp[f % 2], 16 * (f // 2 + 1))
                dve.wait_ge(v["y1"], f + 1)
                dt, ar, th, t8, t64, inv, cr, ci, ta, tb = (sm[:, i] for i in range(10))
                tt(ar, are, dt, ALU.mult)
                tt(th, aim, dt, ALU.mult)
                tt(mag, ar.unsqueeze(2).to_broadcast([P, G, 9]), J.unsqueeze(1).to_broadcast([P, G, 9]), ALU.mult, v["args"])
                reduce_small(th)
                ts(t8, th, 8.0, None, ALU.mult)
                reduce_small(t8)
                ts(t64, t8, 8.0, None, ALU.mult)
                reduce_small(t64)
                for a, n, c in ((th, 9, 0), (t8, 8, 9), (t64, 8, 17)):
                    tt(arg[:, :, c:c + n], a.unsqueeze(2).to_broadcast([P, G, n]),
                       J[:, 0:n].unsqueeze(1).to_broadcast([P, G, n]), ALU.mult)
                reduce_angle(arg)
                ts(arg2, arg, math.pi / 2, None, ALU.add)
                reduce_angle(arg2)
                ts(Y1n, y2, con("sgn", 1), -1.0, ALU.mult, ALU.mult)
                ts(Z1, c1, con("sgn", 1), None, ALU.mult)
                ts(Z2, c2, -1.0, None, ALU.mult, None, v["args"])
                dve.wait_ge(v["sincos"], 2 * f + 2)
                tt(Lr, mag, cs[:, :, 0:9], ALU.mult)
                tt(Li, mag, sn[:, :, 0:9], ALU.mult)
                tt(ta, are, are, ALU.mult)
                tt(tb, aim, aim, ALU.mult)
                tt(ta, ta, tb, ALU.add)
                do(dve.reciprocal(inv, ta))
                nr, ni = sm[:, 10], Li[:, :, 1]
                ts(nr, Lr[:, :, 1], -1.0, None, ALU.add)
                tt(cr, nr, are, ALU.mult)
                tt(ta, ni, aim, ALU.mult)
                tt(cr, cr, ta, ALU.add)
                tt(cr, cr, inv, ALU.mult)
                tt(ci, ni, are, ALU.mult)
                tt(ta, nr, aim, ALU.mult)
                tt(ci, ci, ta, ALU.subtract)
                tt(ci, ci, inv, ALU.mult)
                bc = lambda a, n: a.unsqueeze(2).to_broadcast([P, G, n])
                rev = lambda a: a[:, :, 7::-1]
                t3 = work(TS, 1856, [P, G, 8])
                tt(Lcr, rev(Lr), bc(cr, 8), ALU.mult)
                tt(t3, rev(Li), bc(ci, 8), ALU.mult)
                tt(Lcr, Lcr, t3, ALU.subtract)
                tt(Lci, rev(Lr), bc(ci, 8), ALU.mult)
                tt(t3, rev(Li), bc(cr, 8), ALU.mult)
                tt(Lci, Lci, t3, ALU.add)
                t4 = work(TS, 1920, [P, G, SSM_H])
                tt(X1, y1, bc(cr, SSM_H), ALU.mult)
                tt(t4, Y1n, bc(ci, SSM_H), ALU.mult)
                tt(X1, X1, t4, ALU.add)
                jh = lambda a, n: a.unsqueeze(3).to_broadcast([P, G, n, SSM_H])
                hj = lambda a, n: a.unsqueeze(2).to_broadcast([P, G, n, SSM_H])
                pw = lambda n: pwork[:, 0:G * n * SSM_H].rearrange("p (g j h) -> p g j h", g=G, j=n)
                if f:
                    dve.wait_ge(v["yc"], f)
                tt(W1, jh(Lr, 9), hj(Z1, 9), ALU.mult)
                tt(pw(9), jh(Li, 9), hj(Z2, 9), ALU.mult)
                tt(W1, W1, pw(9), ALU.add)
                tt(W2, jh(Lr[:, :, 1:9], 8), hj(Z2, 8), ALU.mult)
                tt(pw(8), jh(Li[:, :, 1:9], 8), hj(Z1, 8), ALU.mult)
                tt(W2, W2, pw(8), ALU.subtract, v["w12"])
                tt(WbE, jh(Lcr, 8), hj(y1, 8), ALU.mult)
                tt(pw(8), jh(Lci, 8), hj(Y1n, 8), ALU.mult)
                tt(WbE, WbE, pw(8), ALU.add)
                tt(WbI, jh(Lci, 8), hj(y1, 8), ALU.mult)
                tt(pw(8), jh(Lcr, 8), hj(Y1n, 8), ALU.mult)
                tt(WbI, WbI, pw(8), ALU.subtract, v["wb"])
                ab = lambda a: a.rearrange("p g (a b) -> p g a b", b=8)
                ea = lambda a: a[:, :, 17:25].unsqueeze(3).to_broadcast([P, G, 8, 8])
                eb = lambda a: a[:, :, 9:17].unsqueeze(2).to_broadcast([P, G, 8, 8])
                pt = pwork[:, 0:G * 64].rearrange("p (g a b) -> p g a b", g=G, a=8)
                tt(ab(rotC), ea(cs), eb(cs), ALU.mult)
                tt(pt, ea(sn), eb(sn), ALU.mult)
                tt(ab(rotC), ab(rotC), pt, ALU.subtract)
                tt(ab(rotS), ea(sn), eb(cs), ALU.mult)
                tt(pt, ea(cs), eb(sn), ALU.mult)
                tt(ab(rotS), ab(rotS), pt, ALU.add)
                do(dve.tensor_copy(acoef, mag[:, :, 8:9].to_broadcast([P, G, SSM_C])))
                do(dve.memset(acoef[:, :, 0:1], 0.0))
                if f == 0:
                    do(dve.memset(zb[1][:, :, 0:1], 0.0))
                    do(dve.memset(zb[2][:, :, 0:1], 0.0))
                dve.wait_ge(v["e"], f + 1)
                e0 = psS[:, 0, :].rearrange("p (g c) -> p g c", g=G)
                e1 = psS[:, 1, :].rearrange("p (g c) -> p g c", g=G)
                zt = pwork[:, 0:512].rearrange("p (g c) -> p g c", g=G)
                tt(zb[0], e0, rotC, ALU.mult)
                tt(zt, e1, rotS, ALU.mult)
                tt(zb[0], zb[0], zt, ALU.add)
                fl = lambda a: a.rearrange("p g c -> p (g c)")
                do(dve.tensor_tensor_scan(fl(zt), fl(acoef), fl(zb[0]), 0.0, ALU.mult, ALU.add))
                tt(zb[1][:, :, 1:], zt[:, :, :-1], rotC[:, :, :-1], ALU.mult)
                tt(zb[2][:, :, 1:], zt[:, :, :-1], rotS[:, :, :-1], ALU.mult, v["z"])
                dve.wait_ge(v["yt"], f + 1)
                stt(ysf[:, ft].rearrange("p (c j) -> p c j", j=SSM_T), uT[:, ft].rearrange("p (c j) -> p c j", j=SSM_T),
                    par(("ssm_d", l), ft), psO[:, :].rearrange("p (j c) -> p c j", j=SSM_T), ALU.mult, ALU.add, v["ypre"])

            def unit_max(u):
                n, kind, b, W = u["n"], u["kind"], u["b"], u["W"]
                st = stats(u)
                p, _ = probs(u)
                dve.wait_ge(s_sc, n + 1)
                ring = ahead(u) + 1
                if n >= ring:
                    dve.wait_ge(s_tr, n - ring + 1)
                src = score_banks(u)
                if kind == "sw":
                    mask = con("sw", 2 * P)[:, 2 * P - W:]
                elif kind == "dsa":
                    mask = selm[:, 0:W]
                elif kind == "cmp":
                    mask = con("cmp_add", NB * CMP_N)[:, b * CMP_N:(b + 1) * CMP_N]
                else:
                    mask = con("mk", SEQ)[:, SEQ - W:]
                if kind == "x":
                    do(dve.tensor_copy(p, src), s_masked)
                else:
                    tt(p, src, mask.unsqueeze(1).to_broadcast([P, 2, W]), ALU.add, s_masked)
                do(dve.tensor_reduce(st[:, 0:2], p, AX_X, ALU.max))
                scale = {"sw": 1.0, "x": P ** -0.5}.get(kind, HEAD ** -0.5)
                if kind == "sw":
                    snk = par(("sinks", u["l"]), 0, 8)[:, u["j"]::4]
                    tt(st[:, 0:2], st[:, 0:2], snk, ALU.max)
                    tt(st[:, 6:8], snk, st[:, 0:2], ALU.subtract)
                ts(st[:, 2:4], st[:, 0:2], -scale, None, ALU.mult, None, s_neg)

            def unit_scale(u):
                n, kind, b, j = u["n"], u["kind"], u["b"], u["j"]
                st = stats(u)
                p, _ = probs(u)
                dve.wait_ge(s_exp, n + 1)
                den = st[:, 4:6]
                if kind == "sw":
                    tt(den, den, st[:, 6:8], ALU.add)
                if kind == "cmp":
                    mul = con("cmp_mul", NB * CMP_N)[:, b * CMP_N:(b + 1) * CMP_N]
                    tt(p, p, mul.unsqueeze(1).to_broadcast([P, 2, CMP_N]), ALU.mult)
                    do(dve.tensor_reduce(den, p, AX_X, ALU.add))
                    ts(den, den, 1e-30, None, ALU.max)
                if kind in ("cmp", "slc", "win"):
                    do(dve.reciprocal(st[:, 8:10], den))
                    br = ("cmp", "slc", "win").index(kind)
                    tt(st[:, 8:10], st[:, 8:10], gtok[:, b, 3 * j + br::12], ALU.mult, s_norm)
                elif kind == "dsa":
                    do(dve.reciprocal(st[:, 8:10], den), s_norm)
                else:
                    do(dve.reciprocal(st[:, 8:10], den))
                    ts(p[:, 0], p[:, 0], st[:, 8:9], None, ALU.mult)
                    ts(p[:, 1], p[:, 1], st[:, 9:10], None, ALU.mult, None, s_prob)

            def unit_out(u):
                if not u["last"]:
                    return
                kind, b, j = u["kind"], u["b"], u["j"]
                dve.wait_ge(s_pv, u["n"] + 1)
                q = slice(b * P, (b + 1) * P)
                if kind == "x":
                    for a in range(2):
                        o = psO[:, a * P:(a + 1) * P]
                        t = 2 * j + a
                        do(dve.tensor_copy(Hh[:, t, q], o))
                        tt(Hl[:, t, q], o, Hh[:, t, q].bitcast(F32), ALU.subtract, s_oe if a else None)
                    return
                hi, lo, t = {"sw": (Bh, Bl, j), "dsa": (Hh, Hl, j)}.get(kind, (Hh, Hl, 4 + j))
                do(dve.tensor_copy(hi[:, t, q], psO[:, 0:P]))
                tt(lo[:, t, q], psO[:, 0:P], hi[:, t, q].bitcast(F32), ALU.subtract, s_oe)

            def select(i):
                b, r = i // 16 + 1, i % 16
                if b >= NB:
                    return
                W = (b + 1) * P
                if r < 8:
                    dve.wait_ge(s_ir, (b - 1) * 8 + r + 1)
                    w = wtok[:, b, r:r + 1]
                    if r == 0:
                        ts(iacc[:, 0:W], irelu[:, 0, 0:W], w, None, ALU.mult, None, s_ia)
                    else:
                        stt(iacc[:, 0:W], irelu[:, r % 2, 0:W], w, iacc[:, 0:W], ALU.mult, ALU.add, s_ia)
                    return
                if r == 8:
                    tt(iwork[:, 0:W], iacc[:, 0:W], con("mk", SEQ)[:, SEQ - W:], ALU.add)
                for _ in range((3 if r < 10 else 2) if r < 15 else 0):
                    do(dve.max(m8[:, :], iwork[:, 0:W]))
                    do(dve.match_replace(iwork[:, 0:W], m8[:, :], iwork[:, 0:W], TAKEN))
                if r == 14:
                    ts(selm[:, 0:W], iwork[:, 0:W], TAKEN / 2, NEG, ALU.is_gt, ALU.mult)

            def attention(us, side=None):
                la = ahead(us[0])
                for u in us[:la]:
                    unit_max(u)
                for i, u in enumerate(us):
                    unit_scale(u)
                    if i >= 2:
                        unit_out(us[i - 2])
                    if side:
                        side(i)
                    if i + la < len(us):
                        unit_max(us[i + la])
                unit_out(us[-2])
                unit_out(us[-1])

            def phase_of(p, phase):
                kind = p["kind"]
                N = CMP_N if kind == "cmpk" else SEQ
                rt = cmpt[:, 0] if kind == "cmpk" else raws[p["i"] % 4]
                if phase in ("cmp", "cmean"):
                    if phase == "cmp":
                        dve.wait_ge(s_p["cmpo"], p["cmpo"])
                        do(dve.tensor_copy(cmpt[:, 0 if kind == "cmpk" else 1], psO[:, 0:CMP_N]), s_p["cen"])
                    else:
                        dve.wait_ge(s_p["cmean"], p["cmean"])
                        tt(rt, rt, psT[:, 0, 0:N], ALU.subtract, s_p["cen"])
                    if kind != "cmpv":
                        if p["sq_wait"]:
                            dve.wait_ge(s_p["mean"], p["sq_wait"]["mean"])
                        tt(tmp[:, p["sq_at"], 0:N], rt, rt, ALU.mult, s_p["sqd"])
                elif phase == "mean":
                    r = roots[p["sd"] % 2][:, 0:N]
                    dve.wait_ge(s_p["sd"], p["sd"])
                    do(dve.reciprocal(r, r))
                    if kind in ("lat1", "lat2"):
                        tiles = [(0, posts[p["i"] - 1]), (1, p)] if kind == "lat2" else [(2, p)]
                        for n, (i, q) in enumerate(tiles):
                            gain = par("cq", i) if kind == "lat2" else par("ckv")
                            stt(tmp[:, 2, :], raws[q["i"] % 4], gain, r, ALU.mult, ALU.mult)
                            split(Bh[:, 8 + i], Bl[:, 8 + i], tmp[:, 2, :], s_p["out"] if n == len(tiles) - 1 else None)
                    elif kind == "ln":
                        tt(rt, rt, r, ALU.mult)
                        ts(rt, rt, par("lng"), par("lnb"), ALU.mult, ALU.add, s_p["qn"])
                    elif kind == "xrms":
                        stt(p["dest"], rt, par(*p["gain"]), r, ALU.mult, ALU.mult, s_p["out"])
                    else:
                        stt(rt, rt, par(*p["gain"]), r, ALU.mult, ALU.mult, s_p["qn"])
                elif phase == "rot":
                    C, S = tabs[2]
                    if kind == "cmpk":
                        C, S = (a[:, CMP_L - 1::CMP_STRIDE] for a in (C, S))
                    dest = p["dest"]
                    dve.wait_ge(s_p["rot"], p["rot"])
                    tt(tmp[:, 2, 0:N], psS[:, 1, 0:N], S, ALU.mult, s_p["rotd"])
                    tt(dest, rt, C, ALU.mult)
                    tt(dest, dest, tmp[:, 2, 0:N], ALU.add, s_p["out"])

            def windows(p):
                i = 0 if p["kind"] == "cmpk" else 1
                dve.wait_ge(s_p["raw"], p["raw"])
                if i:
                    dve.wait_ge(s_p["cmpo"], i)
                for l0 in (0, CMP_STRIDE):
                    src = raws[p["i"] % 4][:, l0:l0 + CMP_STRIDE * CMP_N].rearrange("p (n l) -> p l n", l=CMP_STRIDE)
                    pe_ = par("pe", CMP_L * i + l0, CMP_STRIDE).unsqueeze(2).to_broadcast([P, CMP_STRIDE, CMP_N])
                    tt(cmpin[:, l0:l0 + CMP_STRIDE], src, pe_, ALU.add, s_p["cmpin"] if l0 else None)

            def project(ps):
                for new, old in waves(ps):
                    for p, phase in old:
                        phase_of(p, phase)
                    if new and new["kind"] in ("cmpk", "cmpv"):
                        windows(new)

            dve.wait_ge(s_in, 48)
            do(dve.memset(zc[:, 0:2], 0.0))
            for k in range(KD):
                add_square(k, X[:, k])
            for l in range(DEPTH):
                normalise(f"mix{l}", ("norm_mix", l))
                do(dve.memset(Gp[:, :, 0:7 * SSM_H], 0.0), v["consts_ready"])
                do(dve.memset(zb[1][:, :, 0:1], 0.0))
                do(dve.memset(zb[2][:, :, 0:1], 0.0))
                for ft in range(4):
                    ssm(l, ft)
                for ft in range(4):
                    dve.wait_ge(v["ys"], l * 4 + ft + 1)
                    split(Bh[:, 4 + ft], Bl[:, 4 + ft], ysf[:, ft], v["ysplit"])
                for i in range(4):
                    dve.wait_ge(s_took["act"], taken["glu", l, i][1])
                    tt(tmp[:, 1, :], tmp[:, 0, :], ysf[:, i], ALU.mult)
                    split(Bh[:, 8 + i], Bl[:, 8 + i], tmp[:, 1, :], v["glu_out"])
                for i in range(5):
                    r = l * 5 + i
                    dve.wait_ge(s_rot, r + 1)
                    dest = qT1[:, i] if i < 4 else kT1
                    tt(tmp[:, 0, :], psS[:, 1, :], tabs[1][1], ALU.mult)
                    tt(tmp[:, 1, :], rawt[:, r % 2, :], tabs[1][0], ALU.mult)
                    tt(dest, tmp[:, 0, :], tmp[:, 1, :], ALU.add, s_rope)
                attention(units[f"sw{l}"])
                do(dve.memset(zc[:, 0:2], 0.0))
                for i in range(4):
                    dve.wait_ge(s_took["act"], taken["cc", l, i][1])
                    bank = from_bank(("cx", l, i))
                    tt(zc[:, 2:], bank, tmp[:, 0, :], ALU.mult, s_took["dve"])
                    ts(ycv, zc[:, 0:SEQ], par(("conv", l), i), None, ALU.mult)
                    stt(ycv, zc[:, 1:SEQ + 1], par(("conv", l), 4 + i), ycv, ALU.mult, ALU.add)
                    stt(ycv, zc[:, 2:SEQ + 2], par(("conv", l), 8 + i), ycv, ALU.mult, ALU.add)
                    bank = from_bank(("cb", l, i))
                    tt(ycv, bank, ycv, ALU.mult, s_took["dve"])
                    split(Bh[:, 4 + i], Bl[:, 4 + i], ycv, s_cy)
                for i in range(KD):
                    for br, kind in enumerate(("ao", "co", "so")):
                        n = 24 * l + 3 * i + br
                        bank = from_bank((kind, l, i))
                        dve.wait_ge(s_took["act"], taken["g" + str(br), l, i][1])
                        gate = rawt[:, n % 2, :]
                        if br == 0:
                            tt(tmp[:, 0, :], bank, gate, ALU.mult, s_took["dve"])
                        else:
                            tt(tmp[:, 1, :], bank, gate, ALU.mult, s_took["dve"])
                            tt(tmp[:, 0, :], tmp[:, 0, :], tmp[:, 1, :], ALU.add)
                        dve.sem_inc(s_sig, 1)
                    split(Mh[:, i], Ml[:, i], tmp[:, 0, :], s_merged)
                for i in range(KD):
                    residual(("mix", l, i), i, True)
                normalise(f"ffn{l}", ("norm_ffn", l))
                for c, (t0, nt) in enumerate(FFN_CHUNKS):
                    if l == DEPTH - 1 and c == 1:
                        memory_normalise()
                    for t in range(t0, t0 + nt):
                        n = FFN_TILES * l + t
                        if l == DEPTH - 1 and t == 6:
                            memory_norm()
                        bank = from_bank(("up", l, t))
                        dve.wait_ge(s_took["act"], taken["gt", l, t][1])
                        tt(tmp[:, 1, :], bank, rawt[:, n % 2, :], ALU.mult, s_took["dve"])
                        split(Mh[:, t - t0], Ml[:, t - t0], tmp[:, 1, :], s_hid)
                    for i in range(KD):
                        residual(("fo", l, c, i), i, c == len(FFN_CHUNKS) - 1)
            normalise("final", "norm_final")
            for k in range(KD):
                dve.wait_ge(s_fin, k + 1)
                add_square(k, X[:, k])
            normalise("norm1", "norm1")
            dve.wait_ge(s_kxsd, XHEADS)
            do(dve.reciprocal(xsd, xsd))
            dve.wait_ge(s_kx, XHEADS)
            tt(kx, kx, xsd, ALU.mult)
            ts(kx, kx, par("xkn"), None, ALU.mult, None, s_kxn)
            project(block2_posts)
            do(dve.tensor_copy(selm[:, 0:P], con("mk", SEQ)[:, SEQ - P:]))
            dve.wait_ge(s_p["toksb"], block2_done["toksb"])
            attention(units2, select)
            for i in range(KD):
                residual(("out2", i), i, True)
            normalise("norm2", "norm2")
            project(x_posts)
            attention(units["x"])
            for i in range(KD):
                residual(("xo", i), i, True)
            normalise("norm3", "norm3")
            for c, (t0, nt) in enumerate(FF2_CHUNKS):
                for t in range(t0, t0 + nt):
                    n = FFN_TILES * DEPTH + t
                    dve.wait_ge(s_took["act"], taken["fi", t][1])
                    tt(tmp[:, 1, :], rawt[:, n % 2, :], rawt[:, n % 2, :], ALU.mult)
                    split(Mh[:, t - t0], Ml[:, t - t0], tmp[:, 1, :], s_hid)
                for i in range(KD):
                    residual(("fo2", c, i), i, False)
            dve.sem_inc(s_y, 1)


def kernel(**inputs):
    import concourse.bacc as bacc
    from concourse.bass_utils import run_bass_kernel_spmd

    w = {k: np.asarray(a) for k, a in inputs.items()}
    parts = []
    for key, K, _, _ in job_plan():
        a = weight_tile(w, key)
        parts.append(a.reshape(K, P, P).transpose(1, 0, 2).reshape(-1))
    arrays = {
        "wstream": np.concatenate(parts),
        "params": pack_params(w),
        "ssmp": pack_ssm(w),
        "cmpw": np.tile(w["w_nsa_cmp_2"][0].transpose(0, 2, 1, 3), (1, 2, 1, 1)).reshape(2, P, CMP_L * HEAD),
        "consts": constants(),
        "xT": np.ascontiguousarray(w["x"][0].T.reshape(KD, P, SEQ).transpose(1, 0, 2)),
        "memT": np.ascontiguousarray(w["mem_2"][0].T.reshape(KD, P, MEM).transpose(1, 0, 2)),
    }
    nc = bacc.Bacc("TRN2", target_bir_lowering=False, num_devices=1)
    args = [nc.dram_tensor(n, a.shape, F32, kind="ExternalInput").ap() for n, a in arrays.items()]
    out = nc.dram_tensor("outT", (P, KD, SEQ), F32, kind="ExternalOutput").ap()
    block_program(nc, *args, out)
    r = run_bass_kernel_spmd(nc, [arrays], core_ids=[0])
    o = r.results[0]["outT"]
    return np.ascontiguousarray(o.transpose(1, 0, 2).reshape(D_MODEL, SEQ).T)[None]
```

```python
import math
from contextlib import ExitStack

import concourse.bass as bass
import numpy as np
from concourse import mybir

F32 = mybir.dt.float32
F32R = mybir.dt.float32r
ALU = mybir.AluOpType
ACT = mybir.ActivationFunctionType
AX_X = mybir.AxisListType.X

P = 128
SEQ = 512
NB = SEQ // P
D_MODEL = 1024
KD = D_MODEL // P
DEPTH = 2
HEAD = 64
HALF = 4
W_IN_COLS = dict(q=0, k=512, v=640, cb=768, cc=1280, cx=1792, u=2304, g=2816)
FFN_TILES = 22
FFN_CHUNKS = [(0, 8), (8, 8), (16, 6)]
FF2_CHUNKS = [(0, 8), (8, 8), (16, 8), (24, 8)]
EPS = 1e-6
NEG = -1e30
TAKEN = -3e38

SSM_STATE = 64
SSM_H = 16
SSM_T = 8
SSM_C = SEQ // SSM_T
SSM_G = P // SSM_H
SSM_GROUPS = 4 * SSM_G
SSM_BC = 4 * SSM_G * SSM_H
SSM_PARAMS = 3 * SSM_GROUPS + 4 * SSM_BC

CMP_N, CMP_L, CMP_STRIDE = 31, 32, 16
TOPK = 128
IDX_SCALE = 8 ** -0.5 * 64 ** -0.5
MEM = 256
UNITS_SW = 16
XHEADS = 4

RAW_SLOTS = 3
SPLIT_SLOTS = 3
GEMM_BANKS = 3



PROJECTIONS = [("p2", n) for n in ("cq0", "cq1", "ckv", "kc", "ki", "wg", "ks")] + [
    ("kvd",), ("p2", "kw"), ("kd",), ("p2", "vc"), ("iq", 0), ("p2", "vs"), ("iq", 1), ("p2", "vw"), ("iq", 2),
    ("p2", "qn0"), ("iq", 3), ("p2", "qn1"), ("uq", 0), ("p2", "qn2"), ("uq", 1), ("p2", "qn3"), ("uq", 2), ("uq", 3)]


FEATURE_TILES = 4
SSM_FIRST, SSM_LAST = -1, 4 * FEATURE_TILES + 2


def mixer_plan(l):
    first = [("u", l, i) for i in range(4)]
    for i in range(4):
        first += [("q", l, i)] + ([("rot", l, i - 1)] if i else [])
    first += [("k", l, 0), ("rot", l, 3), ("v", l, 0), ("rot", l, 4), ("cc", l, 0), ("vt", l), ("cx", l, 0), ("cb", l, 0)]
    for i in range(1, 4):
        first += [("cc", l, i), ("cx", l, i), ("cb", l, i)]
    plan, t, products = [], SSM_FIRST, 0
    ahead = 3 if l == 0 else 2
    for key in first:
        if key[0] not in ("rot", "vt"):
            if products >= ahead and t <= SSM_LAST:
                plan.append(("ssm", t))
                t += 1
            products += 1
        plan.append(("job", key))
    plan += [("ssm", i) for i in range(t, SSM_LAST + 1)]
    unit = -1
    for i in range(4):
        if i % 2 == 0:
            plan.append(("unit", unit))
            unit += 1
        elif unit < UNITS_SW:
            plan.append(("scale", unit))
        plan.append(("job", ("glu", l, i)))
    for gate, out in (("g1", "co"), ("g2", "so"), ("g0", "ao")):
        for i in range(KD):
            if unit <= UNITS_SW + 1:
                plan.append(("unit", unit))
                unit += 1
            plan.append(("job", (gate, l, i)))
            if unit < UNITS_SW:
                plan.append(("scale", unit))
            plan.append(("job", (out, l, i)))
    return plan


def job_plan():
    shape = {"u": (8, "act"), "q": (8, "act"), "k": (8, "act"), "v": (8, "act"), "rot": (0, "dve"), "vt": (0, "act"),
             "cc": (8, "act"), "cx": (8, "dve"), "cb": (8, "dve"), "glu": (4, "act"), "g0": (8, "act"), "g1": (8, "act"),
             "g2": (8, "act"), "ao": (4, "dve"), "co": (4, "dve"), "so": (4, "dve")}
    jobs = []
    for l in range(DEPTH):
        for what, key in mixer_plan(l):
            if what == "job":
                jobs.append((key, shape[key[0]][0], SEQ, shape[key[0]][1]))
        jobs += [(("mix", l, i), 8, SEQ, "dve") for i in range(KD)]
        for c, (t0, nt) in enumerate(FFN_CHUNKS):
            for t in range(t0, t0 + nt):
                jobs += [(("gt", l, t), 8, SEQ, "act"), (("up", l, t), 8, SEQ, "dve")]
            jobs += [(("fo", l, c, i), nt, SEQ, "dve") for i in range(KD)]
    jobs += [(("xk", i), 8, MEM, "act") for i in range(XHEADS)]
    jobs += [(("xv", i), 8, MEM, "act") for i in range(XHEADS)]
    for key in PROJECTIONS:
        K = {"kvd": 1, "kd": 1, "iq": 2, "uq": 2}.get(key[0], 8)
        jobs.append((key, K, SEQ, "act"))
    jobs += [(("out2", i), 8, SEQ, "dve") for i in range(KD)]
    jobs += [(("xq", i), 8, SEQ, "act") for i in range(XHEADS)]
    jobs += [(("xo", i), 4, SEQ, "dve") for i in range(KD)]
    for c, (t0, nt) in enumerate(FF2_CHUNKS):
        jobs += [(("fi", t), 8, SEQ, "act") for t in range(t0, t0 + nt)]
        jobs += [(("fo2", c, i), nt, SEQ, "dve") for i in range(KD)]
    return jobs


def weight_tile(w, key):
    kind = key[0]
    cols = lambda a, c, n=P: a[:, c:c + n]
    both = lambda a, c0, c1: np.concatenate([a[:, c0:c0 + HEAD], a[:, c1:c1 + HEAD]], 1)
    pairs = lambda a: np.concatenate(
        [np.concatenate([a[j * HEAD:(j + 1) * HEAD], a[(j + 4) * HEAD:(j + 5) * HEAD]]) for j in range(4)])
    if kind in ("u", "k", "v", "cc", "cx", "cb"):
        return cols(w["w_in"][key[1]], W_IN_COLS[kind] + P * key[2])
    if kind in ("g0", "g1", "g2"):
        return cols(w["w_in"][key[1]], W_IN_COLS["g"] + D_MODEL * int(kind[1]) + P * key[2])
    if kind == "q":
        return both(w["w_in"][key[1]], key[2] * HEAD, (key[2] + 4) * HEAD)
    if kind == "glu":
        return cols(w["w_ssm_glu"][key[1]], P * key[2])
    if kind == "ao":
        return cols(pairs(w["w_attn_o"][key[1]]), P * key[2])
    if kind == "co":
        return cols(w["w_conv_o"][key[1]], P * key[2])
    if kind == "so":
        return cols(w["w_ssm_o"][key[1]], P * key[2])
    if kind == "mix":
        return cols(w["w_mix_o"][key[1]], P * key[2])
    if kind in ("gt", "up"):
        return cols(w["w_ffn_in"][key[1]], P * key[2] + (FFN_TILES * P if kind == "up" else 0))
    if kind == "fo":
        t0, nt = FFN_CHUNKS[key[2]]
        return cols(w["w_ffn_out"][key[1]][t0 * P:(t0 + nt) * P], P * key[3])
    if kind == "p2":
        a, name = w["w_in_2"][0], key[1]
        if name in ("cq0", "cq1", "ckv"):
            return cols(a, {"cq0": 0, "cq1": 128, "ckv": 256}[name])
        if name == "ki":
            return both(a, 384, 384)
        if name == "wg":
            return np.concatenate([a[:, 448:456], a[:, 1640:1760]], 1)
        if name[:2] == "qn":
            j = int(name[2])
            return both(a, 456 + j * HEAD, 456 + (j + 4) * HEAD)
        return cols(a, 968 + {"kc": 0, "vc": 1, "ks": 2, "vs": 3, "kw": 4, "vw": 5}[name] * P)
    if kind == "kvd":
        return w["w_dsa_ukv_2"][0]
    if kind == "kd":
        return both(w["w_dsa_ukv_2"][0], 0, 0)
    if kind == "iq":
        return cols(w["w_idx_q_2"][0], P * key[1])
    if kind == "uq":
        return cols(w["w_dsa_uq_2"][0], P * key[1])
    if kind == "out2":
        a = w["w_out_2"][0]
        return cols(np.concatenate([a[:512], pairs(a[512:])]), P * key[1])
    if kind in ("xk", "xv", "xq", "xo"):
        return cols(w["w_" + kind + "_2"][0], P * key[1])
    if kind == "fi":
        return cols(w["w_ff_in_2"][0], P * key[1])
    if kind == "fo2":
        t0, nt = FF2_CHUNKS[key[1]]
        return cols(w["w_ff_out_2"][0][t0 * P:(t0 + nt) * P], P * key[2])
    raise KeyError(key)




def param_columns():
    at, n = {}, 0
    for l in range(DEPTH):
        for name, c in (("norm_mix", 8), ("norm_ffn", 8), ("b_gate", 24), ("sinks", 8), ("conv", 12), ("ssm_d", 4)):
            at[name, l] = (n, c)
            n += c
    for name, c in (("norm_final", 8), ("norm1", 8), ("norm2", 8), ("norm3", 8), ("mem_norm", 8), ("cq", 2),
                    ("ckv", 1), ("lng", 1), ("lnb", 1), ("dqn", 1), ("dkn", 1), ("nqn", 1), ("nkn", 3),
                    ("xqn", 1), ("xkn", 1), ("pe", 64), ("J", 9), ("eps", 1), ("sgn", 1)):
        at[name] = (n, c)
        n += c
    return at, n


def pack_params(w):
    at, n = param_columns()
    out = np.zeros((P, n), np.float32)

    def put(key, a):
        c, m = at[key]
        out[:, c:c + m] = a

    feat = lambda v: np.asarray(v).reshape(-1, P).T
    twice = lambda v: np.concatenate([v, v])
    for l in range(DEPTH):
        put(("norm_mix", l), feat(w["norm_mix"][l]))
        put(("norm_ffn", l), feat(w["norm_ffn"][l]))
        put(("b_gate", l), feat(w["b_gate"][l]))
        put(("sinks", l), np.broadcast_to(w["attn_sinks"][l], (P, 8)))
        put(("conv", l), feat(w["conv_w"][l].reshape(-1)))
        put(("ssm_d", l), feat(w["ssm_d"][l]))
    put("norm_final", feat(w["norm_final"]))
    put("norm1", feat(w["norm1_g_2"][0]))
    put("norm2", feat(w["norm2_g_2"][0]))
    put("norm3", feat(w["norm3_g_2"][0]))
    put("mem_norm", feat(w["mem_norm_g_2"][0]))
    put("cq", feat(w["dsa_cq_g_2"][0]))
    put("ckv", feat(w["dsa_ckv_g_2"][0]))
    put("lng", twice(w["idx_k_ln_g_2"][0])[:, None])
    put("lnb", twice(w["idx_k_ln_b_2"][0])[:, None])
    put("dqn", twice(w["dsa_qn_g_2"][0])[:, None])
    put("dkn", twice(w["dsa_kn_g_2"][0])[:, None])
    put("nqn", twice(w["nsa_qn_g_2"][0])[:, None])
    put("nkn", twice(w["nsa_kn_g_2"][0].T))
    put("xqn", w["xq_norm_g_2"][0][:, None])
    put("xkn", w["xk_norm_g_2"][0][:, None])
    pe = w["nsa_cmp_pe_2"][0]
    put("pe", twice(pe.transpose(2, 0, 1).reshape(HEAD, 64)))
    put("J", np.broadcast_to(np.arange(9), (P, 9)))
    put("eps", EPS)
    put("sgn", np.where(np.arange(P) < HEAD, 1.0, -1.0)[:, None])
    return out


def pack_ssm(w):
    out = np.zeros((DEPTH, P, SSM_PARAMS), np.float32)
    for l in range(DEPTH):
        rdt = [w["ssm_a_re"][l].T, w["ssm_a_im"][l].T, np.broadcast_to(w["ssm_log_dt"][l], (SSM_STATE, SSM_GROUPS))]
        top, low = list(rdt), list(rdt)
        for ft in range(FEATURE_TILES):
            g = slice(ft * SSM_G, (ft + 1) * SSM_G)
            br, bi = (w[n][l, g].transpose(1, 0, 2).reshape(SSM_STATE, -1) for n in ("ssm_b_re", "ssm_b_im"))
            cr, ci = (w[n][l, g].transpose(2, 0, 1).reshape(SSM_STATE, -1) for n in ("ssm_c_re", "ssm_c_im"))
            top += [br, bi, cr, ci]
            low += [bi, br, ci, cr]
        out[l] = np.concatenate([np.concatenate(top, 1), np.concatenate(low, 1)])
    return out




CONST_MATS = ("ident", "ones", "blk", "rot1", "rot2")
CONST_AT = {n: i * P for i, n in enumerate(CONST_MATS)}
MATS_N = _n = len(CONST_MATS) * P
for _name, _c in (("C1", SEQ), ("S1", SEQ), ("sw", 2 * P), ("mk", SEQ),
                  ("cmp_add", NB * CMP_N), ("cmp_mul", NB * CMP_N)):
    CONST_AT[_name] = _n
    _n += _c
CONST_N = _n


def constants():
    c = np.zeros((P, CONST_N), np.float32)
    second = np.zeros((P, 2 * SEQ), np.float32)

    def put(name, a):
        a = np.asarray(a, np.float32).reshape(P, -1)
        c[:, CONST_AT[name]:CONST_AT[name] + a.shape[1]] = a

    put("ident", np.eye(P))
    put("ones", np.full((P, P), 1.0 / D_MODEL))
    put("blk", np.kron(np.eye(2), np.full((HEAD, HEAD), 1.0 / HEAD)))

    def rotation(half):
        r = np.zeros((P, P))
        for base in (0, HEAD):
            for d in range(half):
                r[base + d + half, base + d] = -1.0
                r[base + d, base + d + half] = 1.0
        return r

    put("rot1", rotation(8))
    put("rot2", rotation(32))

    def tables(theta, half, width):
        pos = np.arange(SEQ, dtype=np.float32)
        inv = np.float32(theta) ** (-np.arange(half, dtype=np.float32) / np.float32(half))
        if width == 16:
            inv = np.float32(theta) ** (-np.arange(0, 16, 2, dtype=np.float32) / np.float32(16))
        ang = (pos[:, None] * inv.astype(np.float32)[None, :]).astype(np.float32).astype(np.float64)
        co, si = np.cos(ang).T, np.sin(ang).T
        ct, st = np.ones((HEAD, SEQ)), np.zeros((HEAD, SEQ))
        ct[:half], ct[half:2 * half] = co, co
        st[:half], st[half:2 * half] = si, si
        return np.concatenate([ct, ct]), np.concatenate([st, st])

    a, b = tables(500000.0, 8, 16)
    put("C1", a)
    put("S1", b)
    a, b = tables(10000.0, 32, 64)
    second[:, :SEQ], second[:, SEQ:] = a, b
    qi, kj = np.arange(P)[:, None], np.arange(2 * P)[None, :]
    delta = qi + P - kj
    put("sw", np.where((delta >= 0) & (delta < P), 0.0, NEG))
    mk = np.zeros((P, SEQ))
    mk[:, SEQ - P:] = np.where(np.arange(P)[None, :] <= qi, 0.0, NEG)
    put("mk", mk)
    t = np.arange(NB)[None, :, None] * P + np.arange(P)[:, None, None]
    ok = np.arange(CMP_N)[None, None, :] * CMP_STRIDE + CMP_L - 1 <= t
    put("cmp_add", np.where(ok, 0.0, NEG))
    put("cmp_mul", ok)
    return c, second




def units_sw(l):
    out = []
    for b in range(NB):
        for j in range(4):
            out.append(dict(kind="sw", l=l, b=b, j=j, W=P if b == 0 else 2 * P, k0=0 if b == 0 else (b - 1) * P,
                            first=True, last=True))
    return out


def units_dsa(b):
    return [dict(kind="dsa", b=b, j=j, W=(b + 1) * P, k0=0, first=True, last=True) for j in range(4)]


def units_nsa(b):
    out = []
    for j in range(4):
        out.append(dict(kind="slc", b=b, j=j, W=(b + 1) * P, k0=0, first=True, last=False))
        out.append(dict(kind="cmp", b=b, j=j, W=CMP_N, k0=0, first=False, last=False))
        out.append(dict(kind="win", b=b, j=j, W=(b + 1) * P, k0=0, first=False, last=True))
    return out


def units_x():
    return [dict(kind="x", b=b, j=j, W=MEM, k0=0, first=True, last=True) for b in range(NB) for j in range(2)]


def all_units():
    lists = {"sw0": units_sw(0), "sw1": units_sw(1)}
    for kind, make in (("nsa", units_nsa), ("dsa", units_dsa)):
        for b in reversed(range(NB)):
            lists[kind, b] = make(b)
    lists["x"] = units_x()
    n = g = 0
    for us in lists.values():
        for u in us:
            u["n"], u["group"] = n, g
            n += 1
            g += u["last"]
    return lists


class Line:

    def __init__(self, eng, chain):
        self.eng, self.chain, self.count = eng, chain, {}

    def done(self, ins, sem=None):
        sem = sem or self.chain
        ins.then_inc(sem, 1)
        self.count[sem.name] = self.count.get(sem.name, 0) + 1
        self.eng.wait_ge(sem, self.count[sem.name])


def block_program(nc, wstream, params, ssmp, cmpw, consts, rope2, xT, memT, outT):
    jobs = job_plan()
    weights = [j for j in jobs if j[1]]
    offset, number, taken = {}, {}, {}
    tile_of = {key: n for n, (key, *_) in enumerate(weights)}
    at = 0
    free_count = {"act": 0, "dve": 0}
    for n, (key, K, N, who) in enumerate(jobs):
        offset[key], number[key] = at, n
        at += K * P * P
        free_count[who] += 1
        taken[key] = (who, free_count[who])
    units = all_units()
    units2 = [u for kind in ("nsa", "dsa") for b in reversed(range(NB)) for u in units[kind, b]]
    pcol, npar = param_columns()

    ctx = ExitStack()
    with ctx:
        def sem(name):
            return ctx.enter_context(nc.semaphore(name))

        base = (nc.sbuf_base + 63) // 64 * 64
        cursor = [base]

        def place(name, shape, dt, at=None):
            size = 4 * int(np.prod(shape[1:]))
            off = cursor[0] if at is None else at
            if at is None:
                cursor[0] += (size + 31) // 32 * 32
            return nc.alloc_sbuf_tensor_at(name, shape, dt, offset=off), off

        X, _ = place("x", [P, KD, SEQ], F32)
        Hh, _ = place("h_hi", [P, KD, SEQ], F32R)
        Hl, _ = place("h_lo", [P, KD, SEQ], F32R)
        Mh, m_at = place("m_hi", [P, KD, SEQ], F32R)
        Ml, _ = place("m_lo", [P, KD, SEQ], F32R)
        Bh, b_at = place("b_hi", [P, 12, SEQ], F32R)
        Bl, _ = place("b_lo", [P, 12, SEQ], F32R)
        R, _ = place("work_m", [P, 2 * KD * SEQ], F32, at=m_at)
        R2, _ = place("work_b", [P, 24 * SEQ], F32, at=b_at)
        raw, _ = place("w_raw", [P, RAW_SLOTS, 8 * P], F32)
        Wh, _ = place("w_hi", [P, SPLIT_SLOTS, 8, P], F32R)
        Wl, _ = place("w_lo", [P, SPLIT_SLOTS, 8, P], F32R)
        CON, _ = place("consts", [P, CONST_N], F32)
        PAR, _ = place("params", [P, npar], F32)
        sqr, _ = place("squares", [P, 2, SEQ], F32)
        root_tok, _ = place("norm_root_tok", [P, NB], F32)
        tmp, _ = place("tmp", [P, 3, SEQ], F32)
        rawt, _ = place("raw_tile", [P, 2, SEQ], F32)
        stat, _ = place("stats", [P, 4, 12], F32)
        gtok, _ = place("gate_tok", [P, NB, 24], F32)
        wtok, _ = place("widx_tok", [P, NB, 8], F32)
        m8, _ = place("max8", [P, 8], F32)
        TS, _ = place("small_work", [P, 4448], F32)
        assert cursor[0] <= nc.sbuf_usable_end, (cursor[0], nc.sbuf_usable_end)

        psG = ctx.enter_context(nc.psum_tensor("psG", [P, GEMM_BANKS, SEQ], F32))
        psS = ctx.enter_context(nc.psum_tensor("psS", [P, 2, SEQ], F32))
        psT = ctx.enter_context(nc.psum_tensor("psT", [P, 2, SEQ], F32))
        psO = ctx.enter_context(nc.psum_tensor("psO", [P, SEQ], F32))

        def con(name, n, rows=P):
            return CON[0:rows, CONST_AT[name]:CONST_AT[name] + n]

        ident, ones, blk = con("ident", P), con("ones", P), con("blk", P)
        rots = {1: con("rot1", P), 2: con("rot2", P)}
        tabs = con("C1", SEQ), con("S1", SEQ)

        def par(key, i=0, n=1):
            c, _ = pcol[key]
            return PAR[:, c + i:c + i + n]

        eps, sgn, J = par("eps"), par("sgn"), par("J", 0, 9)

        s_raw = [sem(f"weights_landed{i}") for i in range(RAW_SLOTS)]
        s_hi = sem("weights_hi")
        s_split = sem("weights_split")
        s_job = sem("product_done")
        s_took = {"act": sem("product_taken_act"), "dve": sem("product_taken_dve")}
        s_mats = sem("matrices_landed")
        s_in, s_par, s_ssm0, s_rope2 = (sem(n + "_landed") for n in ("consts", "params", "ssm_eigen", "rope2"))
        s_x = [sem(f"x_landed{i}") for i in range(4)]
        s_mem = sem("memory_landed")
        s_ssmp = [sem("ssm_params_landed0"), sem("ssm_params_landed1")]
        s_toep, s_w2 = sem("toeplitz_landed"), sem("swapped_w_landed")
        s_cw = sem("cmp_weights_landed")
        s_out = sem("out_landed")
        c_act, c_dve, c_pool = sem("act_chain"), sem("dve_chain"), sem("pool_chain")
        s_sqk, s_sqm, s_ms, s_sd = sem("squares"), sem("squares_summed"), sem("mean_square"), sem("norm_root")
        s_dg, s_rr = sem("inverse_root_diagonal"), sem("inverse_root_spread")
        s_xs, s_hh, s_h, s_hp = sem("x_scaled"), sem("h_hi_ready"), sem("h_lo_ready_dve"), sem("h_lo_ready_pool")
        s_m, s_kx, s_kxsq, s_kxms, s_xtr, s_vx = (sem("mem_" + n) for n in (
            "h_ready", "keys_raw", "keys_squared", "keys_mean", "values_transposed", "values_ready"))
        s_xtr_in = sem("mem_values_raw")
        s_kxsd, s_kxn, s_norm = sem("mem_keys_root"), sem("mem_keys_ready"), sem("prob_factor")
        s_y, s_fin = sem("final_x_ready"), sem("final_norm")
        names = ("dt args coef wb w1 g_out g_sb wbt wt_sb u2 u2_sb ug ug_sb e z yc yc_sb yt ypre ys "
                 "ysplit glu_out toep_clear").split()
        v = {n: sem("ssm_" + n) for n in names}
        s_rawt, s_rot, s_rope = sem("rope_in"), sem("rotated"), sem("roped")
        s_vraw, s_vt, s_vtok = sem("v_raw"), sem("v_transposed"), sem("v_tok")
        s_cc, s_cy = sem("conv_cc"), sem("conv_y")
        s_sig, s_merged = sem("gate_sigmoid"), sem("merged")
        s_silu, s_hid = sem("silu"), sem("hidden")
        s_sc, s_masked, s_neg, s_exp = sem("scores"), sem("masked"), sem("neg_max"), sem("exped")
        s_prob, s_tr, s_pt, s_pv, s_oe = (sem(x) for x in ("probs", "probs_t", "probs_t_sb", "pv", "attn_out"))
        s_is, s_ir, s_ia, s_sel = sem("idx_scores"), sem("idx_relu"), sem("idx_added"), sem("selected")
        s_p = {n: sem("post_" + n) for n in ("raw", "cmpin", "cmpo", "cmean", "cen", "sqa", "sqd", "mean", "sd",
                                          "qn", "rot", "rotd", "out", "tok", "toksb")}

        block = ctx.enter_context(nc.Block())

        def work(t, off, shape):
            n = int(np.prod(shape[1:]))
            a = t[0:shape[0], off:off + n]
            if len(shape) == 3:
                a = a.rearrange("p (a b) -> p a b", b=shape[2])
            elif len(shape) == 4:
                a = a.rearrange("p (a b c) -> p a b c", b=shape[2], c=shape[3])
            return a

        qT1, kT1, vt1 = work(R, 0, [P, 4, SEQ]), work(R, 2048, [P, SEQ]), work(R, 2560, [P, NB, P])
        rotC, rotS = work(R, 3072, [P, SSM_G, SSM_C]), work(R, 3584, [P, SSM_G, SSM_C])
        uT = work(R, 4096, [P, 4, SEQ])
        ysf = uT
        pwork = work(R, 6144, [P, 2 * SEQ])
        UG = work(R, 7168, [P, SSM_G, SSM_C])
        z1 = work(R, 7680, [P, SSM_G, SSM_C])
        partial = work(R, 4096, [P, KD, SEQ])
        W1 = work(R2, 0, [P, SSM_G, SSM_T + 1, SSM_H])
        z2 = work(R2, 1152, [P, SSM_G, SSM_C])
        Z1, Z2, X1 = (work(R2, 1664 + 128 * i, [P, SSM_G, SSM_H]) for i in range(3))
        W2 = work(R2, 4096, [P, SSM_G, SSM_T, SSM_H])
        WbE = work(R2, 5120, [P, SSM_G, SSM_T, SSM_H])
        Gm = work(R2, 5120, [SSM_H, SSM_G, P])
        WT = work(R2, 6144, [P, SSM_G, P])
        WTI = work(R2, 7168, [P, SSM_G, P])
        TO = work(R2, 10240, [P, SSM_G, P])
        U2 = R2[0:SSM_C, 11264:12288].rearrange("p (g x) -> p g x", x=P)
        Y2 = R2[SSM_C:2 * SSM_C, 11264:12288].rearrange("p (j x) -> p j x", x=P)
        GR = SSM_GROUPS
        eig = work(R2, 4096, [P, 3, GR])
        NJ = 9 + 8 + 8
        arg, arg2, red = (work(R2, 4224 + 800 * i, [P, GR, NJ]) for i in range(3))
        mag, snA, csA = (work(R2, 6624 + 288 * i, [P, GR, 9]) for i in range(3))
        sm = work(R2, 7488, [P, 16, GR])
        t3 = work(R2, 10240, [P, GR, 8])
        zc = work(TS, 0, [P, SEQ + 2])
        Lr, Li = work(TS, 516, [P, GR, 9]), work(TS, 804, [P, GR, 9])
        Lcr, Lci = work(TS, 1092, [P, GR, 8]), work(TS, 1348, [P, GR, 8])
        snB, csB = work(TS, 1604, [P, GR, 16]), work(TS, 2116, [P, GR, 16])
        mag8, cr, ci = (work(TS, 2628 + GR * i, [P, GR]) for i in range(3))
        sp = [work(TS, 2724 + SSM_BC * i, [P, SSM_BC]) for i in range(2)]
        Y1n, t4 = work(TS, 3748, [P, SSM_G, SSM_H]), work(TS, 3876, [P, SSM_G, SSM_H])
        qn, qd, qi = (work(R, 2048 * i, [P, 4, SEQ]) for i in range(3))
        kd, ki, ks, kw = (work(R, 6144 + 512 * i, [P, SEQ]) for i in range(4))
        vd, vs, vw = work(R2, 0, [P, NB, HEAD]), work(R2, 256, [P, NB, P]), work(R2, 768, [P, NB, P])
        vc, kc = work(R2, 1280, [P, P]), work(R2, 1408, [P, CMP_N])
        iacc, iwork = work(R2, 1536, [P, SEQ]), work(R2, 2048, [P, SEQ])
        selected = {3: work(R2, 2560, [P, SEQ]), 2: work(R2, 10240, [P, SEQ]), 1: work(R2, 10752, [P, SEQ])}
        irelu = work(R2, 3072, [P, 2, SEQ])
        cmpW = work(R2, 6144, [P, CMP_L, P])
        cmpin = work(TS, 0, [P, CMP_L, CMP_N])
        cmpt = work(TS, 1000, [P, 2, CMP_N])
        cqf = work(TS, 0, [P, 3, SEQ])
        raws = [rawt[:, 0, :], rawt[:, 1, :], work(R2, 11 * SEQ, [P, SEQ]), work(R2, 23 * SEQ, [P, SEQ])]
        qx, kx, vx = work(R, 0, [P, 4, SEQ]), work(TS, 1100, [P, XHEADS, MEM]), work(TS, 2124, [P, 2, XHEADS * P])
        memf = work(R2, 8192, [P, KD, MEM])
        xsq = work(R2, 2048, [P, 2, MEM])
        xsd = work(R2, 2560, [P, XHEADS, MEM])
        xraw = work(R2, 3584, [P, 2, MEM])
        mH = Bh[:, 0:4, :].rearrange("p a b -> p (a b)").rearrange("p (k n) -> p k n", n=MEM)
        mL = Bl[:, 0:4, :].rearrange("p a b -> p (a b)").rearrange("p (k n) -> p k n", n=MEM)

        def probs(u):
            n, W = u["n"], u["W"]
            if u["kind"] == "sw":
                p = work(R, 3072 + 512 * (n % 2), [P, 2, 2 * P])
                t = work(TS, 2724 + 512 * (n % 2), [P, 2, 2, P])
            else:
                p = work(R2, 4096 + 1024 * (n % 4), [P, 2, SEQ])
                t = work(R2, 8192 + 1024 * (n % 2), [P, 2, NB, P])
            return p[:, :, 0:W], t

        def narrow(u):
            return u["kind"] in ("sw", "x")

        def ahead(u):
            return 1 if u["kind"] == "sw" else 3

        def stats(u):
            return stat[:, u["n"] % 4]

        def score_banks(u):
            if u["kind"] == "sw":
                return psS[:, :, 0:u["W"]]
            return psG[:, 0:2, 0:u["W"]] if u["n"] % 2 else psS[:, :, 0:u["W"]]

        def transpose_banks(u):
            n = u["n"]
            if narrow(u):
                return psT[:, n % 2, :].rearrange("p (a w) -> p a w", a=2)
            return psT[:, :, :]

        def key_blocks(u):
            return [(0, u["W"])] if u["kind"] == "cmp" else [(i, P) for i in range(u["W"] // P)]

        def moving(key, k):
            kind = key[0]
            if kind == "glu":
                return Bh[:, k, :], Bl[:, k, :]
            if kind == "ao":
                return Bh[:, k, :], Bl[:, k, :]
            if kind == "co":
                return Bh[:, 4 + k, :], Bl[:, 4 + k, :]
            if kind == "so":
                return Bh[:, 8 + k, :], Bl[:, 8 + k, :]
            if kind in ("mix", "fo", "fo2"):
                return Mh[:, k, :], Ml[:, k, :]
            if kind in ("iq", "uq"):
                return Bh[:, 8 + k, :], Bl[:, 8 + k, :]
            if kind in ("kd", "kvd"):
                return Bh[:, 10, :], Bl[:, 10, :]
            if kind in ("xk", "xv"):
                return mH[:, k, :], mL[:, k, :]
            return Hh[:, k, :], Hl[:, k, :]

        NORMS = {"mix0": 0, "ffn0": 1, "mix1": 2, "ffn1": 3, "mem": 4, "final": 5, "norm1": 6, "norm2": 7, "norm3": 8}
        h_norm = {name: i for i, name in enumerate(n for n in NORMS if n not in ("final", "mem"))}
        first_job = {"mix0": ("u", 0, 0), "ffn0": ("gt", 0, 0), "mix1": ("u", 1, 0), "ffn1": ("gt", 1, 0),
                     "norm1": PROJECTIONS[0], "norm2": ("xq", 0), "norm3": ("fi", 0)}
        NEXT_NORM = [f"mix{l}" for l in range(1, DEPTH)] + ["final"]
        last_product = {"norm2": ("out2",), "norm3": ("xo",)}
        for l in range(DEPTH):
            last_product[f"ffn{l}"] = ("mix", l)
            last_product[NEXT_NORM[l]] = ("fo", l, len(FFN_CHUNKS) - 1)
        norm_before = {tile_of[key] + SPLIT_SLOTS: name for name, key in first_job.items()}

        roots = (sqr[:, 0, :], sqr[:, 1, :])
        qs, qneg = (work(TS, 3200 + 64 * i, [P, 8, NB, 2]) for i in range(2))
        xs, xneg = (work(TS, 3328 + 16 * i, [P, XHEADS, NB]) for i in range(2))

        def query_factors(u, sign=1):
            if u["kind"] == "x":
                return (xs if sign > 0 else xneg)[:, 2 * u["j"]:2 * u["j"] + 2, u["b"]]
            return (qs if sign > 0 else qneg)[:, u["j"] + (4 if u["kind"] == "dsa" else 0), u["b"], :]

        def description(key):
            kind, name = key[0], key[1] if len(key) > 1 else None
            if kind == "p2":
                return {"kc": ("cmpk", ("nkn", 0), kc), "vc": ("cmpv", None, None), "cq0": ("lat", None, 0),
                        "cq1": ("lat2", None, 1), "ckv": ("lat1", None, 2), "wg": ("tokwg", None, None),
                        "vs": ("tok", None, vs), "vw": ("tok", None, vw), "ki": ("ln", None, ki),
                        "ks": ("rms", ("nkn", 1), ks), "kw": ("rms", ("nkn", 2), kw),
                        }.get(name) or ("qrms", ("nqn", 0), qn[:, int(name[2])], int(name[2]))
            return {"kvd": lambda: ("tokd", None, None), "kd": lambda: ("rms", ("dkn", 0), kd),
                    "iq": lambda: ("rope", None, qi[:, name]), "uq": lambda: ("qrms", ("dqn", 0), qd[:, name], 4 + name),
                    "xq": lambda: ("xqrms", ("xqn", 0), qx[:, name], name)}[kind]()

        PHASES = {"cmpk": ("", "", "cmp", "mean", "rot"), "cmpv": ("", "", "cmp", "tok"), "lat": ("",), "lat2": ("", "mean"),
                  "lat1": ("", "mean"), "tokwg": ("", "tok"), "tok": ("", "tok"), "tokd": ("", "tok"),
                  "ln": ("", "cmean", "mean", "rot"), "rms": ("", "mean", "rot"), "rope": ("", "rot"), "qrms": ("", "query"), "xqrms": ("", "query")}
        posts = []
        for key in PROJECTIONS + [("xq", j) for j in range(4)]:
            kind, gain, dest, *tile = description(key)
            posts.append(dict(key=key, kind=kind, gain=gain, dest=dest, i=len(posts), tile=tile[0] if tile else None))
        by_key = {p["key"]: p for p in posts}
        block2_posts, x_posts = posts[:len(PROJECTIONS)], posts[len(PROJECTIONS):]

        def waves(ps):
            for s_ in range(len(ps) + 4):
                old = [(ps[s_ - f], PHASES[ps[s_ - f]["kind"]][f]) for f in (4, 3, 2, 1)
                       if 0 <= s_ - f < len(ps) and f < len(PHASES[ps[s_ - f]["kind"]])]
                yield (ps[s_] if s_ < len(ps) else None), old

        def gate_number(key):
            return 24 * key[1] + {"g1": 0, "g2": 1, "g0": 2}[key[0]] * KD + key[2]

        tally = {n: 0 for n in s_p}
        square_reader = [None, None]

        def step(p, *names_):
            for n_ in names_:
                tally[n_] += 1
                p[n_] = tally[n_]

        def square_place(p):
            i_ = (tally["sqa"] + tally["sqd"]) % 2
            p["sq_at"], p["sq_wait"] = i_, square_reader[i_]
            square_reader[i_] = posts[p["i"] + 1] if p["kind"] == "lat" else p

        for ps in (block2_posts, x_posts):
            for new, old in waves(ps):
                if new:
                    step(new, "raw")
                    if new["kind"] in ("lat", "lat2", "lat1", "rms", "qrms", "xqrms"):
                        square_place(new)
                        step(new, "sqa")
                for p, phase in old:
                    if phase in ("cmp", "cmean"):
                        step(p, "cmpo" if phase == "cmp" else "cmean", "cen")
                        if p["kind"] != "cmpv":
                            square_place(p)
                            step(p, "sqd")
                    elif phase == "mean":
                        step(p, "mean", "sd", "qn" if "rot" in PHASES[p["kind"]] else "out")
                    elif phase == "rot":
                        step(p, "rot", "rotd", "out")
                    elif phase == "query":
                        step(p, "mean", "sd", *(("rot", "rotd") if p["kind"] == "qrms" else ()), "out")
                    elif phase == "tok":
                        step(p, "tok", "toksb")
                if new and new["kind"] in ("cmpk", "cmpv"):
                    step(new, "cmpin")
        def beside(i, which):
            b, r = NB - 1 - i // 12, 2 * (i % 12) + which
            return (b, r) if i < 12 * (NB - 1) else None

        all_done = dict(tally)
        block2_done = {n_: max(p.get(n_, 0) for p in block2_posts) for n_ in s_p}

        @block.sync
        def _(sp_eng):
            for i in range(4):
                sp_eng.dma_start(X[:, 2 * i:2 * i + 2, :], xT[:, 2 * i:2 * i + 2, :]).then_inc(s_x[i], 16)
            for n, (key, K, N, who) in enumerate(weights):
                if n >= RAW_SLOTS:
                    sp_eng.wait_ge(s_split, n - RAW_SLOTS + 1)
                src = wstream[offset[key]:offset[key] + K * P * P].rearrange("(p f) -> p f", p=P)
                sp_eng.dma_start(raw[:, n % RAW_SLOTS, 0:K * P], src).then_inc(s_raw[n % RAW_SLOTS], 16)
                if n == 1:
                    sp_eng.dma_start(CON[:, MATS_N:], consts[:, MATS_N:]).then_inc(s_in, 16)
            sp_eng.wait_ge(s_y, 1)
            sp_eng.dma_start(outT, X[:, :, :]).then_inc(s_out, 16)
            sp_eng.wait_ge(s_out, 16)

        @block.gpsimd
        def _(pool):
            def split_weights(n):
                key, K, N, who = weights[n]
                pool.wait_ge(s_raw[n % RAW_SLOTS], 16 * (n // RAW_SLOTS + 1))
                if n >= SPLIT_SLOTS:
                    pool.wait_ge(s_job, n - SPLIT_SLOTS + 1)
                w = raw[:, n % RAW_SLOTS, 0:K * P]
                hi = Wh[:, n % SPLIT_SLOTS, 0:K, :].rearrange("p k n -> p (k n)")
                lo = Wl[:, n % SPLIT_SLOTS, 0:K, :].rearrange("p k n -> p (k n)")
                pool.tensor_scalar(hi, w, 1.0, 0.0, ALU.mult, ALU.add).then_inc(s_hi, 1)
                pool.wait_ge(s_hi, n + 1)
                pool.tensor_tensor(lo, w, hi.bitcast(F32), ALU.subtract).then_inc(s_split, 1)

            def norm_low_parts(name):
                for k in range(1, KD, 2):
                    pool.wait_ge(s_hh, KD * h_norm[name] + k + 1)
                    pool.tensor_tensor(Hl[:, k], tmp[:, k % 3, :], Hh[:, k].bitcast(F32), ALU.subtract).then_inc(s_hp, 1)

            def scale_probs(u):
                n = u["n"]
                p, _ = probs(u)
                st = stats(u)
                pool.wait_ge(s_norm, n - units2[0]["n"] + 1)
                for a in range(2):
                    gate = 1.0
                    if u["kind"] != "dsa":
                        c = 3 * (u["j"] + 4 * a) + ("cmp", "slc", "win").index(u["kind"])
                        gate = gtok[:, u["b"], c:c + 1]
                    ins = pool.tensor_scalar(p[:, a], p[:, a], st[:, 8 + a:9 + a], gate, ALU.mult, ALU.mult)
                    ins.then_inc(s_prob if a else c_pool, 1)

            for n in range(len(weights)):
                if n in norm_before:
                    norm_low_parts(norm_before[n])
                if n == tile_of["out2", 0] + SPLIT_SLOTS:
                    for u in units2:
                        scale_probs(u)
                split_weights(n)

        group_total = {"mixer2": units2[-1]["group"] + 1, "x": units["x"][-1]["group"] + 1}

        @block.tensor
        def _(pe):
            def free_bank(key):
                n = number[key]
                if n >= GEMM_BANKS:
                    who, count = taken[jobs[n - GEMM_BANKS][0]]
                    pe.wait_ge(s_took[who], count)
                return psG[:, n % GEMM_BANKS, 0:jobs[n][2]]

            def product(key):
                w = tile_of[key]
                K = weights[w][1]
                pe.wait_ge(s_split, w + 1)
                out = free_bank(key)
                for k in range(K):
                    hi, lo = moving(key, k)
                    for need in h_need(key, k):
                        pe.wait_ge(*need)
                    whi, wlo = Wh[:, w % SPLIT_SLOTS, k, :], Wl[:, w % SPLIT_SLOTS, k, :]
                    pe.matmul(out, whi, hi, start=(k == 0), stop=False)
                    pe.matmul(out, whi, lo, start=False, stop=False)
                    ins = pe.matmul(out, wlo, hi, start=False, stop=(k == K - 1))
                ins.then_inc(s_job, 1)

            def h_need(key, k):
                kind = key[0]
                for name, first in first_job.items():
                    if key == first:
                        n_ = KD // 2 * h_norm[name] + k // 2 + 1
                        return [(s_hp if k % 2 else s_h, n_)]
                if kind == "xk" and key[1] == 0:
                    return [(s_m, k + 1)]
                if kind == "glu" and key[2] == 0:
                    return [(v["ysplit"], key[1] * 4 + k + 1)]
                if kind == "ao" and key[2] == 0:
                    return [(s_oe, 16 * (key[1] + 1))]
                if kind == "co" and key[2] == 0:
                    return [(s_cy, 4 * (key[1] + 1))]
                if kind == "so" and key[2] == 0:
                    return [(v["glu_out"], 4 * (key[1] + 1))]
                if kind == "mix" and key[2] == 0:
                    return [(s_merged, 8 * key[1] + k + 1)]
                if kind == "fo" and key[3] == 0:
                    return [(s_hid, FFN_TILES * key[1] + FFN_CHUNKS[key[2]][0] + k + 1)]
                if kind == "fo2" and key[2] == 0:
                    return [(s_hid, FFN_TILES * DEPTH + FF2_CHUNKS[key[1]][0] + k + 1)]
                if kind == "kvd":
                    return [(s_p["out"], by_key["p2", "ckv"]["out"])]
                if key == ("iq", 0):
                    return [(s_p["out"], by_key["p2", "cq1"]["out"])]
                if kind == "out2" and key[1] == 0:
                    return [(s_oe, group_total["mixer2"])]
                if kind == "xo" and key[1] == 0:
                    return [(s_oe, group_total["x"])]
                return []

            def square_mean(name):
                pe.wait_ge(s_sqm, (KD - 1) * (NORMS[name] + 1))
                blocks = MEM // P if name == "mem" else NB
                for b in range(blocks):
                    ins = pe.matmul(psS[:, 0, b:b + 1], tmp[:, 2, b * P:(b + 1) * P], ones[:, 0:1], start=True, stop=True)
                ins.then_inc(s_ms, 1)

            def spread_root(name, cols=SEQ):
                pe.wait_ge(s_dg, NORMS[name] + 1)
                pe.matmul(psO[:, 0:cols], ones, tmp[:, 0, 0:cols], start=True, stop=True).then_inc(s_rr, 1)

            def positions_to_partitions(f):
                l, ft = divmod(f, FEATURE_TILES)
                pe.wait_ge(s_took["act"], taken["u", l, ft][1])
                if f:
                    pe.wait_ge(v["wt_sb"], f)
                for j in range(SSM_T):
                    ins = pe.transpose(psT[0:SSM_C, j // 4, (j % 4) * P:(j % 4 + 1) * P], uT[:, ft, j::SSM_T], ident)
                ins.then_inc(v["u2"], 1)

            def ssm_step(l, t):
                f, phase = l * FEATURE_TILES + t // 4, t % 4
                ft = t // 4
                if t == -1:
                    positions_to_partitions(f + 1)
                elif phase == 0 and ft <= FEATURE_TILES:
                    if ft:
                        pe.wait_ge(v["yc_sb"], f)
                        for j in range(SSM_T):
                            ins = pe.transpose(psO[:, j * SSM_C:(j + 1) * SSM_C], Y2[:, j],
                                               ident[SSM_C:2 * SSM_C, SSM_C:2 * SSM_C])
                        ins.then_inc(v["yt"], 1)
                    if ft < FEATURE_TILES:
                        pe.wait_ge(v["w1"], f + 1)
                        for g in range(SSM_G):
                            ins = pe.matmul(psS[0:SSM_H, g // 4, (g % 4) * P:(g % 4 + 1) * P], X1[:, g],
                                            W1[:, g, 0:SSM_T, :], start=True, stop=True)
                        ins.then_inc(v["g_out"], 1)
                        pe.wait_ge(v["u2_sb"], f + 1)
                        pe.wait_ge(v["wb"], f + 1)
                        for g in range(SSM_G):
                            ins = pe.transpose(psT[:, g // 4, (g % 4) * P:(g % 4 + 1) * P],
                                               WbE[:, g].rearrange("p a b -> p (a b)"), ident)
                        ins.then_inc(v["wbt"], 1)
                elif phase == 1 and ft < FEATURE_TILES:
                    pe.wait_ge(v["u2_sb"], f + 1)
                    if ft:
                        pe.wait_ge(v["ypre"], f)
                    for g in range(SSM_G):
                        ins = pe.transpose(psO[:, g * SSM_C:(g + 1) * SSM_C], U2[:, g], ident[0:SSM_C, 0:SSM_C])
                    ins.then_inc(v["ug"], 1)
                elif phase == 2 and ft < FEATURE_TILES:
                    pe.wait_ge(v["ug_sb"], f + 1)
                    pe.wait_ge(v["wt_sb"], f + 1)
                    pe.wait_ge(v["g_sb"], f + 1)
                    for g in range(SSM_G):
                        pe.matmul(psS[:, 0, g * SSM_C:(g + 1) * SSM_C], WT[:, g], UG[:, g], start=True, stop=True)
                        ins = pe.matmul(psS[:, 1, g * SSM_C:(g + 1) * SSM_C], WTI[:, g], UG[:, g], start=True, stop=True)
                    ins.then_inc(v["e"], 1)
                    if ft + 1 < FEATURE_TILES:
                        positions_to_partitions(f + 1)
                elif phase == 3 and ft < FEATURE_TILES:
                    pe.wait_ge(v["z"], f + 1)
                    pe.wait_ge(s_toep, 16 * SSM_T * (f + 1))
                    pe.wait_ge(s_w2, 32 * (f + 1))
                    if ft + 1 < FEATURE_TILES:
                        pe.wait_ge(v["u2_sb"], f + 2)
                    for g in range(SSM_G):
                        o = psT[SSM_C:2 * SSM_C, g // 4, (g % 4) * P:(g % 4 + 1) * P]
                        pe.matmul(o, UG[:, g], TO[:, g], start=True, stop=False)
                        pe.matmul(o, z1[:, g], W1[:, g, 1:SSM_T + 1, :], start=False, stop=False)
                        ins = pe.matmul(o, z2[:, g], W2[:, g], start=False, stop=True)
                    ins.then_inc(v["yc"], 1)

            def unit_scores(u):
                n, kind, b, j = u["n"], u["kind"], u["b"], u["j"]
                before = n if kind == "sw" else n - 1
                if before > 0:
                    pe.wait_ge(s_masked, before)
                out = score_banks(u)
                for a in range(2):
                    h = slice(64 * a, 64 * a + 64)
                    q = slice(b * P, (b + 1) * P)
                    k = slice(u["k0"], u["k0"] + u["W"])
                    if kind == "sw":
                        lhs, rhs = qT1[h, j, q], kT1[h, k]
                    elif kind == "dsa":
                        lhs, rhs = qd[h, j, q], kd[h, k]
                    elif kind == "x":
                        lhs, rhs = qx[:, 2 * j + a, q], kx[:, 2 * j + a, :]
                    else:
                        lhs, rhs = qn[h, j, q], {"cmp": kc[h, :], "slc": ks[h, k], "win": kw[h, k]}[kind]
                    ins = pe.matmul(out[:, a], lhs, rhs, start=True, stop=True)
                ins.then_inc(s_sc, 1)

            def unit_transpose(u):
                n = u["n"]
                pe.wait_ge(s_prob, n + 1)
                before = n - 1 if narrow(u) else n
                if before > 0:
                    pe.wait_ge(s_pt, before)
                p, _ = probs(u)
                out = transpose_banks(u)
                for a in range(2):
                    for i, m in key_blocks(u):
                        ins = pe.transpose(out[0:m, a, i * P:(i + 1) * P], p[:, a, i * P:i * P + m], ident)
                ins.then_inc(s_tr, 1)

            def unit_pv(u):
                n, kind, b, j = u["n"], u["kind"], u["b"], u["j"]
                pe.wait_ge(s_pt, n + 1)
                if u["first"] and u["group"]:
                    pe.wait_ge(s_oe, u["group"])
                _, t = probs(u)
                for a in range(2):
                    h = slice(64 * a, 64 * a + 64)
                    blocks = key_blocks(u)
                    for i, m in blocks:
                        kb = u["k0"] // P + i
                        if kind == "x":
                            o, lhs = psO[:, a * P:(a + 1) * P], vx[:, i, (2 * j + a) * P:(2 * j + a + 1) * P]
                        else:
                            o = psO[h, 0:P]
                            lhs = {"sw": lambda: vt1[:, kb, h], "dsa": lambda: vd[:, kb, :], "cmp": lambda: vc[0:m, h],
                                   "slc": lambda: vs[:, kb, h], "win": lambda: vw[:, kb, h]}[kind]()
                        ins = pe.matmul(o, lhs, t[0:m, a, i, :], start=(u["first"] and i == 0),
                                        stop=(u["last"] and i == blocks[-1][0]))
                ins.then_inc(s_pv, 1)

            def indexer_head(b, h):
                n = (NB - 1 - b) * 8 + h
                W = (b + 1) * P
                hh = slice(64 * (h % 2), 64 * (h % 2) + 64)
                if n:
                    pe.wait_ge(s_ir, n)
                pe.matmul(psG[:, 2, 0:W], qi[hh, h // 2, b * P:(b + 1) * P], ki[hh, 0:W],
                          start=True, stop=True).then_inc(s_is, 1)

            def attention(us, side=None):
                la = ahead(us[0]) + 1
                for u in us[:la]:
                    unit_scores(u)
                for i, u in enumerate(us):
                    if i + la < len(us):
                        unit_scores(us[i + la])
                    if side:
                        side(i, 0)
                    unit_transpose(u)
                    if i:
                        unit_pv(us[i - 1])
                    if side:
                        side(i, 1)
                unit_pv(us[-1])

            def unit_step(l, i):
                us = units[f"sw{l}"]
                if i + 1 < UNITS_SW:
                    unit_scores(us[i + 1])
                if 0 <= i < UNITS_SW:
                    unit_transpose(us[i])
                if 1 <= i <= UNITS_SW:
                    unit_pv(us[i - 1])

            def rotate(key):
                r = key[1] * 5 + key[2]
                pe.wait_ge(s_rawt, r + 1)
                pe.matmul(free_bank(key), rots[1], rawt[:, r % 2, :], start=True, stop=True).then_inc(s_rot, 1)

            def values_to_partitions(l):
                out = free_bank(("vt", l))
                pe.wait_ge(s_vraw, l + 1)
                for b in range(NB):
                    ins = pe.transpose(out[:, b * P:(b + 1) * P], tmp[:, 2, b * P:(b + 1) * P], ident)
                ins.then_inc(s_vt, 1)

            def phase_of(p, phase):
                kind = p["kind"]
                N = CMP_N if kind == "cmpk" and phase != "cmp" else SEQ
                rt = cmpt[:, 0] if kind == "cmpk" else raws[p["i"] % 4][:, 0:N]
                sq = tmp[:, p.get("sq_at", 0), 0:N]
                if phase == "cmp":
                    i = 0 if kind == "cmpk" else 1
                    pe.wait_ge(s_p["cmpin"], i + 1)
                    pe.wait_ge(s_cw, 16 * (i + 1))
                    if p["cen"] > 1:
                        pe.wait_ge(s_p["cen"], p["cen"] - 1)
                    for t in range(CMP_L):
                        ins = pe.matmul(psO[:, 0:CMP_N], cmpW[:, t, :], cmpin[:, t, :], start=(t == 0), stop=(t == CMP_L - 1))
                    ins.then_inc(s_p["cmpo"], 1)
                elif phase == "cmean":
                    pe.wait_ge(s_p["raw"], p["raw"])
                    pe.matmul(psT[:, 0, 0:N], blk, rt, start=True, stop=True).then_inc(s_p["cmean"], 1)
                elif phase == "mean":
                    if "sqa" in p:
                        pe.wait_ge(s_p["sqa"], p["sqa"])
                    else:
                        pe.wait_ge(s_p["sqd"], p["sqd"])
                    if p["sd"] > 1:
                        pe.wait_ge(s_p["sd"], p["sd"] - 1)
                    if kind == "lat2":
                        pe.matmul(psT[:, 1, 0:N], ones, tmp[:, posts[p["i"] - 1]["sq_at"], 0:N], start=True, stop=False)
                        pe.matmul(psT[:, 1, 0:N], ones, sq, start=False, stop=True).then_inc(s_p["mean"], 1)
                    else:
                        m = ones if kind == "lat1" else blk
                        pe.matmul(psT[:, 1, 0:N], m, sq, start=True, stop=True).then_inc(s_p["mean"], 1)
                elif phase == "query":
                    pe.wait_ge(s_p["sqa"], p["sqa"])
                    if p["sd"] > 1:
                        pe.wait_ge(s_p["sd"], p["sd"] - 1)
                    w, m = (2, blk[:, 0::HEAD]) if kind == "qrms" else (1, ones[:, 0:1])
                    for b in range(NB):
                        ins = pe.matmul(psT[:, 1, b * w:(b + 1) * w], sq[:, b * P:(b + 1) * P], m, start=True, stop=True)
                    ins.then_inc(s_p["mean"], 1)
                    if kind == "qrms":
                        pe.wait_ge(s_p["raw"], p["raw"])
                        if p["rotd"] > 1:
                            pe.wait_ge(s_p["rotd"], p["rotd"] - 1)
                        pe.matmul(psS[:, 1, 0:N], rots[2], rt, start=True, stop=True).then_inc(s_p["rot"], 1)
                elif phase == "rot":
                    if "qn" in p:
                        pe.wait_ge(s_p["qn"], p["qn"])
                    else:
                        pe.wait_ge(s_p["raw"], p["raw"])
                    if p["rotd"] > 1:
                        pe.wait_ge(s_p["rotd"], p["rotd"] - 1)
                    pe.matmul(psS[:, 1, 0:N], rots[2], rt, start=True, stop=True).then_inc(s_p["rot"], 1)
                elif phase == "tok":
                    if kind == "cmpv":
                        pe.wait_ge(s_p["cen"], p["cen"])
                    else:
                        pe.wait_ge(s_p["raw"], p["raw"])
                    if p["toksb"] > 1:
                        pe.wait_ge(s_p["toksb"], p["toksb"] - 1)
                    if kind == "cmpv":
                        ins = pe.transpose(psS[0:CMP_N, 0, 0:P], cmpt[:, 1], ident)
                    else:
                        for i in range(NB):
                            ins = pe.transpose(psS[:, 0, i * P:(i + 1) * P], rt[:, i * P:(i + 1) * P], ident)
                    ins.then_inc(s_p["tok"], 1)

            def project(ps):
                for new, old in waves(ps):
                    if new:
                        product(new["key"])
                    for p, phase in old:
                        phase_of(p, phase)

            def memory_keys_mean(j):
                pe.wait_ge(s_kxsq, j + 1)
                if j:
                    pe.wait_ge(s_kxsd, j)
                pe.matmul(psT[:, 0, 0:MEM], ones, xsq[:, j % 2], start=True,
                          stop=True).then_inc(s_kxms, 1)

            def memory_values_transpose(j):
                pe.wait_ge(s_xtr_in, j + 1)
                if j:
                    pe.wait_ge(s_vx, j)
                for i in range(2):
                    ins = pe.transpose(psT[:, 1, i * P:(i + 1) * P],
                                       xraw[:, j % 2, i * P:(i + 1) * P], ident)
                ins.then_inc(s_xtr, 1)

            pe.wait_ge(s_mats, 16)
            for l in range(DEPTH):
                if l == 0:
                    square_mean("mix0")
                spread_root(f"mix{l}")
                for what, key in mixer_plan(l):
                    if what == "ssm":
                        ssm_step(l, key)
                    elif what == "unit":
                        unit_step(l, key)
                    elif what == "scale":
                        pass
                    elif key[0] == "rot":
                        rotate(key)
                    elif key[0] == "vt":
                        values_to_partitions(l)
                    else:
                        product(key)
                for i in range(KD):
                    product(("mix", l, i))
                square_mean(f"ffn{l}")
                spread_root(f"ffn{l}")
                for c, (t0, nt) in enumerate(FFN_CHUNKS):
                    for t in range(t0, t0 + nt):
                        product(("gt", l, t))
                        if l == DEPTH - 1 and c == 1 and t < t0 + 5:
                            if t == t0 + 3:
                                square_mean("mem")
                            elif t == t0 + 4:
                                spread_root("mem", MEM)
                        product(("up", l, t))
                    for i in range(KD):
                        product(("fo", l, c, i))
                square_mean(NEXT_NORM[l])
            product(("xk", 0))
            spread_root("final")
            product(("xk", 1))
            memory_keys_mean(0)
            product(("xk", 2))
            memory_keys_mean(1)
            product(("xk", 3))
            memory_keys_mean(2)
            product(("xv", 0))
            square_mean("norm1")
            memory_keys_mean(3)
            for j in range(1, XHEADS):
                product(("xv", j))
                if j == 1:
                    spread_root("norm1")
                memory_values_transpose(j - 1)
            memory_values_transpose(XHEADS - 1)
            project(block2_posts)
            pe.wait_ge(s_p["out"], block2_done["out"])
            pe.wait_ge(s_p["toksb"], block2_done["toksb"])
            attention(units2, lambda i, w: indexer_head(*beside(i, w)) if beside(i, w) and beside(i, w)[1] < 8 else None)
            for i in range(KD):
                product(("out2", i))
            square_mean("norm2")
            spread_root("norm2")
            project(x_posts)
            pe.wait_ge(s_p["out"], all_done["out"])
            pe.wait_ge(s_kxn, XHEADS)
            attention(units["x"])
            for i in range(KD):
                product(("xo", i))
            square_mean("norm3")
            spread_root("norm3")
            for c, (t0, nt) in enumerate(FF2_CHUNKS):
                for t in range(t0, t0 + nt):
                    product(("fi", t))
                for i in range(KD):
                    product(("fo2", c, i))

        @block.scalar
        def _(act):
            line = Line(act, c_act)
            do = line.done
            act.dma_start(PAR[:, :], params).then_inc(s_par, 16)
            act.dma_start(eig, ssmp[0][:, 0:3 * SSM_GROUPS]).then_inc(s_ssm0, 16)
            for i in range(2):
                act.dma_start(sp[i], ssmp[0][:, 3 * GR + SSM_BC * i:3 * GR + SSM_BC * (i + 1)]).then_inc(s_ssmp[i], 16)
            act.dma_start(CON[:, 0:MATS_N], consts[:, 0:MATS_N]).then_inc(s_mats, 16)
            act.wait_ge(s_par, 16)

            def from_bank(key):
                n = number[key]
                act.wait_ge(s_job, tile_of[key] + 1)
                return psG[:, n % GEMM_BANKS, 0:jobs[n][2]]

            def square(name, k):
                n = KD * NORMS[name] + k
                cols = SEQ
                if name == "mix0":
                    act.wait_ge(s_x[k // 2], 16)
                elif name == "mem":
                    act.wait_ge(s_mem, 16)
                    cols = MEM
                elif name == "norm1":
                    act.wait_ge(s_fin, k + 1)
                else:
                    act.wait_ge(s_took["dve"], taken[last_product[name] + (k,)][1])
                if k >= 3:
                    act.wait_ge(s_sqm, (KD - 1) * NORMS[name] + k - 2)
                src = memf[:, k] if name == "mem" else X[:, k]
                dest = sqr[:, k % 2, 0:cols] if k else tmp[:, 2, 0:cols]
                do(act.activation(dest, src, ACT.Square), s_sqk)

            def root(name):
                blocks = MEM // P if name == "mem" else NB
                act.wait_ge(s_ms, NORMS[name] + 1)
                do(act.activation(root_tok[:, 0:blocks], psS[:, 0, 0:blocks], ACT.Sqrt, bias=eps), s_sd)

            def squares_and_root(name):
                do(act.activation(stat[:, 3, 11:12], eps, ACT.Sqrt))
                for k in range(KD):
                    square(name, k)
                root(name)

            def high_parts(name):
                for k in range(KD):
                    n = KD * h_norm[name] + k + 1
                    act.wait_ge(s_xs, n)
                    act.activation(Hh[:, k], tmp[:, k % 3, :], ACT.Copy).then_inc(s_hh, 1)

            def eigen_exp(l):
                act.wait_ge(s_ssm0, 16 * (l + 1))
                do(act.activation(sm[:, 0], eig[:, 2], ACT.Exp), v["dt"])

            def magnitudes(l):
                act.wait_ge(v["args"], 2 * l + 1)
                do(act.activation(mag, mag, ACT.Exp), v["coef"])

            def sines(l):
                act.wait_ge(v["args"], 2 * l + 2)
                do(act.activation(snA, arg[:, :, 0:9], ACT.Sin))
                do(act.activation(csA, arg2[:, :, 0:9], ACT.Sin))
                do(act.activation(snB, arg[:, :, 9:], ACT.Sin))
                do(act.activation(csB, arg2[:, :, 9:], ACT.Sin), v["coef"])

            def ssm_step(l, t):
                f, phase = l * FEATURE_TILES + t // 4, t % 4
                ft = t // 4
                if t == -1:
                    inputs_copy(f + 1)
                elif phase == 0 and ft < FEATURE_TILES:
                    act.wait_ge(v["w1"], f + 1)
                    act.wait_ge(v["g_out"], f + 1)
                    lo, up = slice(0, SSM_STATE), slice(SSM_STATE, P)
                    act.dma_start(W2[lo], W1[up, :, 1:SSM_T + 1, :]).then_inc(s_w2, 16)
                    act.dma_start(W2[up], W1[lo, :, 1:SSM_T + 1, :]).then_inc(s_w2, 16)
                    act.wait_ge(v["wbt"], f + 1)
                    do(act.activation(Gm, psS[0:SSM_H, :, :].rearrange("p a (g x) -> p (a g) x", g=4), ACT.Copy), v["g_sb"])
                    act.wait_ge(v["toep_clear"], l + 1)
                    for j in range(SSM_T):
                        act.dma_start(TO[j * SSM_H:(j + 1) * SSM_H, :, j * SSM_H:],
                                      Gm[:, :, 0:(SSM_T - j) * SSM_H]).then_inc(s_toep, 16)
                    w = psT[:, :, :].rearrange("p a (g x) -> p (a g) x", g=4)
                    do(act.activation(WT, w, ACT.Copy))
                    do(act.activation(WTI[:, :, 0:HEAD], w[:, :, HEAD:P], ACT.Copy))
                    do(act.activation(WTI[:, :, HEAD:P], w[:, :, 0:HEAD], ACT.Copy, scale=-1.0), v["wt_sb"])
                    if ft < 2:
                        i = 3 * GR + SSM_BC * (ft + 2)
                        act.dma_start(sp[ft], ssmp[l][:, i:i + SSM_BC]).then_inc(s_ssmp[ft], 16)
                elif phase == 1:
                    if ft < FEATURE_TILES:
                        act.wait_ge(v["ug"], f + 1)
                        do(act.activation(UG[:, :, :].rearrange("p a b -> p (a b)"), psO[:, :], ACT.Copy), v["ug_sb"])
                    if ft:
                        act.wait_ge(v["ypre"], f)
                        do(act.activation(ysf[:, ft - 1], ysf[:, ft - 1], ACT.Gelu_apprx_tanh), v["ys"])
                elif phase == 2 and ft + 1 < FEATURE_TILES:
                    inputs_copy(f + 1)
                elif phase == 3 and ft < FEATURE_TILES:
                    act.wait_ge(v["yc"], f + 1)
                    by_group = Y2.rearrange("c j (g h) -> c g j h", h=SSM_H)
                    for i, s_i in ((0, None), (1, v["yc_sb"])):
                        do(act.activation(by_group[:, 4 * i:4 * i + 4],
                                          psT[SSM_C:2 * SSM_C, i, :].rearrange("c (g j h) -> c g j h", j=SSM_T, h=SSM_H),
                                          ACT.Copy), s_i)

            def inputs_copy(f):
                act.wait_ge(v["u2"], f + 1)
                by_position = U2.rearrange("c g (j h) -> c j g h", h=SSM_H)
                for i, s_i in ((0, None), (1, v["u2_sb"])):
                    do(act.activation(by_position[:, 4 * i:4 * i + 4],
                                      psT[0:SSM_C, i, :].rearrange("c (j g h) -> c j g h", g=SSM_G, h=SSM_H), ACT.Copy), s_i)

            def unit_exp(u):
                n, kind = u["n"], u["kind"]
                st = stats(u)
                p, _ = probs(u)
                act.wait_ge(s_neg, n + 1)
                scale = [1.0, 1.0] if kind == "sw" else [query_factors(u)[:, a:a + 1] for a in range(2)]
                do(act.activation(p[:, 0], p[:, 0], ACT.Exp, bias=st[:, 2:3], scale=scale[0], accum_out=st[:, 4:5]))
                ins = act.activation(p[:, 1], p[:, 1], ACT.Exp, bias=st[:, 3:4], scale=scale[1], accum_out=st[:, 5:6])
                if kind == "sw":
                    do(ins)
                    ins = act.activation(st[:, 6:8], st[:, 6:8], ACT.Exp)
                do(ins, s_exp)

            def unit_copy(u):
                n = u["n"]
                act.wait_ge(s_tr, n + 1)
                if n >= 2:
                    act.wait_ge(s_pv, n - 1)
                _, t = probs(u)
                m, w = (CMP_N, 1) if u["kind"] == "cmp" else (P, u["W"] // P)
                src = transpose_banks(u)[0:m, :, 0:w * P].rearrange("p a (b c) -> p a b c", c=P)
                do(act.activation(t[0:m, 0, 0:w, :], src[:, 0], ACT.Copy))
                do(act.activation(t[0:m, 1, 0:w, :], src[:, 1], ACT.Copy), s_pt)

            def indexer_head(b, h):
                n = (NB - 1 - b) * 8 + h
                W = (b + 1) * P
                act.wait_ge(s_is, n + 1)
                if n >= 2:
                    act.wait_ge(s_ia, n - 1)
                do(act.activation(irelu[:, h % 2, 0:W], psG[:, 2, 0:W], ACT.Relu), s_ir)

            def attention(us, side=None):
                la = ahead(us[0])
                for u in us[:la]:
                    unit_exp(u)
                for i, u in enumerate(us):
                    if side:
                        side(i, 0)
                    unit_copy(u)
                    if side:
                        side(i, 1)
                    if i + la < len(us):
                        unit_exp(us[i + la])

            def take(p):
                bank = from_bank(p["key"])
                rt = raws[p["i"] % 4]
                if p["i"] >= 4:
                    prev = posts[p["i"] - 4]
                    if prev["kind"] == "lat":
                        prev = posts[p["i"] - 3]
                    for n in (("cmpin",) if "cmpin" in prev else ("out", "toksb")):
                        if n in prev:
                            act.wait_ge(s_p[n], prev[n])
                if "sqa" in p:
                    if p["tile"] is None:
                        do(act.activation(rt, bank, ACT.Copy), s_p["raw"])
                    else:
                        do(act.activation(rt if p["kind"] == "qrms" else p["dest"], bank, ACT.Copy,
                                          scale=par(*p["gain"])), s_p["raw"])
                    if p["sq_wait"]:
                        act.wait_ge(s_p["mean"], p["sq_wait"]["mean"])
                    do(act.activation(tmp[:, p["sq_at"], :], bank, ACT.Square), s_took["act"])
                    act.sem_inc(s_p["sqa"], 1)
                else:
                    do(act.activation(rt, bank, ACT.Copy), s_took["act"])
                    act.sem_inc(s_p["raw"], 1)

            def phase_of(p, phase):
                kind = p["kind"]
                N = CMP_N if kind == "cmpk" else SEQ
                if phase == "mean":
                    act.wait_ge(s_p["mean"], p["mean"])
                    if p["sd"] > 2:
                        q = next(q for q in posts if q.get("sd") == p["sd"] - 2)
                        act.wait_ge(s_p["qn" if "qn" in q else "out"], q["qn" if "qn" in q else "out"])
                    scale = {"lat2": 4.0, "lat1": 8.0}.get(kind, 1.0)
                    do(act.activation(roots[p["sd"] % 2][:, 0:N], psT[:, 1, 0:N], ACT.Sqrt, bias=eps, scale=scale), s_p["sd"])
                elif phase == "query":
                    act.wait_ge(s_p["mean"], p["mean"])
                    if kind == "qrms":
                        src = psT[:, 1, 0:2 * NB].rearrange("p (b h) -> p b h", h=2)
                        do(act.activation(qs[:, p["tile"]], src, ACT.Sqrt, bias=eps), s_p["sd"])
                    else:
                        do(act.activation(xs[:, p["tile"]], psT[:, 1, 0:NB], ACT.Sqrt, bias=eps, scale=8.0), s_p["sd"])
                elif phase == "tok":
                    act.wait_ge(s_p["tok"], p["tok"])
                    t = psS[:, 0, :].rearrange("p (b c) -> p b c", c=P)
                    if kind == "tok":
                        do(act.activation(p["dest"], t, ACT.Copy), s_p["toksb"])
                    elif kind == "tokd":
                        do(act.activation(vd, t[:, :, HEAD:P], ACT.Copy), s_p["toksb"])
                    elif kind == "tokwg":
                        do(act.activation(wtok[:, :, :], t[:, :, 0:8], ACT.Copy, scale=IDX_SCALE))
                        do(act.activation(gtok[:, :, :], t[:, :, 104:128], ACT.Sigmoid), s_p["toksb"])
                    elif kind == "cmpv":
                        do(act.activation(vc[0:CMP_N, :], psS[0:CMP_N, 0, 0:P], ACT.Copy), s_p["toksb"])

            def project(ps):
                for new, old in waves(ps):
                    if new:
                        take(new)
                    for p, phase in old:
                        phase_of(p, phase)
                        if p["kind"] == "cmpk" and phase == "mean":
                            act.wait_ge(s_p["cmpo"], 1)
                            act.dma_start(cmpW.rearrange("p a b -> p (a b)"), cmpw[1]).then_inc(s_cw, 16)

            def memory_keys_take(j):
                bank = from_bank(("xk", j))
                do(act.activation(kx[:, j], bank, ACT.Copy), s_kx)
                if j >= 2:
                    act.wait_ge(s_kxms, j - 1)
                do(act.activation(xsq[:, j % 2], bank, ACT.Square), s_took["act"])
                act.sem_inc(s_kxsq, 1)

            def memory_keys_root(j):
                act.wait_ge(s_kxms, j + 1)
                do(act.activation(xsd[:, j], psT[:, 0, 0:MEM], ACT.Sqrt, bias=eps, scale=8.0), s_kxsd)

            def memory_values_take(j):
                bank = from_bank(("xv", j))
                if j >= 2:
                    act.wait_ge(s_xtr, j - 1)
                do(act.activation(xraw[:, j % 2], bank, ACT.Copy), s_took["act"])
                act.sem_inc(s_xtr_in, 1)

            def memory_values_copy(j):
                act.wait_ge(s_xtr, j + 1)
                src = psT[:, 1, 0:MEM].rearrange("p (b c) -> p b c", c=P)
                do(act.activation(vx[:, :, j * P:(j + 1) * P], src, ACT.Copy), s_vx)

            def unit_step(l, i):
                us = units[f"sw{l}"]
                if 0 <= i < UNITS_SW:
                    unit_copy(us[i])
                if i + 1 < UNITS_SW:
                    unit_exp(us[i + 1])

            def take_mixer(key):
                kind, l = key[0], key[1]
                if kind == "u":
                    do(act.activation(uT[:, key[2]], from_bank(key), ACT.Copy), s_took["act"])
                elif kind in ("q", "k"):
                    r = l * 5 + (key[2] if kind == "q" else 4)
                    bank = from_bank(key)
                    if r >= 2:
                        act.wait_ge(s_rope, r - 1)
                    do(act.activation(rawt[:, r % 2, :], bank, ACT.Copy, scale=HEAD ** -0.5 if kind == "q" else 1.0),
                       s_took["act"])
                    act.sem_inc(s_rawt, 1)
                elif kind == "v":
                    do(act.activation(tmp[:, 2, :], from_bank(key), ACT.Copy), s_took["act"])
                    act.sem_inc(s_vraw, 1)
                elif kind == "vt":
                    act.wait_ge(s_vt, l + 1)
                    bank = psG[:, number[key] % GEMM_BANKS, :]
                    do(act.activation(vt1[:, :, :].rearrange("p a b -> p (a b)"), bank, ACT.Copy), s_took["act"])
                    act.sem_inc(s_vtok, 1)
                elif kind == "cc":
                    bank = from_bank(key)
                    i = key[2]
                    act.wait_ge(*((s_cy, 4 * l + i) if i else (s_rope, 5 * (l + 1))))
                    do(act.activation(tmp[:, 0, :], bank, ACT.Copy), s_took["act"])
                elif kind == "glu":
                    bank = from_bank(key)
                    i = key[2]
                    act.wait_ge(*((v["glu_out"], 4 * l + i) if i else (s_cy, 4 * (l + 1))))
                    do(act.activation(tmp[:, 0, :], bank, ACT.Sigmoid), s_took["act"])
                elif kind in ("g0", "g1", "g2"):
                    bank = from_bank(key)
                    n = gate_number(key)
                    if n >= 2:
                        act.wait_ge(s_sig, n - 1)
                    do(act.activation(rawt[:, n % 2, :], bank, ACT.Sigmoid, bias=par(("b_gate", l), int(kind[1]) * KD + key[2])),
                       s_took["act"])

            eigen_exp(0)
            magnitudes(0)
            for l in range(DEPTH):
                squares_and_root(f"mix{l}")
                high_parts(f"mix{l}")
                if l == 0:
                    sines(0)
                for what, key in mixer_plan(l):
                    if what == "ssm":
                        ssm_step(l, key)
                    elif what == "unit":
                        unit_step(l, key)
                    elif what == "job":
                        take_mixer(key)
                squares_and_root(f"ffn{l}")
                high_parts(f"ffn{l}")
                if l == DEPTH - 1:
                    act.dma_start(memf, memT).then_inc(s_mem, 16)
                    act.dma_start(CON[:, CONST_AT["C1"]:CONST_AT["C1"] + 2 * SEQ], rope2).then_inc(s_rope2, 16)
                else:
                    act.dma_start(eig, ssmp[l + 1][:, 0:3 * GR]).then_inc(s_ssm0, 16)
                    for i in range(2):
                        at = 3 * GR + SSM_BC * i
                        act.dma_start(sp[i], ssmp[l + 1][:, at:at + SSM_BC]).then_inc(s_ssmp[i], 16)
                for t in range(FFN_TILES):
                    at = t - FFN_CHUNKS[1][0]
                    if l == DEPTH - 1 and 0 <= at < 4:
                        square("mem", 2 * at)
                        square("mem", 2 * at + 1)
                    elif l == DEPTH - 1 and at == 4:
                        root("mem")
                    if l + 1 < DEPTH:
                        if t == 2:
                            eigen_exp(l + 1)
                        elif t == 5:
                            magnitudes(l + 1)
                        elif t == 13:
                            sines(l + 1)
                    bank = from_bank(("gt", l, t))
                    n = FFN_TILES * l + t
                    if n >= 2:
                        act.wait_ge(s_hid, n - 1)
                    do(act.activation(rawt[:, n % 2, :], bank, ACT.Silu), s_took["act"])
            squares_and_root("final")
            memory_keys_take(0)
            memory_keys_take(1)
            memory_keys_root(0)
            for k in range(4):
                square("norm1", k)
            memory_keys_take(2)
            memory_keys_root(1)
            for k in range(4, KD):
                square("norm1", k)
            memory_keys_take(3)
            memory_keys_root(2)
            memory_values_take(0)
            root("norm1")
            memory_keys_root(3)
            for j in range(1, XHEADS):
                memory_values_take(j)
                memory_values_copy(j - 1)
            memory_values_copy(XHEADS - 1)
            high_parts("norm1")
            act.dma_start(cmpW.rearrange("p a b -> p (a b)"), cmpw[0]).then_inc(s_cw, 16)
            project(block2_posts)
            attention(units2, lambda i, w: indexer_head(*beside(i, w)) if beside(i, w) and beside(i, w)[1] < 8 else None)
            squares_and_root("norm2")
            high_parts("norm2")
            project(x_posts)
            attention(units["x"])
            squares_and_root("norm3")
            high_parts("norm3")
            for t in range(32):
                bank = from_bank(("fi", t))
                n = FFN_TILES * DEPTH + t
                act.wait_ge(s_hid, n - 1)
                do(act.activation(rawt[:, n % 2, :], bank, ACT.Relu), s_took["act"])

        @block.vector
        def _(dve):
            line = Line(dve, c_dve)
            do = line.done

            def from_bank(key):
                n = number[key]
                dve.wait_ge(s_job, tile_of[key] + 1)
                return psG[:, n % GEMM_BANKS, 0:jobs[n][2]]

            def tt(out, a, b, op, s=None):
                do(dve.tensor_tensor(out, a, b, op), s)

            def stt(out, a, s_, b, op0, op1, s=None):
                do(dve.scalar_tensor_tensor(out, a, s_, b, op0, op1), s)

            def ts(out, a, s1, s2, op0, op1=None, s=None):
                do(dve.tensor_scalar(out, a, s1, s2, op0, op1) if op1 is not None
                   else dve.tensor_scalar(out, a, s1, None, op0), s)

            def split(hi, lo, src, s):
                do(dve.tensor_copy(hi, src))
                tt(lo, src, hi.bitcast(F32), ALU.subtract, s)

            def add_square(name, k):
                if k:
                    n = MEM if name == "mem" else SEQ
                    dve.wait_ge(s_sqk, KD * NORMS[name] + k + 1)
                    tt(tmp[:, 2, 0:n], tmp[:, 2, 0:n], sqr[:, k % 2, 0:n], ALU.add, s_sqm)

            def inverse_root(name):
                blocks = MEM // P if name == "mem" else NB
                r = root_tok[:, 0:blocks]
                dve.wait_ge(s_sd, NORMS[name] + 1)
                do(dve.reciprocal(r, r))
                ts(r, r, float(D_MODEL), None, ALU.mult)
                tt(tmp[:, 0, 0:blocks * P].rearrange("p (b c) -> p b c", c=P), ident.unsqueeze(1).to_broadcast([P, blocks, P]),
                   r.unsqueeze(2).to_broadcast([P, blocks, P]), ALU.mult, s_dg)
                dve.wait_ge(s_rr, NORMS[name] + 1)

            def normalise(name, gain):
                inverse_root(name)
                rinv = psO
                if name == "final":
                    for k in range(KD):
                        dve.scalar_tensor_tensor(X[:, k], X[:, k], par(gain, k), rinv[:, :], ALU.mult, ALU.mult).then_inc(s_fin, 1)
                    return
                base = h_norm[name]

                def low_part(k):
                    dve.wait_ge(s_hh, KD * base + k + 1)
                    dve.tensor_tensor(Hl[:, k], tmp[:, k % 3, :], Hh[:, k].bitcast(F32), ALU.subtract).then_inc(s_h, 1)

                for k in range(KD):
                    if k >= 3:
                        dve.wait_ge(*((s_h, KD // 2 * base + (k - 3) // 2 + 1) if k % 2 else
                                      (s_hp, KD // 2 * base + (k - 3) // 2 + 1)))
                    dve.scalar_tensor_tensor(tmp[:, k % 3, :], X[:, k], par(gain, k), rinv[:, :],
                                             ALU.mult, ALU.mult).then_inc(s_xs, 1)
                    if k % 2:
                        low_part(k - 1)
                dve.wait_ge(s_h, KD // 2 * (base + 1))
                dve.wait_ge(s_hp, KD // 2 * (base + 1))
                dve.wait_ge(s_xs, KD * (base + 1))

            def memory_normalise():
                inverse_root("mem")
                for k in range(KD):
                    t = tmp[:, 1, 0:MEM]
                    stt(t, memf[:, k], par("mem_norm", k), psO[:, 0:MEM], ALU.mult, ALU.mult)
                    split(mH[:, k], mL[:, k], t, s_m)

            def residual(key, i, norm=None):
                bank = from_bank(key)
                tt(X[:, i], X[:, i], bank, ALU.add, s_took["dve"])
                if norm and i:
                    add_square(norm, i - 1)
                if norm and i == KD - 1:
                    add_square(norm, i)

            def reduce_angle(a):
                big = 1.5 * 2.0 ** 23
                ts(red, a, 1.0 / (2 * math.pi), big, ALU.mult, ALU.add)
                ts(red, red, big, None, ALU.subtract)
                for c in (6.28125, 1.93500518798828125e-3, 3.01991598195675286e-7):
                    stt(a, red, -c, a, ALU.mult, ALU.add)
                ts(a, a, 3.1415925, -3.1415925, ALU.min, ALU.max)

            def reduce_small(a):
                big = 1.5 * 2.0 ** 23
                t = sm[:, 15]
                ts(t, a, 1.0 / (2 * math.pi), big, ALU.mult, ALU.add)
                ts(t, t, big, None, ALU.subtract)
                for c in (6.28125, 1.93500518798828125e-3, 3.01991598195675286e-7):
                    stt(a, t, -c, a, ALU.mult, ALU.add)

            def coefficient_angles(l):
                are, aim = eig[:, 0], eig[:, 1]
                dve.wait_ge(v["dt"], l + 1)
                dt, ar, th, t8, t64 = (sm[:, i] for i in range(5))
                tt(ar, are, dt, ALU.mult)
                tt(th, aim, dt, ALU.mult)
                tt(mag, ar.unsqueeze(2).to_broadcast([P, GR, 9]), J.unsqueeze(1).to_broadcast([P, GR, 9]), ALU.mult, v["args"])
                reduce_small(th)
                ts(t8, th, 8.0, None, ALU.mult)
                reduce_small(t8)
                ts(t64, t8, 8.0, None, ALU.mult)
                reduce_small(t64)
                for a, n, c in ((th, 9, 0), (t8, 8, 9), (t64, 8, 17)):
                    tt(arg[:, :, c:c + n], a.unsqueeze(2).to_broadcast([P, GR, n]),
                       J[:, 0:n].unsqueeze(1).to_broadcast([P, GR, n]), ALU.mult)

            def coefficient_sine():
                reduce_angle(arg)

            def coefficient_cosine():
                ts(arg2, arg, math.pi / 2, None, ALU.add)
                reduce_angle(arg2)
                dve.sem_inc(v["args"], 1)

            def coefficients(l):
                are, aim = eig[:, 0], eig[:, 1]
                dve.wait_ge(v["coef"], 2 * l + 2)
                tt(Lr, mag, csA, ALU.mult)
                tt(Li, mag, snA, ALU.mult)
                do(dve.tensor_copy(mag8, mag[:, :, 8]))
                ta, tb, inv, nr = (sm[:, i] for i in range(5, 9))
                ni = Li[:, :, 1]
                tt(ta, are, are, ALU.mult)
                tt(tb, aim, aim, ALU.mult)
                tt(ta, ta, tb, ALU.add)
                do(dve.reciprocal(inv, ta))
                ts(nr, Lr[:, :, 1], -1.0, None, ALU.add)
                tt(cr, nr, are, ALU.mult)
                tt(ta, ni, aim, ALU.mult)
                tt(cr, cr, ta, ALU.add)
                tt(cr, cr, inv, ALU.mult)
                tt(ci, ni, are, ALU.mult)
                tt(ta, nr, aim, ALU.mult)
                tt(ci, ci, ta, ALU.subtract)
                tt(ci, ci, inv, ALU.mult)
                bc = lambda a: a.unsqueeze(2).to_broadcast([P, GR, 8])
                rev = lambda a: a[:, :, 7::-1]
                tt(Lcr, rev(Lr), bc(cr), ALU.mult)
                tt(t3, rev(Li), bc(ci), ALU.mult)
                tt(Lcr, Lcr, t3, ALU.subtract)
                tt(Lci, rev(Lr), bc(ci), ALU.mult)
                tt(t3, rev(Li), bc(cr), ALU.mult)
                tt(Lci, Lci, t3, ALU.add)

            def groups(ft):
                return slice(ft * SSM_G, (ft + 1) * SSM_G)

            jh = lambda a, n: a.unsqueeze(3).to_broadcast([P, a.shape[1], n, SSM_H])
            hj = lambda a, n: a.unsqueeze(2).to_broadcast([P, a.shape[1], n, SSM_H])

            def build_inputs(f, scratch):
                l, ft = divmod(f, FEATURE_TILES)
                s = sp[ft % 2]
                y1, y2, c1, c2 = (s[:, i * P:(i + 1) * P].rearrange("p (g h) -> p g h", g=SSM_G) for i in range(4))
                bc = lambda a: a[:, groups(ft)].unsqueeze(2).to_broadcast([P, SSM_G, SSM_H])
                dve.wait_ge(s_ssmp[ft % 2], 16 * (2 * l + ft // 2 + 1))
                ts(Y1n, y2, sgn, -1.0, ALU.mult, ALU.mult)
                ts(Z1, c1, sgn, None, ALU.mult)
                ts(Z2, c2, -1.0, None, ALU.mult)
                tt(X1, y1, bc(cr), ALU.mult)
                tt(t4, Y1n, bc(ci), ALU.mult)
                tt(X1, X1, t4, ALU.add)
                pw = scratch.rearrange("p (g j h) -> p g j h", g=SSM_G, j=SSM_T)
                tt(WbE, jh(Lcr[:, groups(ft)], 8), hj(y1, 8), ALU.mult)
                tt(pw, jh(Lci[:, groups(ft)], 8), hj(Y1n, 8), ALU.mult)
                tt(WbE, WbE, pw, ALU.add, v["wb"])

            def build_outputs(f, scratch):
                ft = f % FEATURE_TILES
                half = SSM_G // 2
                for i in range(2):
                    g = slice(ft * SSM_G + i * half, ft * SSM_G + (i + 1) * half)
                    w = W1[:, i * half:(i + 1) * half]
                    pw = scratch[:, 0:half * 9 * SSM_H].rearrange("p (g j h) -> p g j h", g=half, j=9)
                    tt(w, jh(Lr[:, g], 9), hj(Z1[:, i * half:(i + 1) * half], 9), ALU.mult)
                    tt(pw, jh(Li[:, g], 9), hj(Z2[:, i * half:(i + 1) * half], 9), ALU.mult)
                    tt(w, w, pw, ALU.add, v["w1"] if i else None)

            def rotations(ft):
                ab = lambda a: a.rearrange("p g (a b) -> p g a b", b=8)
                ea = lambda a: a[:, groups(ft), 8:16].unsqueeze(3).to_broadcast([P, SSM_G, 8, 8])
                eb = lambda a: a[:, groups(ft), 0:8].unsqueeze(2).to_broadcast([P, SSM_G, 8, 8])
                pt = pwork[:, 0:SEQ].rearrange("p (g a b) -> p g a b", g=SSM_G, a=8)
                tt(ab(rotC), ea(csB), eb(csB), ALU.mult)
                tt(pt, ea(snB), eb(snB), ALU.mult)
                tt(ab(rotC), ab(rotC), pt, ALU.subtract)
                tt(ab(rotS), ea(snB), eb(csB), ALU.mult)
                tt(pt, ea(csB), eb(snB), ALU.mult)
                tt(ab(rotS), ab(rotS), pt, ALU.add)

            def states(f):
                ft = f % FEATURE_TILES
                by_group = lambda a: a.rearrange("p (g c) -> p g c", g=SSM_G)
                e0, e1 = by_group(psS[:, 0, :]), by_group(psS[:, 1, :])
                zt, z0 = by_group(pwork[:, 0:SEQ]), by_group(pwork[:, SEQ:2 * SEQ])
                dve.wait_ge(v["e"], f + 1)
                tt(z0, e0, rotC, ALU.mult)
                tt(zt, e1, rotS, ALU.mult)
                tt(z0, z0, zt, ALU.add)
                for g in range(SSM_G):
                    step = mag8[:, ft * SSM_G + g:ft * SSM_G + g + 1].to_broadcast([P, SSM_C])
                    do(dve.tensor_tensor_scan(zt[:, g], step, z0[:, g], 0.0, ALU.mult, ALU.add))
                tt(z1[:, :, 1:], zt[:, :, :-1], rotC[:, :, :-1], ALU.mult)
                stt(z2[:, :, 1:], zt[:, :, :-1], sgn, rotS[:, :, :-1], ALU.mult, ALU.mult, v["z"])

            def ssm_step(l, t):
                f, phase = l * FEATURE_TILES + t // 4, t % 4
                ft = t // 4
                if t == -1:
                    do(dve.memset(z1[:, :, 0:1], 0.0))
                    do(dve.memset(z2[:, :, 0:1], 0.0))
                elif phase == 0:
                    if ft:
                        dve.wait_ge(v["yt"], f)
                        stt(ysf[:, ft - 1].rearrange("p (c j) -> p c j", j=SSM_T),
                            uT[:, ft - 1].rearrange("p (c j) -> p c j", j=SSM_T), par(("ssm_d", l), ft - 1),
                            psO[:, :].rearrange("p (j c) -> p c j", j=SSM_T), ALU.mult, ALU.add, v["ypre"])
                    if ft < FEATURE_TILES:
                        rotations(ft)
                elif phase == 1 and ft + 1 < FEATURE_TILES:
                    dve.wait_ge(s_toep, 16 * SSM_T * (f + 1))
                    build_inputs(f + 1, pwork)
                elif phase == 2 and ft < FEATURE_TILES:
                    states(f)
                elif phase == 3 and ft + 1 < FEATURE_TILES:
                    dve.wait_ge(v["yc"], f + 1)
                    build_outputs(f + 1, pwork)
                if t >= 4 * FEATURE_TILES + 1:
                    for i in ((0, 1, 2) if t == 4 * FEATURE_TILES + 1 else (3,)):
                        dve.wait_ge(v["ys"], l * FEATURE_TILES + i + 1)
                        split(Bh[:, i], Bl[:, i], ysf[:, i], v["ysplit"])

            def prepare(l, part):
                scratch = TO.rearrange("p a b -> p (a b)")
                if part == 0:
                    coefficient_angles(l)
                elif part == 1:
                    coefficient_sine()
                elif part == 2:
                    coefficient_cosine()
                elif part == 3:
                    coefficients(l)
                elif part == 4:
                    build_inputs(l * FEATURE_TILES, scratch)
                elif part == 5:
                    build_outputs(l * FEATURE_TILES, scratch)
                    do(dve.memset(TO, 0.0), v["toep_clear"])

            def unit_max(u):
                n, kind, b, W = u["n"], u["kind"], u["b"], u["W"]
                st = stats(u)
                p, _ = probs(u)
                dve.wait_ge(s_sc, n + 1)
                ring = ahead(u) + 1
                if n >= ring:
                    dve.wait_ge(s_tr, n - ring + 1)
                src = score_banks(u)
                if kind == "sw":
                    mask = con("sw", 2 * P)[:, 2 * P - W:]
                elif kind == "dsa":
                    mask = selected[b][:, 0:W] if b else con("mk", SEQ)[:, SEQ - W:]
                elif kind == "cmp":
                    mask = con("cmp_add", NB * CMP_N)[:, b * CMP_N:(b + 1) * CMP_N]
                else:
                    mask = con("mk", SEQ)[:, SEQ - W:]
                if kind == "x":
                    do(dve.tensor_copy(p, src), s_masked)
                else:
                    tt(p, src, mask.unsqueeze(1).to_broadcast([P, 2, W]), ALU.add, s_masked)
                do(dve.tensor_reduce(st[:, 0:2], p, AX_X, ALU.max))
                if kind == "sw":
                    snk = par(("sinks", u["l"]), 0, 8)[:, u["j"]::4]
                    tt(st[:, 0:2], st[:, 0:2], snk, ALU.max)
                    tt(st[:, 6:8], snk, st[:, 0:2], ALU.subtract)
                    ts(st[:, 2:4], st[:, 0:2], -1.0, None, ALU.mult, None, s_neg)
                else:
                    if kind == "cmp":
                        ts(st[:, 0:2], st[:, 0:2], NEG / 10, None, ALU.max)
                    tt(st[:, 2:4], st[:, 0:2], query_factors(u, -1), ALU.mult, s_neg)

            def unit_scale(u):
                n, kind, b, j = u["n"], u["kind"], u["b"], u["j"]
                st = stats(u)
                p, _ = probs(u)
                dve.wait_ge(s_exp, n + 1)
                den = st[:, 4:6]
                if kind == "sw":
                    tt(den, den, st[:, 6:8], ALU.add)
                if kind == "cmp":
                    mul = con("cmp_mul", NB * CMP_N)[:, b * CMP_N:(b + 1) * CMP_N]
                    tt(p, p, mul.unsqueeze(1).to_broadcast([P, 2, CMP_N]), ALU.mult)
                    do(dve.tensor_reduce(den, p, AX_X, ALU.add))
                    ts(den, den, 1e-30, None, ALU.max)
                if kind in ("cmp", "slc", "win", "dsa"):
                    do(dve.reciprocal(st[:, 8:10], den), s_norm)
                else:
                    do(dve.reciprocal(st[:, 8:10], den))
                    ts(p[:, 0], p[:, 0], st[:, 8:9], None, ALU.mult)
                    ts(p[:, 1], p[:, 1], st[:, 9:10], None, ALU.mult, None, s_prob)

            def unit_out(u):
                if not u["last"]:
                    return
                kind, b, j = u["kind"], u["b"], u["j"]
                dve.wait_ge(s_pv, u["n"] + 1)
                q = slice(b * P, (b + 1) * P)
                if kind == "x":
                    for a in range(2):
                        o = psO[:, a * P:(a + 1) * P]
                        t = 2 * j + a
                        do(dve.tensor_copy(Hh[:, t, q], o))
                        tt(Hl[:, t, q], o, Hh[:, t, q].bitcast(F32), ALU.subtract, s_oe if a else None)
                    return
                hi, lo, t = {"sw": (Bh, Bl, j), "dsa": (Hh, Hl, j)}.get(kind, (Hh, Hl, 4 + j))
                do(dve.tensor_copy(hi[:, t, q], psO[:, 0:P]))
                tt(lo[:, t, q], psO[:, 0:P], hi[:, t, q].bitcast(F32), ALU.subtract, s_oe)

            def unit_step(l, i):
                us = units[f"sw{l}"]
                if 2 <= i < UNITS_SW + 2:
                    unit_out(us[i - 2])
                if i + 1 < UNITS_SW:
                    unit_max(us[i + 1])

            def take_mixer(key):
                kind, l = key[0], key[1]
                if kind == "rot":
                    i = key[2]
                    r = l * 5 + i
                    dve.wait_ge(s_rot, r + 1)
                    dest = qT1[:, i] if i < 4 else kT1
                    tt(tmp[:, 0, :], psG[:, number[key] % GEMM_BANKS, :], tabs[1], ALU.mult, s_took["dve"])
                    tt(tmp[:, 1, :], rawt[:, r % 2, :], tabs[0], ALU.mult)
                    tt(dest, tmp[:, 0, :], tmp[:, 1, :], ALU.add, s_rope)
                elif kind == "cx":
                    i = key[2]
                    dve.wait_ge(s_took["act"], taken["cc", l, i][1])
                    tt(zc[:, 2:], from_bank(key), tmp[:, 0, :], ALU.mult, s_took["dve"])
                    y = tmp[:, 1, :]
                    ts(y, zc[:, 0:SEQ], par(("conv", l), i), None, ALU.mult)
                    stt(y, zc[:, 1:SEQ + 1], par(("conv", l), 4 + i), y, ALU.mult, ALU.add)
                    stt(y, zc[:, 2:SEQ + 2], par(("conv", l), 8 + i), y, ALU.mult, ALU.add)
                elif kind == "cb":
                    i = key[2]
                    y = tmp[:, 1, :]
                    tt(y, from_bank(key), y, ALU.mult, s_took["dve"])
                    split(Bh[:, 4 + i], Bl[:, 4 + i], y, s_cy)
                elif kind == "glu":
                    i = key[2]
                    dve.wait_ge(s_took["act"], taken[key][1])
                    tt(tmp[:, 1, :], tmp[:, 0, :], ysf[:, i], ALU.mult)
                    split(Bh[:, 8 + i], Bl[:, 8 + i], tmp[:, 1, :], v["glu_out"])
                elif kind in ("co", "so", "ao"):
                    i = key[2]
                    gate = ({"co": "g1", "so": "g2", "ao": "g0"}[kind], l, i)
                    n = gate_number(gate)
                    bank = from_bank(key)
                    dve.wait_ge(s_took["act"], taken[gate][1])
                    g = rawt[:, n % 2, :]
                    if kind == "co":
                        tt(partial[:, i], bank, g, ALU.mult, s_took["dve"])
                        dve.sem_inc(s_sig, 1)
                    else:
                        tt(tmp[:, 0, :], bank, g, ALU.mult, s_took["dve"])
                        dve.sem_inc(s_sig, 1)
                        dest = partial[:, i] if kind == "so" else tmp[:, 0, :]
                        tt(dest, partial[:, i], tmp[:, 0, :], ALU.add)
                        if kind == "ao":
                            split(Mh[:, i], Ml[:, i], tmp[:, 0, :], s_merged)

            def indexer_step(b, r):
                W = (b + 1) * P
                if r < 8:
                    dve.wait_ge(s_ir, (NB - 1 - b) * 8 + r + 1)
                    w = wtok[:, b, r:r + 1]
                    if r == 0:
                        ts(iacc[:, 0:W], irelu[:, 0, 0:W], w, None, ALU.mult, None, s_ia)
                    else:
                        stt(iacc[:, 0:W], irelu[:, r % 2, 0:W], w, iacc[:, 0:W], ALU.mult, ALU.add, s_ia)
                    return
                if r == 8:
                    tt(iwork[:, 0:W], iacc[:, 0:W], con("mk", SEQ)[:, SEQ - W:], ALU.add)
                do(dve.max(m8[:, :], iwork[:, 0:W]))
                do(dve.match_replace(iwork[:, 0:W], m8[:, :], iwork[:, 0:W], TAKEN))
                if r == 8 + TOPK // 8 - 1:
                    ts(selected[b][:, 0:W], iwork[:, 0:W], TAKEN / 2, NEG, ALU.is_gt, ALU.mult)

            def attention(us, side=None):
                la = ahead(us[0])
                for u in us[:la]:
                    unit_max(u)
                unit_scale(us[0])
                for i, u in enumerate(us):
                    if i + 1 < len(us):
                        unit_scale(us[i + 1])
                    if i >= 2:
                        unit_out(us[i - 2])
                    if i + la < len(us):
                        unit_max(us[i + la])
                    if side:
                        side(i, 0)
                        side(i, 1)
                unit_out(us[-2])
                unit_out(us[-1])

            def phase_of(p, phase):
                kind = p["kind"]
                N = CMP_N if kind == "cmpk" else SEQ
                rt = cmpt[:, 0] if kind == "cmpk" else raws[p["i"] % 4]
                if phase in ("cmp", "cmean"):
                    if phase == "cmp":
                        dve.wait_ge(s_p["cmpo"], p["cmpo"])
                        do(dve.tensor_copy(cmpt[:, 0 if kind == "cmpk" else 1], psO[:, 0:CMP_N]), s_p["cen"])
                    else:
                        dve.wait_ge(s_p["cmean"], p["cmean"])
                        tt(rt, rt, psT[:, 0, 0:N], ALU.subtract, s_p["cen"])
                    if kind != "cmpv":
                        if p["sq_wait"]:
                            dve.wait_ge(s_p["mean"], p["sq_wait"]["mean"])
                        tt(tmp[:, p["sq_at"], 0:N], rt, rt, ALU.mult, s_p["sqd"])
                elif phase == "mean":
                    r = roots[p["sd"] % 2][:, 0:N]
                    dve.wait_ge(s_p["sd"], p["sd"])
                    do(dve.reciprocal(r, r))
                    if kind in ("lat1", "lat2"):
                        tiles = [(0, posts[p["i"] - 1]), (1, p)] if kind == "lat2" else [(2, p)]
                        for n, (i, q) in enumerate(tiles):
                            gain = par("cq", i) if kind == "lat2" else par("ckv")
                            stt(tmp[:, 2, :], raws[q["i"] % 4], gain, r, ALU.mult, ALU.mult)
                            split(Bh[:, 8 + i], Bl[:, 8 + i], tmp[:, 2, :], s_p["out"] if n == len(tiles) - 1 else None)
                    elif kind == "ln":
                        tt(rt, rt, r, ALU.mult)
                        ts(rt, rt, par("lng"), par("lnb"), ALU.mult, ALU.add, s_p["qn"])
                    else:
                        stt(rt, rt, par(*p["gain"]), r, ALU.mult, ALU.mult, s_p["qn"])
                elif phase == "query":
                    C, S = tabs
                    pos, neg, scale = ((qs[:, p["tile"]], qneg[:, p["tile"]], HEAD ** -0.5) if kind == "qrms" else
                                       (xs[:, p["tile"]], xneg[:, p["tile"]], P ** -0.5))
                    dve.wait_ge(s_p["sd"], p["sd"])
                    do(dve.reciprocal(pos, pos))
                    ts(neg, pos, -scale, None, ALU.mult)
                    ts(pos, pos, scale, None, ALU.mult, None, None if kind == "qrms" else s_p["out"])
                    if kind == "qrms":
                        dve.wait_ge(s_p["rot"], p["rot"])
                        tt(tmp[:, 2, :], psS[:, 1, :], S, ALU.mult, s_p["rotd"])
                        tt(p["dest"], rt, C, ALU.mult)
                        tt(p["dest"], p["dest"], tmp[:, 2, :], ALU.add, s_p["out"])
                elif phase == "rot":
                    C, S = tabs
                    if kind == "cmpk":
                        C, S = (a[:, CMP_L - 1::CMP_STRIDE] for a in (C, S))
                    dest = p["dest"]
                    dve.wait_ge(s_p["rot"], p["rot"])
                    tt(tmp[:, 2, 0:N], psS[:, 1, 0:N], S, ALU.mult, s_p["rotd"])
                    tt(dest, rt, C, ALU.mult)
                    tt(dest, dest, tmp[:, 2, 0:N], ALU.add, s_p["out"])

            def windows(p):
                i = 0 if p["kind"] == "cmpk" else 1
                dve.wait_ge(s_p["raw"], p["raw"])
                if i:
                    dve.wait_ge(s_p["cmpo"], i)
                for l0 in (0, CMP_STRIDE):
                    src = raws[p["i"] % 4][:, l0:l0 + CMP_STRIDE * CMP_N].rearrange("p (n l) -> p l n", l=CMP_STRIDE)
                    pe_ = par("pe", CMP_L * i + l0, CMP_STRIDE).unsqueeze(2).to_broadcast([P, CMP_STRIDE, CMP_N])
                    tt(cmpin[:, l0:l0 + CMP_STRIDE], src, pe_, ALU.add, s_p["cmpin"] if l0 else None)

            def memory_keys(j):
                dve.wait_ge(s_kxsd, j + 1)
                do(dve.reciprocal(xsd[:, j], xsd[:, j]))
                dve.wait_ge(s_kx, j + 1)
                stt(kx[:, j], kx[:, j], par("xkn"), xsd[:, j], ALU.mult, ALU.mult, s_kxn)

            MEMORY_KEYS_AT = [("iq", 2), ("p2", "qn0"), ("p2", "qn1"), ("p2", "qn2")]

            def project(ps):
                for new, old in waves(ps):
                    if new and new["key"] in MEMORY_KEYS_AT:
                        memory_keys(MEMORY_KEYS_AT.index(new["key"]))
                    for p, phase in old:
                        phase_of(p, phase)
                    if new and new["kind"] in ("cmpk", "cmpv"):
                        windows(new)

            dve.wait_ge(s_par, 16)
            dve.wait_ge(s_ssm0, 16)
            for part in range(2):
                prepare(0, part)
            for k in range(KD):
                add_square("mix0", k)
            dve.wait_ge(s_mats, 16)
            for l in range(DEPTH):
                normalise(f"mix{l}", ("norm_mix", l))
                if l == 0:
                    dve.wait_ge(s_in, 16)
                    for part in range(2, 6):
                        prepare(0, part)
                do(dve.memset(zc[:, 0:2], 0.0))
                for what, key in mixer_plan(l):
                    if what == "ssm":
                        ssm_step(l, key)
                    elif what == "unit":
                        unit_step(l, key)
                    elif what == "scale":
                        unit_scale(units[f"sw{l}"][key])
                    else:
                        take_mixer(key)
                for i in range(KD):
                    residual(("mix", l, i), i, f"ffn{l}")
                normalise(f"ffn{l}", ("norm_ffn", l))
                for c, (t0, nt) in enumerate(FFN_CHUNKS):
                    for t in range(t0, t0 + nt):
                        n = FFN_TILES * l + t
                        at = t - FFN_CHUNKS[1][0]
                        if l == DEPTH - 1 and 0 <= at < 4:
                            add_square("mem", 2 * at)
                            add_square("mem", 2 * at + 1)
                        elif l == DEPTH - 1 and at == 4:
                            memory_normalise()
                        if l + 1 < DEPTH and t in (3, 6, 9, 14, 16, 18):
                            prepare(l + 1, (3, 6, 9, 14, 16, 18).index(t))
                        bank = from_bank(("up", l, t))
                        dve.wait_ge(s_took["act"], taken["gt", l, t][1])
                        tt(tmp[:, 1, :], bank, rawt[:, n % 2, :], ALU.mult, s_took["dve"])
                        split(Mh[:, t - t0], Ml[:, t - t0], tmp[:, 1, :], s_hid)
                    for i in range(KD):
                        residual(("fo", l, c, i), i, NEXT_NORM[l] if c == len(FFN_CHUNKS) - 1 else None)
            normalise("final", "norm_final")
            for k in range(KD):
                add_square("norm1", k)
            normalise("norm1", "norm1")
            dve.wait_ge(s_rope2, 16)
            project(block2_posts)
            dve.wait_ge(s_p["toksb"], block2_done["toksb"])
            attention(units2, lambda i, w: indexer_step(*beside(i, w)) if beside(i, w) else None)
            for i in range(KD):
                residual(("out2", i), i, "norm2")
            normalise("norm2", "norm2")
            project(x_posts)
            attention(units["x"])
            for i in range(KD):
                residual(("xo", i), i, "norm3")
            normalise("norm3", "norm3")
            for c, (t0, nt) in enumerate(FF2_CHUNKS):
                for t in range(t0, t0 + nt):
                    n = FFN_TILES * DEPTH + t
                    dve.wait_ge(s_took["act"], taken["fi", t][1])
                    tt(tmp[:, 1, :], rawt[:, n % 2, :], rawt[:, n % 2, :], ALU.mult)
                    split(Mh[:, t - t0], Ml[:, t - t0], tmp[:, 1, :], s_hid)
                for i in range(KD):
                    residual(("fo2", c, i), i)
            dve.sem_inc(s_y, 1)


def cmp_weights(a):
    out = np.zeros((2, P, CMP_L, P), np.float32)
    for g in (slice(0, HEAD), slice(HEAD, P)):
        out[:, g, :, g] = a.transpose(0, 2, 1, 3)
    return out.reshape(2, P, CMP_L * P)


def kernel(**inputs):
    import concourse.bacc as bacc
    from concourse.bass_utils import run_bass_kernel_spmd

    w = {k: np.asarray(a) for k, a in inputs.items()}
    parts = []
    for key, K, _, _ in (job for job in job_plan() if job[1]):
        a = weight_tile(w, key)
        parts.append(a.reshape(K, P, P).transpose(1, 0, 2).reshape(-1))
    arrays = {
        "wstream": np.concatenate(parts),
        "params": pack_params(w),
        "ssmp": pack_ssm(w),
        "cmpw": cmp_weights(w["w_nsa_cmp_2"][0]),
        "consts": constants()[0],
        "rope2": constants()[1],
        "xT": np.ascontiguousarray(w["x"][0].T.reshape(KD, P, SEQ).transpose(1, 0, 2)),
        "memT": np.ascontiguousarray(w["mem_2"][0].T.reshape(KD, P, MEM).transpose(1, 0, 2)),
    }
    nc = bacc.Bacc("TRN2", target_bir_lowering=False, num_devices=1)
    args = [nc.dram_tensor(n, a.shape, F32, kind="ExternalInput").ap() for n, a in arrays.items()]
    out = nc.dram_tensor("outT", (P, KD, SEQ), F32, kind="ExternalOutput").ap()
    block_program(nc, *args, out)
    r = run_bass_kernel_spmd(nc, [arrays], core_ids=[0])
    o = r.results[0]["outT"]
    return np.ascontiguousarray(o.transpose(1, 0, 2).reshape(D_MODEL, SEQ).T)[None]
```
